# Optimizing a Trainium2 kernel written in Bass

```python
import math
import numpy as np
import jax, jax.numpy as jnp
from jax import lax

D_MODEL = 1024
BATCH = 1
SEQ = 256
DEPTH = 2

GRID_W = 64
MEM_LEN = 256
HEAD_DIM = 64
DA_HEADS = 4
DA_VDIM = 2 * HEAD_DIM
DA_QK = DA_HEADS * 2 * HEAD_DIM
DA_V = DA_HEADS * DA_VDIM
Q_BLOCK = 128
NA_HEADS = 8
NA_W = NA_HEADS * HEAD_DIM
NA_WIN_ROWS = 8
NA_WIN_COLS = 16
NA_QCOLS = 16
NA_KCOLS = 32
SC_W = 512
SC_K = 3
N_BRANCH = 3
BRANCH_W = 512
IN_SPLITS = (DA_QK, DA_QK, DA_V, NA_W, NA_W, NA_W, SC_W, SC_W, SC_W, N_BRANCH * D_MODEL)
IN_COLS = 7680
XA_HEADS = 4
XA_DIM = D_MODEL // XA_HEADS
D_FF = 2816
FFN_K = 3
ROPE_THETA = 10000.0
LN_EPS = 1e-5


def layer_norm(x, g, b):
    xf = x.astype(jnp.float32)
    mu = jnp.mean(xf, axis=-1, keepdims=True)
    var = jnp.mean(jnp.square(xf - mu), axis=-1, keepdims=True)
    y = (xf - mu) * lax.rsqrt(var + LN_EPS)
    return (y * g.astype(jnp.float32) + b.astype(jnp.float32)).astype(x.dtype)

def rms_norm(x, g):
    xf = x.astype(jnp.float32)
    y = xf * lax.rsqrt(jnp.mean(jnp.square(xf), axis=-1, keepdims=True) + LN_EPS)
    return (y * g.astype(jnp.float32)).astype(x.dtype)

def rope(x, pos):
    d = x.shape[-1]
    half = d // 2
    inv = ROPE_THETA ** (-jnp.arange(half, dtype=jnp.float32) * 2.0 / d)
    ang = pos.astype(jnp.float32)[:, None] * inv[None, :]
    cos = jnp.cos(ang).astype(x.dtype)
    sin = jnp.sin(ang).astype(x.dtype)
    x1, x2 = x[..., :half], x[..., half:]
    return jnp.concatenate([x1 * cos - x2 * sin, x2 * cos + x1 * sin], axis=-1)

def dwconv(x, w):
    k, c = w.shape
    return lax.conv_general_dilated(x, w[:, None, :], window_strides=(1,), padding=[(k // 2, k // 2)],
                                    dimension_numbers=('NWC', 'WIO', 'NWC'), feature_group_count=c)

def diff_attention(q, k, v, lam, pos):
    b, s = q.shape[0], q.shape[1]
    q = rope(q.transpose(0, 2, 3, 1, 4), pos) * (HEAD_DIM ** -0.5)
    k = rope(k.transpose(0, 2, 3, 1, 4), pos)
    vt = v.transpose(0, 2, 1, 3)
    nb = s // Q_BLOCK
    qb = q.reshape(b, DA_HEADS, 2, nb, Q_BLOCK, HEAD_DIM).transpose(3, 0, 1, 2, 4, 5)

    def block(qblk):
        sc = jnp.einsum('bhmqd,bhmkd->bhmqk', qblk, k, preferred_element_type=jnp.float32)
        p = jax.nn.softmax(sc, axis=-1)
        w = p[:, :, 0] - lam * p[:, :, 1]
        return jnp.einsum('bhqk,bhkv->bhqv', w.astype(vt.dtype), vt)

    o = lax.map(block, qb)
    return o.transpose(1, 2, 0, 3, 4).reshape(b, DA_HEADS, s, DA_VDIM)

def _na_static(rows):
    wr = min(NA_WIN_ROWS, rows)
    n_cb = GRID_W // NA_QCOLS
    c = np.arange(GRID_W).reshape(n_cb, NA_QCOLS)
    cs = np.clip(c - NA_WIN_COLS // 2, 0, GRID_W - NA_WIN_COLS)
    kstart = np.minimum(cs[:, 0], GRID_W - NA_KCOLS)
    kcol = kstart[:, None] + np.arange(NA_KCOLS)
    rel = kcol[:, None, :] - c[:, :, None]
    valid = (kcol[:, None, :] >= cs[:, :, None]) & (kcol[:, None, :] < cs[:, :, None] + NA_WIN_COLS)
    dc_idx = np.clip(rel + NA_WIN_COLS - 1, 0, 2 * NA_WIN_COLS - 2)
    return wr, n_cb, kcol.astype(np.int32), dc_idx.astype(np.int32), valid

def neighbourhood_attention(q, k, v, rpb):
    b, s = q.shape[0], q.shape[1]
    rows = s // GRID_W
    wr, n_cb, kcol, dc_idx, valid = _na_static(rows)

    def grid(t):
        return t.reshape(b, rows, GRID_W, NA_HEADS, HEAD_DIM).transpose(0, 3, 1, 2, 4)

    qg = grid(q) * (HEAD_DIM ** -0.5)
    kg = grid(k)
    vg = grid(v)
    qr = qg.reshape(b, NA_HEADS, rows, n_cb, NA_QCOLS, HEAD_DIM).transpose(2, 0, 1, 3, 4, 5)
    kcol_j = jnp.asarray(kcol)
    mask = jnp.asarray(valid)[:, :, None, :]
    bias_c = rpb[:, :, jnp.asarray(dc_idx)]

    def row_block(args):
        r, qblk = args
        rs = jnp.clip(r - wr // 2, 0, rows - wr)
        k_rows = lax.dynamic_slice_in_dim(kg, rs, wr, axis=2)
        v_rows = lax.dynamic_slice_in_dim(vg, rs, wr, axis=2)
        k_blk = jnp.take(k_rows, kcol_j, axis=3)
        v_blk = jnp.take(v_rows, kcol_j, axis=3)
        sc = jnp.einsum('bhjqd,bhrjkd->bhjqrk', qblk, k_blk, preferred_element_type=jnp.float32)
        dr_idx = rs + jnp.arange(wr) - r + (NA_WIN_ROWS - 1)
        bias = jnp.take(bias_c, dr_idx, axis=1).transpose(0, 2, 3, 1, 4)
        sc = jnp.where(mask, sc + bias[None].astype(jnp.float32), -jnp.inf)
        p = jax.nn.softmax(sc.reshape(sc.shape[:4] + (wr * NA_KCOLS,)), axis=-1).reshape(sc.shape)
        return jnp.einsum('bhjqrk,bhrjkd->bhjqd', p.astype(v_blk.dtype), v_blk)

    o = lax.map(row_block, (jnp.arange(rows, dtype=jnp.int32), qr))
    return o.transpose(1, 0, 3, 4, 2, 5).reshape(b, s, NA_W)

def hybrid_mixer(x, w_in, lam_q1, lam_k1, lam_q2, lam_k2, subln_g, rpb, sc_conv_w, w_branch, w_mix_out, lam_init, pos):
    b, s, _ = x.shape
    proj = x @ w_in
    qa, ka, va, qb, kb, vb, gb, gc, hc, gates = jnp.split(proj, np.cumsum(IN_SPLITS)[:-1].tolist(), axis=-1)
    lam = (jnp.exp(jnp.sum(lam_q1.astype(jnp.float32) * lam_k1.astype(jnp.float32)))
           - jnp.exp(jnp.sum(lam_q2.astype(jnp.float32) * lam_k2.astype(jnp.float32))) + lam_init)
    oa = diff_attention(qa.reshape(b, s, DA_HEADS, 2, HEAD_DIM), ka.reshape(b, s, DA_HEADS, 2, HEAD_DIM),
                        va.reshape(b, s, DA_HEADS, DA_VDIM), lam, pos)
    ya = (rms_norm(oa, subln_g) * (1.0 - lam_init)).transpose(0, 2, 1, 3).reshape(b, s, DA_V)
    yb = neighbourhood_attention(qb, kb, vb, rpb)
    yc = gb * dwconv(gc * hc, sc_conv_w)
    g = jax.nn.sigmoid(gates.reshape(b, s, N_BRANCH, D_MODEL))
    merged = (g[:, :, 0] * (ya @ w_branch[0]) + g[:, :, 1] * (yb @ w_branch[1])
              + g[:, :, 2] * (yc @ w_branch[2]))
    return merged @ w_mix_out

def memory_cross_attention(x, mem, xa_q, xa_kv, xa_o):
    b, s, _ = x.shape
    q = (x @ xa_q).reshape(b, s, XA_HEADS, XA_DIM) * (XA_DIM ** -0.5)
    k, v = jnp.split(mem @ xa_kv, 2, axis=-1)
    k = k.reshape(b, mem.shape[1], XA_HEADS, XA_DIM)
    v = v.reshape(b, mem.shape[1], XA_HEADS, XA_DIM)
    p = jax.nn.softmax(jnp.einsum('bqhd,bkhd->bhqk', q, k, preferred_element_type=jnp.float32), axis=-1)
    o = jnp.einsum('bhqk,bkhd->bqhd', p.astype(v.dtype), v).reshape(b, s, D_MODEL)
    return o @ xa_o

def conv_ffn(x, ffn_w_in, ffn_conv_w, ffn_conv_b, ffn_w_out):
    u, gt = jnp.split(x @ ffn_w_in, 2, axis=-1)
    a = dwconv(gt, ffn_conv_w) + ffn_conv_b
    return (jax.nn.silu(a) * u) @ ffn_w_out

def first_inputs(seed: int = 0) -> dict:
    key = jax.random.key(seed)
    ks = jax.random.split(key, 24)
    beta = (8.0 * DEPTH) ** -0.25

    def nrm(k, shape, scale):
        return jax.random.normal(k, shape, jnp.float32) * scale

    is_value = (False, False, True, False, False, True, False, False, True, False)
    col_scale = np.concatenate([np.full(n, beta if iv else 1.0, np.float32) for n, iv in zip(IN_SPLITS, is_value)])
    kv_scale = np.concatenate([np.ones(D_MODEL, np.float32), np.full(D_MODEL, beta, np.float32)])
    return {
        'x': nrm(ks[0], (BATCH, SEQ, D_MODEL), 1.0),
        'mem': nrm(ks[1], (BATCH, MEM_LEN, D_MODEL), 1.0),
        'emb_ln_g': 1.0 + nrm(ks[2], (D_MODEL,), 0.02),
        'emb_ln_b': nrm(ks[3], (D_MODEL,), 0.02),
        'w_in': nrm(ks[4], (DEPTH, D_MODEL, IN_COLS), D_MODEL ** -0.5) * jnp.asarray(col_scale),
        'lam_q1': nrm(ks[5], (DEPTH, HEAD_DIM), 0.1),
        'lam_k1': nrm(ks[6], (DEPTH, HEAD_DIM), 0.1),
        'lam_q2': nrm(ks[7], (DEPTH, HEAD_DIM), 0.1),
        'lam_k2': nrm(ks[8], (DEPTH, HEAD_DIM), 0.1),
        'subln_g': 1.0 + nrm(ks[9], (DEPTH, DA_VDIM), 0.02),
        'rpb': nrm(ks[10], (DEPTH, NA_HEADS, 2 * NA_WIN_ROWS - 1, 2 * NA_WIN_COLS - 1), 0.1),
        'sc_conv_w': nrm(ks[11], (DEPTH, SC_K, SC_W), SC_K ** -0.5),
        'w_branch': nrm(ks[12], (DEPTH, N_BRANCH, BRANCH_W, D_MODEL), BRANCH_W ** -0.5 * beta),
        'w_mix_out': nrm(ks[13], (DEPTH, D_MODEL, D_MODEL), D_MODEL ** -0.5 * beta),
        'xa_q': nrm(ks[14], (DEPTH, D_MODEL, D_MODEL), D_MODEL ** -0.5),
        'xa_kv': nrm(ks[15], (DEPTH, D_MODEL, 2 * D_MODEL), D_MODEL ** -0.5) * jnp.asarray(kv_scale),
        'xa_o': nrm(ks[16], (DEPTH, D_MODEL, D_MODEL), D_MODEL ** -0.5 * beta),
        'ffn_w_in': nrm(ks[17], (DEPTH, D_MODEL, 2 * D_FF), D_MODEL ** -0.5 * beta),
        'ffn_conv_w': nrm(ks[18], (DEPTH, FFN_K, D_FF), FFN_K ** -0.5),
        'ffn_conv_b': nrm(ks[19], (DEPTH, D_FF), 0.02),
        'ffn_w_out': nrm(ks[20], (DEPTH, D_FF, D_MODEL), D_FF ** -0.5 * beta),
        'ln_g': 1.0 + nrm(ks[21], (DEPTH, 3, D_MODEL), 0.02),
        'ln_b': nrm(ks[22], (DEPTH, 3, D_MODEL), 0.02),
    }

def first_block(x, mem, emb_ln_g, emb_ln_b, w_in, lam_q1, lam_k1, lam_q2, lam_k2, subln_g, rpb, sc_conv_w,
              w_branch, w_mix_out, xa_q, xa_kv, xa_o, ffn_w_in, ffn_conv_w, ffn_conv_b, ffn_w_out, ln_g, ln_b):
    alpha = (2.0 * DEPTH) ** 0.25
    pos = jnp.arange(x.shape[1], dtype=jnp.int32)
    x = layer_norm(x, emb_ln_g, emb_ln_b)
    for l in range(DEPTH):
        lam_init = 0.8 - 0.6 * math.exp(-0.3 * l)
        h = hybrid_mixer(x, w_in[l], lam_q1[l], lam_k1[l], lam_q2[l], lam_k2[l], subln_g[l], rpb[l],
                         sc_conv_w[l], w_branch[l], w_mix_out[l], lam_init, pos)
        x = layer_norm(alpha * x + h, ln_g[l, 0], ln_b[l, 0])
        h = memory_cross_attention(x, mem, xa_q[l], xa_kv[l], xa_o[l])
        x = layer_norm(alpha * x + h, ln_g[l, 1], ln_b[l, 1])
        h = conv_ffn(x, ffn_w_in[l], ffn_conv_w[l], ffn_conv_b[l], ffn_w_out[l])
        x = layer_norm(alpha * x + h, ln_g[l, 2], ln_b[l, 2])
    return x


D_MIX = D_MODEL
POOL_WIDTH = D_MIX // 4
POOL_WINDOWS = (2, 4, 8, 16)
POOL_GROUP = POOL_WIDTH // len(POOL_WINDOWS)
MOBA_WIDTH = D_MIX // 4
MOBA_HEADS = MOBA_WIDTH // HEAD_DIM
MOBA_BLOCK = 256
MOBA_TOPK = 3
MOBA_QCHUNK = 32
DIL_WIDTH = D_MIX // 4
DIL_HEADS = DIL_WIDTH // HEAD_DIM
DILATIONS = ((128, 1), (512, 4), (2048, 16))
CONV_WIDTH = D_MIX - POOL_WIDTH - MOBA_WIDTH - DIL_WIDTH
CONV_KERNEL = 31
ROPE_THETA_2 = 500000.0
ROPE_DIMS = HEAD_DIM // 4
RMS_EPS = 1e-6
NEG_INF = -1e30
OFF_POOL = 0
OFF_MOBA = OFF_POOL + POOL_WIDTH
OFF_DIL = OFF_MOBA + 3 * MOBA_WIDTH
OFF_CONV = OFF_DIL + 3 * DIL_WIDTH
D_IN = OFF_CONV + 2 * CONV_WIDTH


def rms_norm_2(x, g):
    xf = x.astype(jnp.float32)
    y = xf * lax.rsqrt(jnp.mean(xf * xf, axis=-1, keepdims=True) + RMS_EPS)
    return (y * g.astype(jnp.float32)).astype(x.dtype)

def layer_norm_2(x, g, b):
    xf = x.astype(jnp.float32)
    mu = jnp.mean(xf, axis=-1, keepdims=True)
    var = jnp.mean(jnp.square(xf - mu), axis=-1, keepdims=True)
    y = (xf - mu) * lax.rsqrt(var + LN_EPS)
    return (y * g.astype(jnp.float32) + b.astype(jnp.float32)).astype(x.dtype)

def swiglu(x, wg, wu, wd):
    return (jax.nn.silu(x @ wg) * (x @ wu)) @ wd

def rope_tables(positions, dtype):
    inv = ROPE_THETA_2 ** (-jnp.arange(0, ROPE_DIMS, 2, dtype=jnp.float32) / ROPE_DIMS)
    ang = positions.astype(jnp.float32)[..., None] * inv
    return (jnp.cos(ang)[:, :, None, :].astype(dtype), jnp.sin(ang)[:, :, None, :].astype(dtype))

def apply_rope(t, cos, sin):
    half = ROPE_DIMS // 2
    t1 = t[..., :half]
    t2 = t[..., half:ROPE_DIMS]
    return jnp.concatenate([t1 * cos - t2 * sin, t2 * cos + t1 * sin, t[..., ROPE_DIMS:]], axis=-1)

def pool_mixer(u, w, scale):
    B, S, _ = u.shape
    ug = u.reshape(B, S, len(POOL_WINDOWS), POOL_GROUP)
    t_count = jnp.arange(S, dtype=jnp.float32) + 1.0
    outs = []
    for g, wnd in enumerate(POOL_WINDOWS):
        ch = ug[:, :, g].astype(jnp.float32)
        c = jnp.cumsum(ch, axis=1)
        c_back = jnp.pad(c, ((0, 0), (wnd, 0), (0, 0)))[:, :S]
        cnt = jnp.minimum(t_count, float(wnd))[None, :, None]
        outs.append(((c - c_back) / cnt - ch).astype(u.dtype))
    pooled = jnp.stack(outs, axis=2)
    mixed = jnp.einsum('bsgc,gcd->bsgd', pooled, w)
    return mixed.reshape(B, S, POOL_WIDTH) * scale

def moba_attention(q, k, v):
    B, H, S, dh = q.shape
    L = MOBA_BLOCK
    Sp = -(-S // L) * L
    pad = ((0, 0), (0, 0), (0, Sp - S), (0, 0))
    q, k, v = jnp.pad(q, pad), jnp.pad(k, pad), jnp.pad(v, pad)
    NB = Sp // L
    kb = k.reshape(B, H, NB, L, dh)
    vb = v.reshape(B, H, NB, L, dh)
    kmean = jnp.mean(kb.astype(jnp.float32), axis=3)
    gate = jnp.einsum('bhsd,bhnd->bhsn', q.astype(jnp.float32), kmean)
    qblk = jnp.arange(Sp) // L
    past = jnp.arange(NB)[None, :] < qblk[:, None]
    gate = jnp.where(past, gate, NEG_INF)
    topk = min(MOBA_TOPK, NB)
    _, idx = lax.top_k(gate, topk)
    QC = MOBA_QCHUNK
    nc = Sp // QC
    qc = q.reshape(B, H, nc, QC, dh).transpose(2, 0, 1, 3, 4)
    ic = idx.reshape(B, H, nc, QC, topk).transpose(2, 0, 1, 3, 4)
    gather = jax.vmap(jax.vmap(lambda blocks, ii: blocks[ii]))
    scale = HEAD_DIM ** -0.5

    def chunk(args):
        c, qi, ii = args
        start = c * QC
        blk = start // L
        t = start + jnp.arange(QC)
        k_own = lax.dynamic_index_in_dim(kb, blk, axis=2, keepdims=False)
        v_own = lax.dynamic_index_in_dim(vb, blk, axis=2, keepdims=False)
        s_own = jnp.einsum('bhqd,bhkd->bhqk', qi, k_own).astype(jnp.float32) * scale
        kpos = blk * L + jnp.arange(L)
        s_own = jnp.where(kpos[None, :] <= t[:, None], s_own, NEG_INF)
        k_sel = gather(kb, ii)
        v_sel = gather(vb, ii)
        s_sel = jnp.einsum('bhqd,bhqnkd->bhqnk', qi, k_sel).astype(jnp.float32) * scale
        valid = jnp.arange(topk) < blk
        s_sel = jnp.where(valid[:, None], s_sel, NEG_INF)
        logits = jnp.concatenate([s_sel.reshape(B, H, QC, topk * L), s_own], axis=-1)
        p = jax.nn.softmax(logits, axis=-1).astype(qi.dtype)
        p_sel = p[..., :topk * L].reshape(B, H, QC, topk, L)
        p_own = p[..., topk * L:]
        return (jnp.einsum('bhqnk,bhqnkd->bhqd', p_sel, v_sel)
                + jnp.einsum('bhqk,bhkd->bhqd', p_own, v_own))

    out = lax.map(chunk, (jnp.arange(nc), qc, ic))
    out = out.transpose(1, 2, 0, 3, 4).reshape(B, H, Sp, dh)
    return out[:, :, :S]

def dilated_branch(q, k, v, window, dil):
    B, H, S, dh = q.shape
    n = S // dil
    bw = window // dil
    n_p = -(-n // bw) * bw
    nb = n_p // bw

    def to_sub(t):
        t = t.reshape(B, H, n, dil, dh).transpose(0, 1, 3, 2, 4)
        t = jnp.pad(t, ((0, 0), (0, 0), (0, 0), (0, n_p - n), (0, 0)))
        return t.reshape(B, H, dil, nb, bw, dh)

    def with_prev(t):
        prev = jnp.pad(t, ((0, 0), (0, 0), (0, 0), (1, 0), (0, 0), (0, 0)))[:, :, :, :nb]
        return jnp.concatenate([prev, t], axis=4)

    qs = to_sub(q)
    kk = with_prev(to_sub(k))
    vv = with_prev(to_sub(v))
    logits = jnp.einsum('bhrnqd,bhrnkd->bhrnqk', qs, kk).astype(jnp.float32) * (HEAD_DIM ** -0.5)
    qi = jnp.arange(bw)[:, None]
    kj = jnp.arange(2 * bw)[None, :]
    rel = qi + bw - kj
    band = (rel >= 0) & (rel <= bw)
    has_prev = (jnp.arange(nb)[:, None, None] > 0) | (kj[None] >= bw)
    mask = band[None] & has_prev
    logits = jnp.where(mask, logits, NEG_INF)
    m = jnp.max(logits, axis=-1, keepdims=True)
    e = jnp.exp(logits - m)
    den = jnp.sum(e, axis=-1, keepdims=True)
    lse = (m + jnp.log(den))[..., 0]
    p = (e / den).astype(v.dtype)
    out = jnp.einsum('bhrnqk,bhrnkd->bhrnqd', p, vv)
    out = out.reshape(B, H, dil, n_p, dh)[:, :, :, :n].transpose(0, 1, 3, 2, 4).reshape(B, H, S, dh)
    lse = lse.reshape(B, H, dil, n_p)[:, :, :, :n].transpose(0, 1, 3, 2).reshape(B, H, S)
    return out, lse

def dilated_attention(q, k, v):
    outs, lses = [], []
    for window, dil in DILATIONS:
        o, l = dilated_branch(q, k, v, window, dil)
        outs.append(o)
        lses.append(l)
    w = jax.nn.softmax(jnp.stack(lses, axis=0), axis=0)
    o = jnp.stack(outs, axis=0).astype(jnp.float32)
    return jnp.sum(w[..., None] * o, axis=0).astype(q.dtype)

def conv_module(u, conv_w, conv_b, ln_g, ln_b):
    a, g = jnp.split(u, 2, axis=-1)
    h = a * jax.nn.sigmoid(g)
    y = lax.conv_general_dilated(h, conv_w[:, None, :].astype(h.dtype), window_strides=(1,),
                                 padding=((CONV_KERNEL - 1, 0),),
                                 dimension_numbers=('NWC', 'WIO', 'NWC'),
                                 feature_group_count=CONV_WIDTH)
    y = y + conv_b
    return jax.nn.silu(layer_norm_2(y, ln_g, ln_b))

def to_heads(t, h):
    B, S, _ = t.shape
    return t.reshape(B, S, h, HEAD_DIM)

def second_inputs(seed: int = 0) -> dict:
    key = jax.random.key(seed)
    ks = jax.random.split(key, 24)
    f32 = jnp.float32

    def nrm(k, shape, fan_in):
        return jax.random.normal(k, shape, f32) * (fan_in ** -0.5)

    def gain(k, shape):
        return 1.0 + 0.05 * jax.random.normal(k, shape, f32)

    x = jax.random.normal(ks[0], (BATCH, SEQ, D_MODEL), f32)
    positions = jnp.arange(SEQ, dtype=jnp.int32)[None, :] + jax.random.randint(ks[1], (BATCH, 1), 0, 4096, jnp.int32)
    return {
        "x": x,
        "positions": positions,
        "ffn1_norm": gain(ks[2], (DEPTH, D_MODEL)),
        "ffn1_gate": nrm(ks[3], (DEPTH, D_MODEL, D_FF), D_MODEL),
        "ffn1_up": nrm(ks[4], (DEPTH, D_MODEL, D_FF), D_MODEL),
        "ffn1_down": nrm(ks[5], (DEPTH, D_FF, D_MODEL), D_FF),
        "mix_norm": gain(ks[6], (DEPTH, D_MODEL)),
        "w_in": nrm(ks[7], (DEPTH, D_MODEL, D_IN), D_MODEL),
        "pool_w": nrm(ks[8], (DEPTH, len(POOL_WINDOWS), POOL_GROUP, POOL_GROUP), POOL_GROUP),
        "pool_scale": 1.0 + 0.1 * jax.random.normal(ks[9], (DEPTH, POOL_WIDTH), f32),
        "conv_w": nrm(ks[10], (DEPTH, CONV_KERNEL, CONV_WIDTH), CONV_KERNEL),
        "conv_b": 0.01 * jax.random.normal(ks[11], (DEPTH, CONV_WIDTH), f32),
        "conv_ln_g": gain(ks[12], (DEPTH, CONV_WIDTH)),
        "conv_ln_b": 0.01 * jax.random.normal(ks[13], (DEPTH, CONV_WIDTH), f32),
        "w_out": nrm(ks[14], (DEPTH, D_MIX, D_MODEL), D_MIX),
        "ffn2_norm": gain(ks[15], (DEPTH, D_MODEL)),
        "ffn2_gate": nrm(ks[16], (DEPTH, D_MODEL, D_FF), D_MODEL),
        "ffn2_up": nrm(ks[17], (DEPTH, D_MODEL, D_FF), D_MODEL),
        "ffn2_down": nrm(ks[18], (DEPTH, D_FF, D_MODEL), D_FF),
        "final_norm": gain(ks[19], (D_MODEL,)),
    }

def second_block(x, positions, ffn1_norm, ffn1_gate, ffn1_up, ffn1_down, mix_norm, w_in, pool_w, pool_scale,
              conv_w, conv_b, conv_ln_g, conv_ln_b, w_out, ffn2_norm, ffn2_gate, ffn2_up, ffn2_down, final_norm):
    cos, sin = rope_tables(positions, x.dtype)
    for l in range(DEPTH):
        x = x + 0.5 * swiglu(rms_norm_2(x, ffn1_norm[l]), ffn1_gate[l], ffn1_up[l], ffn1_down[l])
        h = rms_norm_2(x, mix_norm[l]) @ w_in[l]
        u_pool = h[..., OFF_POOL:OFF_MOBA]
        qm, km, vm = jnp.split(h[..., OFF_MOBA:OFF_DIL], 3, axis=-1)
        qd, kd, vd = jnp.split(h[..., OFF_DIL:OFF_CONV], 3, axis=-1)
        u_conv = h[..., OFF_CONV:]
        B, S, _ = x.shape
        y_pool = pool_mixer(u_pool, pool_w[l], pool_scale[l])
        qm = apply_rope(to_heads(qm, MOBA_HEADS), cos, sin).transpose(0, 2, 1, 3)
        km = apply_rope(to_heads(km, MOBA_HEADS), cos, sin).transpose(0, 2, 1, 3)
        vm = to_heads(vm, MOBA_HEADS).transpose(0, 2, 1, 3)
        y_moba = moba_attention(qm, km, vm).transpose(0, 2, 1, 3).reshape(B, S, MOBA_WIDTH)
        qd = apply_rope(to_heads(qd, DIL_HEADS), cos, sin).transpose(0, 2, 1, 3)
        kd = apply_rope(to_heads(kd, DIL_HEADS), cos, sin).transpose(0, 2, 1, 3)
        vd = to_heads(vd, DIL_HEADS).transpose(0, 2, 1, 3)
        y_dil = dilated_attention(qd, kd, vd).transpose(0, 2, 1, 3).reshape(B, S, DIL_WIDTH)
        y_conv = conv_module(u_conv, conv_w[l], conv_b[l], conv_ln_g[l], conv_ln_b[l])
        mix = jnp.concatenate([y_pool, y_moba, y_dil, y_conv], axis=-1)
        x = x + mix @ w_out[l]
        x = x + 0.5 * swiglu(rms_norm_2(x, ffn2_norm[l]), ffn2_gate[l], ffn2_up[l], ffn2_down[l])
    return rms_norm_2(x, final_norm)


def setup_inputs(seed=0):
    out = dict(first_inputs(seed))
    for name, value in second_inputs(seed + 1).items():
        if name != "x":
            out[name + "_2"] = value
    return out


def reference(
    x, mem, emb_ln_g, emb_ln_b, w_in, lam_q1, lam_k1, lam_q2, lam_k2, subln_g, rpb, sc_conv_w,
    w_branch, w_mix_out, xa_q, xa_kv, xa_o, ffn_w_in, ffn_conv_w, ffn_conv_b, ffn_w_out, ln_g,
    ln_b, positions_2, ffn1_norm_2, ffn1_gate_2, ffn1_up_2, ffn1_down_2, mix_norm_2, w_in_2,
    pool_w_2, pool_scale_2, conv_w_2, conv_b_2, conv_ln_g_2, conv_ln_b_2, w_out_2, ffn2_norm_2,
    ffn2_gate_2, ffn2_up_2, ffn2_down_2, final_norm_2,
):
    x = first_block(
        x, mem, emb_ln_g, emb_ln_b, w_in, lam_q1, lam_k1, lam_q2, lam_k2, subln_g, rpb,
        sc_conv_w, w_branch, w_mix_out, xa_q, xa_kv, xa_o, ffn_w_in, ffn_conv_w, ffn_conv_b,
        ffn_w_out, ln_g, ln_b,
    )
    return second_block(
        x, positions_2, ffn1_norm_2, ffn1_gate_2, ffn1_up_2, ffn1_down_2, mix_norm_2, w_in_2,
        pool_w_2, pool_scale_2, conv_w_2, conv_b_2, conv_ln_g_2, conv_ln_b_2, w_out_2,
        ffn2_norm_2, ffn2_gate_2, ffn2_up_2, ffn2_down_2, final_norm_2,
    )


_drawn_inputs = setup_inputs


def setup_inputs(seed=0):
    import zlib

    import numpy as np

    out = dict(_drawn_inputs(seed))
    spreads = {}
    factors = {'lam_q1': 6.622,
     'lam_q2': 4.96,
     'lam_k2': 7.276,
     'subln_g': 24.818,
     'rpb': 38.629,
     'ffn_conv_b': 8.0,
     'conv_b_2': 6.724,
     'conv_ln_b_2': 8.0}
    for name, (base, spread) in spreads.items():
        noise = np.random.default_rng([zlib.crc32(name.encode()), seed]).standard_normal(out[name].shape)
        drawn = base * np.exp(spread * noise) if base else spread * noise
        out[name] = __import__('jax').numpy.asarray(drawn.astype(out[name].dtype))
    for name, factor in factors.items():
        out[name] = (out[name] * factor).astype(out[name].dtype)
    return out
```

```python
import math
from contextlib import ExitStack

import numpy as np

import concourse.bass as bass
from concourse import mybir

P = 128
S = 256
D = 1024
KT = D // P
NB = KT // 2
DEPTH = 2
FF = 2816
FG = FF // 256
CH = 2048
RING = 3
LN_EPS, RMS_EPS = 1e-5, 1e-6
ALPHA = (2.0 * DEPTH) ** 0.25
TAPS = 31
LNS = 3
TURN = (6.28125, 2029 / 2.0 ** 20, 2 * math.pi - 6.28125 - 2029 / 2.0 ** 20)
PI32 = 3.1415925

F32 = mybir.dt.float32
F32R = mybir.dt.float32r
ALU = mybir.AluOpType
ACT = mybir.ActivationFunctionType
AX = mybir.AxisListType.X

P1 = {}
_at = 0
for _name, _n in (("ln_g", 24), ("ln_b", 24), ("ffn_w", 66), ("ffn_b", 22), ("sc_w", 12), ("subln", 1),
                  ("lam", 256), ("lam_init", 1), ("one_minus", 1)):
    P1[_name] = (_at, _at + _n)
    _at += _n
NP1 = _at
P2 = {}
_at = 0
for _name, _n in (("norm_g", 24), ("pool_s", 2), ("conv_w", 62), ("conv_b", 2), ("cln_g", 2), ("cln_b", 2),
                  ("pool_w", 128)):
    P2[_name] = (_at, _at + _n)
    _at += _n
NP2 = _at
C0 = {}
_at = 0
for _name, _n in (("ident", 128), ("rot1", 128), ("rot2", 128), ("cos1", 256), ("sin1", 256), ("inv2", 1),
                  ("emb_g", 8), ("emb_b", 8), ("fin_g", 8)):
    C0[_name] = (_at, _at + _n)
    _at += _n
NC0 = _at
NC2 = 4 * 512 + 512 + 512


class Signal:

    def __init__(self, sem, steps):
        self.sem = sem
        self.value = {k: n + 1 for n, k in enumerate(steps)}

    def at(self, key):
        return self.value[key]


class Bank:

    def __init__(self):
        self.reader = None

    def claim(self, pe, signal, key):
        if self.reader is not None:
            pe.wait_ge(self.reader[0].sem, self.reader[0].at(self.reader[1]))
        self.reader = (signal, key)


def plan():
    chunks, heads, steps = [], [], {}

    def add(kind, role, l, j=0, **more):
        chunks.append(dict(kind=kind, role=role, l=l, j=j, c=len(chunks), **more))
        return len(chunks) - 1

    def at(pos, *step):
        steps.setdefault(pos, []).append(step)

    norm = 0
    for l in range(DEPTH):
        base = len(chunks)
        todo = {}

        def at(pos, *step):
            todo.setdefault(pos, []).append(step)

        def head(kind, j, pos, last):
            h = dict(kind=kind, l=l, j=j, n=len(heads))
            heads.append(h)
            at(pos, "scores", h)
            at(pos + 1, "turn", h)
            at(pos + 2, "mix", h)
            if last:
                at(pos + 3, "back", h)

        at(base + 1, "lam", l)
        for j in range(2):
            at(add("F", "dq", l, j) + 2, "rot", chunks[-1])
            at(add("F", "dk", l, j) + 2, "rot", chunks[-1])
            add("T", "va", l, j)
        for j in range(2):
            add("F", "qb", l, j)
            add("F", "kb", l, j)
            add("T", "vb", l, j)
        for j in range(2):
            for r in ("gb", "gc", "hc"):
                add("F", r, l, j)
        for half in range(2):
            for b in range(3):
                for j in range(2):
                    add("F", "gate", l, j, half=half, b=b)
            for b in range(3):
                add("B", "branch", l, 0, half=half, b=b)
        for j in range(3):
            add("O", "mo", l, j)
        add("M", "mem", l)
        chunks[-1]["after"] = [c["c"] for c in chunks if c["role"] == "branch"][-1]
        add("O", "mo", l, 3)
        chunks[base]["norm"] = norm
        norm += 1
        chunks[-1]["ends"] = norm
        where = {}
        for r, j in (("xk", 0), ("xv", 0), ("xk", 1), ("xv", 1), ("xq", 0), ("xk", 2), ("xq", 1), ("xv", 2),
                     ("xq", 2), ("xk", 3), ("xq", 3), ("xv", 3)):
            where[r, j] = add("T" if r == "xv" else "F", r, l, j)
        chunks[where["xq", 0]]["norm"] = norm
        for j in range(4):
            add("O", "xo", l, j)
        norm += 1
        chunks[-1]["ends"] = norm
        for j in range(FG + 1):
            if j < FG:
                c = add("F", "fu", l, j)
                if j == 0:
                    chunks[c]["norm"] = norm
                add("F", "fg", l, j)
            if j:
                add("O", "fo", l, j - 1)
        norm += 1
        chunks[-1]["ends"] = norm
        for j in range(4):
            head("diff", j, base + 4 + 2 * j, True)
        for j in range(8):
            head("win", j, base + 12 + j, j % 2 == 1)
        for j in range(4):
            head("xa", j, where["xq", j] + 2, True)
        order = dict(lam=-1, rot=0, back=1, mix=2, turn=3, scores=4)
        for pos, some in todo.items():
            steps[pos] = sorted(some, key=lambda s: order[s[0]])
    norm += 1
    chunks[0]["part2"] = len(chunks)
    for l in range(DEPTH, 2 * DEPTH):
        for f in range(2):
            for j in range(FG + 1):
                if j < FG:
                    c = add("F", "sg", l, j, f=f)
                    if j == 0:
                        chunks[c]["norm"] = norm
                    add("F", "su", l, j, f=f)
                if j:
                    add("O", "sd", l, j - 1, f=f)
            norm += 1
            chunks[-1]["ends"] = norm
            if l == DEPTH and f == 0:
                steps.setdefault(chunks[0]["part2"] + 3, []).append(("trig", l))
            if f:
                continue
            base = len(chunks)
            todo = {}

            def at(pos, *step):
                todo.setdefault(pos, []).append(step)

            def head(kind, j, pos):
                h = dict(kind=kind, l=l, j=j, n=len(heads))
                heads.append(h)
                at(pos, "scores", h)
                at(pos + 1, "turn", h)
                at(pos + 2, "mix", h)
                if j % 2:
                    at(pos + 3, "back", h)

            for r, k in (("qm", "F"), ("km", "F"), ("vm", "T"), ("cg", "F"), ("ca", "F"), ("up", "T"),
                         ("qd", "F"), ("kd", "F"), ("vd", "T")):
                c = add(k, r, l)
                if r in ("qm", "km", "qd", "kd"):
                    at(c + 2, "rot", chunks[c])
                if r == "up":
                    at(c + 2, "pool", chunks[c])
                    at(c + 3, "poolw", chunks[c])
            chunks[base]["norm"] = norm
            for j in (1, 0, 3, 2):
                add("O", "wo", l, j)
            norm += 1
            chunks[-1]["ends"] = norm
            for j in range(4):
                head("moba", j, base + 4 + j // 2)
            for j in range(4):
                head("dil", j, base + 10 + j // 2)
            at(base + 10, "cstats", l)
            at(base + 11, "cspread", l)
            for n in range(5, 9):
                at(base + n, "taps", l, n - 5)
            at(base + 9, "csquare", l)
            order = dict(taps=-2, csquare=-1, rot=0, cstats=1, cspread=1, pool=1, poolw=1, back=2, mix=3,
                         turn=4, scores=5)
            for pos in sorted(todo):
                steps.setdefault(min(pos, base + 12), []).extend(sorted(todo[pos], key=lambda s: order[s[0]]))
    products = [c for c in chunks if c["kind"] != "M"]
    for n, c in enumerate(products):
        c["p"] = n
    return chunks, products, heads, steps, norm


def kernel_program(nc, xT, memT, consts, consts2, pos, par1, par2, bias, W, out):
    chunks, products, heads, steps, LAST = plan()
    END1 = 3 * DEPTH
    ctx = ExitStack()
    with ctx:
        def sb(name, shape, dt=F32, where=ctx):
            return where.enter_context(nc.sbuf_tensor(name, shape, dt))

        def sem(name):
            return ctx.enter_context(nc.semaphore(name))

        raw = sb("raw", [P, RING, CH])
        whi = sb("whi", [P, RING, CH], F32R)
        wlo = sb("wlo", [P, RING, CH], F32R)
        x = sb("x", [P, KT, S])
        xh = sb("xh", [P, KT, S], F32R)
        xl = sb("xl", [P, KT, S], F32R)
        c0 = sb("c0", [P, NC0])
        ones = sb("ones", [P, P])
        par = sb("par", [P, NP1])
        small = sb("small", [P, 64])
        mrs = sb("mrs", [P, 16])
        negmax = sb("negmax", [P, 16])
        rsum = sb("rsum", [P, 16])
        diag = sb("diag", [P, 2, 2, P])
        rstdb = sb("rstdb", [P, S])
        rraw = sb("rraw", [P, 2, 512])
        osq = sb("osq", [P, 2 * P])

        lnreg = ExitStack()
        sq = sb("sq", [P, 2, 512], where=lnreg)
        acc = sb("acc", [P, 2, 512], where=lnreg)
        cen = sb("cen", [P, 2, 512], where=lnreg)
        lnreg.close()
        logit = sb("logit", [P, 2, 2, S])
        ew = sb("ew", [P, 4, S])
        wd = sb("wd", [P, 2, S])
        eT = sb("eT", [P, 2, 2, S])
        otok = sb("otok", [P, 2, S])

        part1 = ExitStack()
        yh = sb("yh", [P, 3, 4, S], F32R, part1)
        yl = sb("yl", [P, 3, 4, S], F32R, part1)
        att = ExitStack()
        biasr = sb("biasr", [P, 3, 2, S], where=att)
        qr = sb("qr", [P, 4, S], where=att)
        kr = sb("kr", [P, 4, S], where=att)
        qb = sb("qb", [P, 4, S], where=att)
        kb = sb("kb", [P, 4, S], where=att)
        va = sb("va", [P, 2, 512], where=att)
        vb = sb("vb", [P, 2, 512], where=att)
        att.close()
        mrg = ExitStack()
        mh = sb("mh", [P, KT, S], F32R, mrg)
        ml = sb("ml", [P, KT, S], F32R, mrg)
        macc = sb("macc", [P, 4, S], where=mrg)
        mrg.close()
        hold = ExitStack()
        _skip = sb("skip_att", [P, 30 * 256], where=hold)
        gates = sb("gates", [P, 3, 4, S], where=hold)
        gbv = sb("gbv", [P, 2, S], where=hold)
        gcv = sb("gcv", [P, 2, S], where=hold)
        pc = sb("pc", [P, 2, S + 2], where=hold)
        cv = sb("cv", [P, 2, S], where=hold)
        mtmp = sb("mtmp", [P, 4, S], where=hold)
        hold.close()
        part1.close()
        xat = ExitStack()
        memh = sb("memh", [P, KT, S], F32R, xat)
        meml = sb("meml", [P, KT, S], F32R, xat)
        _skip2 = sb("skip_y", [P, 8 * 256], where=xat)
        _skip3 = sb("skip_m", [P, 20 * 256], where=xat)
        kx = sb("kx", [P, KT, S], where=xat)
        vx = sb("vx", [P, 2, D], where=xat)
        qx = sb("qx", [P, 2, 2, S], where=xat)
        xat.close()
        oxs = ExitStack()
        _skip4 = sb("skip_mem", [P, 24 * 256], where=oxs)
        oh = sb("oh", [P, KT, S], F32R, oxs)
        ol = sb("ol", [P, KT, S], F32R, oxs)
        oxs.close()
        ff = ExitStack()
        fu = sb("fu", [P, 2, 512], where=ff)
        fgp = sb("fgp", [P, 2, 2, S + 2], where=ff)
        fa = sb("fa", [P, 512], where=ff)
        fth = sb("fth", [P, 512], where=ff)
        fp = sb("fp", [P, 512], where=ff)
        fh = sb("fh", [P, 2, 2, S], F32R, ff)
        fl = sb("fl", [P, 2, 2, S], F32R, ff)
        cc = sb("cc", [P, NC2], where=ff)
        cs2 = sb("cs2", [P, 2, S], where=ff)
        angle = sb("angle", [P, 2, S], where=ff)
        posf = sb("posf", [P, S], where=ff)
        posi = sb("posi", [P, S], mybir.dt.int32, ff)
        q2 = sb("q2", [P, 2, 2, S], where=ff)
        k2 = sb("k2", [P, 2, 2, S], where=ff)
        v2 = sb("v2", [P, 2, 512], where=ff)
        up = sb("up", [P, 2, S], where=ff)
        pooled = sb("pooled", [P, 2, S], where=ff)
        hpad = sb("hpad", [P, 2, S + TAPS - 1], where=ff)
        sgm = sb("sgm", [P, 512], where=ff)
        yc = sb("yc", [P, 2, S], where=ff)
        yc2 = sb("yc2", [P, 2, S], where=ff)
        zh = sb("zh", [P, KT, S], F32R, ff)
        zl = sb("zl", [P, KT, S], F32R, ff)
        ff.close()

        accM = ctx.enter_context(nc.psum_tensor("accM", [P, 4, 512], F32))
        scoreP = ctx.enter_context(nc.psum_tensor("scoreP", [P, 2, 512], F32))
        turnP = ctx.enter_context(nc.psum_tensor("turnP", [P, 512], F32))
        outP = ctx.enter_context(nc.psum_tensor("outP", [P, 512], F32))

        def con(name):
            return c0[:, C0[name][0]:C0[name][1]]

        ident = con("ident")

        def col(name, i, n=1, table=P1):
            a = table[name][0] + i
            return par[:, a:a + n]

        poolm = cc[:, 0:2048].rearrange("p (t g s) -> p t g s", t=2, g=4)
        biasc = cc[:, 2048:3072].rearrange("p (b t s) -> p b t s", b=2, t=2)

        banks_of, claims, turn = {}, {}, 0
        for c in chunks:
            if c["role"] in ("fu", "fg", "sg", "su"):
                odd, second = c["j"] % 2, c["role"] in ("fg", "su")
                name = ("out" if second else "turn") if odd else f"score{int(second)}"
                claims[c["c"]] = [name]
                banks_of[c["c"]] = {"out": outP, "turn": turnP}[name][:, :] if odd else scoreP[:, int(second), :]
            elif c["kind"] in ("F", "T"):
                claims[c["c"]] = [f"acc{turn % 4}"]
                banks_of[c["c"]] = accM[:, turn % 4, :]
                turn += 1
            elif c["kind"] == "B":
                turn += turn % 2
                claims[c["c"]] = [f"acc{turn % 4}", f"acc{turn % 4 + 1}"]
                banks_of[c["c"]] = accM[:, turn % 4:turn % 4 + 2, :].rearrange("p b n -> p (b n)")
                turn += 2

        def sig(name, keys):
            return Signal(sem(name), keys)

        stage = {}
        for c in chunks:
            for name, what, *more in steps.get(c["c"], []):
                key = what["n"] if isinstance(what, dict) and "n" in what else what["c"] if isinstance(what, dict) \
                    else what
                stage.setdefault(name, []).append(key)
        hs = {h["n"]: h for h in heads}
        cs = [c["c"] for c in chunks]
        landed = [sem(f"landed{i}") for i in range(RING)]
        split_hi = sig("split_hi", cs)
        split_lo = sig("split_lo", cs)
        used = sig("used", [c["c"] for c in products if "ends" not in c])
        ACT_TAKES = ("dq", "dk", "va", "qb", "kb", "vb", "gb", "gc", "gate", "xk", "xv", "xq", "fu", "fg",
                     "vm", "vd", "up")
        DVE_TAKES = ("hc", "branch", "sg", "su", "qm", "km", "qd", "kd", "cg", "ca")
        act_took = sig("act_took", [c["c"] for c in products if c["role"] in ACT_TAKES])
        dve_took = sig("dve_took", [c["c"] for c in products if c["role"] in DVE_TAKES])

        def finished(c):
            return (obank, (c["ends"], NB - 1)) if "ends" in c else (used, c["c"])

        def await_chunk(engine, c):
            signal, key = finished(c)
            engine.wait_ge(signal.sem, signal.at(key))

        def taker(c):
            return (act_took if c["role"] in ACT_TAKES else dve_took), c["c"]

        norms = list(range(LAST + 1))
        ended = [n for n in norms if n not in (0, END1 + 1)]
        lns = [n for n in norms if n <= END1]
        fed = [n for n in norms if n not in (END1, LAST)]
        obank = sig("obank", [(n, b) for n in ended for b in range(NB)])
        resid = sig("resid", [(n, b) for n in ended for b in range(NB)])
        squared = sig("squared", [(n, b) for n in norms for b in range(NB)])
        summed = sig("summed", [(n, b) for n in norms for b in range(1, NB)])
        stats = sig("stats", norms)
        varied = sig("varied", norms)
        rooted = sig("rooted", norms)
        diaged = sig("diaged", norms)
        spread = sig("spread", norms)
        centred = sig("centred", [(n, b) for n in lns + [LAST] for b in range(NB)])
        xnew = sig("xnew", [(n, b) for n in lns + [LAST] for b in range(NB)])
        spread_kept = sig("spread_kept", [n for n in norms if END1 < n < LAST])
        xhi = sig("xhi", [(n, b) for n in fed for b in range(NB)])
        xlo = sig("xlo", [(n, b) for n in fed for b in range(NB)])
        x_in = sem("x_in")
        c0_in = sem("c0_in")
        cc_in = sem("cc_in")
        par_in = sem("par_in")
        pos_in = sem("pos_in")
        set_up = sem("set_up")
        bias_in = [sem(f"bias_in{i}") for i in range(3)]
        out_done = sem("out_done")

        scored = sig("scored", stage["scores"])
        biased = sig("biased", [n for n in stage["scores"] if hs[n]["kind"] in ("win", "moba", "dil")])
        maxed = sig("maxed", stage["scores"])
        expd = sig("expd", stage["scores"])
        weighed = sig("weighed", [n for n in stage["scores"] if hs[n]["kind"] == "diff"])
        inverted = sig("inverted", stage["scores"])
        turned = sig("turned", stage["turn"])
        turn_kept = sig("turn_kept", stage["turn"])
        mixed = sig("mixed", stage["mix"])
        oscaled = sig("oscaled", stage["mix"])
        o2 = sig("o2", [n for n in stage["mix"] if hs[n]["kind"] == "diff"])
        omean = sig("omean", [n for n in stage["mix"] if hs[n]["kind"] == "diff"])
        oroot = sig("oroot", [n for n in stage["mix"] if hs[n]["kind"] == "diff"])
        backed = sig("backed", stage["back"])
        back_hi = sig("back_hi", stage["back"])
        back_lo = sig("back_lo", stage["back"])
        rotated = sig("rotated", stage["rot"])
        roped = sig("roped", stage["rot"])
        lam_sum = sig("lam_sum", range(DEPTH))
        lam_exp = sig("lam_exp", range(DEPTH))
        yc_sum = sig("yc_sum", [(l, j) for l in range(DEPTH) for j in range(2)])
        yc_hi = sig("yc_hi", [(l, j) for l in range(DEPTH) for j in range(2)])
        yc_lo = sig("yc_lo", [(l, j) for l in range(DEPTH) for j in range(2)])
        merged = sig("merged", [(l, h) for l in range(DEPTH) for h in range(2)])
        merged_hi = sig("merged_hi", [(l, h) for l in range(DEPTH) for h in range(2)])
        merged_lo = sig("merged_lo", [(l, h) for l in range(DEPTH) for h in range(2)])
        groups = [c["c"] for c in chunks if c["role"] in ("fg", "su")]
        gated = [c["c"] for c in chunks if c["role"] in ("fg", "sg")]
        f_conv = sig("f_conv", [c["c"] for c in chunks if c["role"] == "fg"])
        f_tanh = sig("f_tanh", [c for c in gated])
        f_prod = sig("f_prod", groups)
        f_hi = sig("f_hi", groups)
        f_lo = sig("f_lo", groups)
        L2 = list(range(DEPTH, 2 * DEPTH))
        cg_tanh = sig("cg_tanh", L2)
        tapped = sig("tapped", L2)
        c_sq = sig("c_sq", L2)
        c_stats = sig("c_stats", L2)
        c_var = sig("c_var", L2)
        c_root = sig("c_root", L2)
        c_diag = sig("c_diag", L2)
        c_spread = sig("c_spread", L2)
        c_cen = sig("c_cen", L2)
        c_norm = sig("c_norm", L2)
        c_tanh = sig("c_tanh", L2)
        c_act = sig("c_act", L2)
        c_hi = sig("c_hi", L2)
        c_lo = sig("c_lo", L2)
        pool_done = sig("pool_done", L2)
        pool_kept = sig("pool_kept", L2)
        poolw_done = sig("poolw_done", L2)
        poolw_hi = sig("poolw_hi", L2)
        poolw_lo = sig("poolw_lo", L2)
        angled = sem("angled")
        tabled = sem("tabled")

        by_role = {}
        for c in chunks:
            by_role.setdefault((c["role"], c["l"]), []).append(c)
        part2_from = by_role["sg", DEPTH][0]["c"]
        wins = [n for n in stage["scores"] if hs[n]["kind"] == "win"]

        def slot(c):
            return c["p"] % RING

        def layer_of(c):
            return c["l"] % DEPTH

        def unpack(t, c):
            v = t[:, slot(c), :]
            if c["kind"] == "B":
                return v.rearrange("p (k n) -> p k n", k=4)
            if c["kind"] == "O":
                return v.rearrange("p (k n) -> p k n", k=2)
            return v.rearrange("p (k n) -> p k n", k=KT)

        def head_place(kind, j, part):
            if kind in ("diff", "win"):
                return (yh, yl)[part][:, 0, j, :] if kind == "diff" else (yh, yl)[part][:, 1, j // 2, :]
            return (zh, zl)[part][:, (2 if kind == "moba" else 4) + j // 2, :]

        def inverse_column(kind, j):
            return 4 if kind == "diff" else 4 + 2 * (j % (4 if kind in ("moba", "dil") else 2))

        mean, var = small[:, 0:2], small[:, 2:4]
        root, mroot = small[:, 4:6], small[:, 6:8]
        msq = small[:, 8:10]
        cmean, cvar = small[:, 10:12], small[:, 12:14]
        croot, cmroot = small[:, 14:16], small[:, 16:18]
        cmsq = small[:, 18:20]
        lamv, lame, neglam, gsub = small[:, 20:22], small[:, 22:24], small[:, 24:25], small[:, 25:26]
        oss, oms, ort = small[:, 26:28], small[:, 28:30], small[:, 30:32]
        mhalf = small[:, 32:34]

        block = ctx.enter_context(nc.Block())

        @block.sync
        def _(sp):
            for b in range(NB):
                sp.dma_start(x[:, 2 * b:2 * b + 2, :], xT[:, 2 * b:2 * b + 2, :]).then_inc(x_in, 16)
            sp.dma_start(c0[:, :], consts).then_inc(c0_in, 16)
            nbias = 0
            for c in chunks:
                r = c["c"] % RING
                if c["c"] >= RING:
                    sp.wait_ge(split_lo.sem, split_lo.at(c["c"] - RING))
                src = memT if c["kind"] == "M" else W[c["p"]]
                sp.dma_start(raw[:, r, :], src).then_inc(landed[r], 16)
                for n in wins:
                    if c["c"] == by_role["dq", hs[n]["l"]][0]["c"] + 12 + hs[n]["j"]:
                        if nbias >= 3:
                            sp.wait_ge(biased.sem, biased.at(wins[nbias - 3]))
                        sp.dma_start(biasr[:, nbias % 3, :, :], bias[nbias]).then_inc(bias_in[nbias % 3], 16)
                        nbias += 1
            for b in range(NB):
                sp.wait_ge(xnew.sem, xnew.at((LAST, b)))
                sp.dma_start(out[:, 2 * b:2 * b + 2, :], x[:, 2 * b:2 * b + 2, :]).then_inc(out_done, 16)
            sp.wait_ge(out_done, 16 * NB)

        @block.gpsimd
        def _(pool):
            nc.gpsimd.memset(ones[:, :], 1.0).then_inc(set_up, 1)
            nc.gpsimd.memset(mhalf, -0.5).then_inc(set_up, 1)
            pool.wait_ge(set_up, 2)
            pool.dma_start(par[:, 0:NP1], par1[0]).then_inc(par_in, 16)

            def norm(n):
                pool.wait_ge(varied.sem, varied.at(n))
                nc.gpsimd.tensor_tensor(root, var, mhalf, ALU.pow).then_inc(rooted.sem, 1)
                if n == LNS:
                    pool.wait_ge(xnew.sem, xnew.at((n, NB - 1)))
                    pool.dma_start(par[:, 0:NP1], par1[1]).then_inc(par_in, 16)
                if n == END1 - 1:
                    last = by_role["xo", DEPTH - 1][-1]
                    await_chunk(pool, last)
                    pool.dma_start(cc[:, :], consts2).then_inc(cc_in, 16)
                    pool.dma_start(posi[:, :], pos).then_inc(pos_in, 16)
                if n == END1:
                    pool.wait_ge(xnew.sem, xnew.at((n, NB - 1)))
                    pool.dma_start(par[:, 0:NP2], par2[0]).then_inc(par_in, 16)
                if n == END1 + 3:
                    pool.wait_ge(xlo.sem, xlo.at((n, NB - 1)))
                    pool.dma_start(par[:, 0:NP2], par2[1]).then_inc(par_in, 16)

            norm(0)
            for c in chunks:
                for name, what, *more in steps.get(c["c"], []):
                    if name == "mix" and what["kind"] == "diff":
                        pool.wait_ge(omean.sem, omean.at(what["n"]))
                        nc.gpsimd.tensor_tensor(ort, oms, mhalf, ALU.pow).then_inc(oroot.sem, 1)
                    if name == "cstats":
                        pool.wait_ge(c_var.sem, c_var.at(what))
                        nc.gpsimd.tensor_tensor(croot, cvar, mhalf, ALU.pow).then_inc(c_root.sem, 1)
                if "ends" in c:
                    norm(c["ends"])
                    if c["ends"] == END1:
                        norm(END1 + 1)

        @block.scalar
        def _(act):
            def split(c):
                n = c["c"]
                act.wait_ge(landed[n % RING], 16 * (n // RING + 1))
                if c["kind"] == "M":
                    act.wait_ge(used.sem, used.at(c["after"]))
                    nc.scalar.activation(memh[:, :, :].rearrange("p k s -> p (k s)"), raw[:, n % RING, :],
                                         ACT.Copy).then_inc(split_hi.sem, 1)
                    return
                if c["p"] >= RING:
                    await_chunk(act, products[c["p"] - RING])
                nc.scalar.activation(whi[:, slot(c), :], raw[:, n % RING, :], ACT.Copy).then_inc(split_hi.sem, 1)

            def split_at(pos):
                if pos < len(chunks):
                    split(chunks[pos])

            def norm(n, between=None):
                for b in range(NB):
                    if n in ended:
                        act.wait_ge(resid.sem, resid.at((n, b)))
                    elif n == 0:
                        act.wait_ge(x_in, 16 * NB)
                    else:
                        act.wait_ge(xnew.sem, xnew.at((END1, b)))
                    if n > END1 and n != LAST:
                        if b == 0:
                            act.wait_ge(par_in, 16 * (DEPTH + 1 + (n > END1 + 3)))
                        for m in range(2):
                            k = 2 * b + m
                            g = col("norm_g", ((n - END1 - 1) % 3) * KT + k, 1, P2)
                            ins = nc.scalar.activation(xh[:, k, :], x[:, k, :], ACT.Copy, scale=g)
                        ins.then_inc(xhi.sem, 1)
                    if b >= 2:
                        act.wait_ge(summed.sem, summed.at((n, b - 1)))
                    nc.scalar.activation(sq[:, b % 2, :], x[:, 2 * b:2 * b + 2, :].rearrange("p k s -> p (k s)"),
                                         ACT.Square).then_inc(squared.sem, 1)
                if between:
                    between()
                if END1 < n < LAST:
                    return
                if n == 0:
                    act.wait_ge(c0_in, 16)
                elif n == LAST:
                    pass
                else:
                    act.wait_ge(par_in, 16 * (1 + (n > LNS)))
                for b in range(NB):
                    act.wait_ge(centred.sem, centred.at((n, b)))
                    for m in range(2):
                        k = 2 * b + m
                        src = cen[:, b % 2, m * S:(m + 1) * S]
                        if n == LAST:
                            g0 = C0["fin_g"][0] + k
                            ins = nc.scalar.activation(x[:, k, :], src, ACT.Copy, scale=c0[:, g0:g0 + 1])
                        else:
                            if n == 0:
                                g, bb = (c0[:, C0[q][0] + k:C0[q][0] + k + 1] for q in ("emb_g", "emb_b"))
                            else:
                                g, bb = (col(q, ((n - 1) % 3) * KT + k) for q in ("ln_g", "ln_b"))
                            ins = nc.scalar.activation(x[:, k, :], src, ACT.Identity, bias=bb, scale=g)
                    ins.then_inc(xnew.sem, 1)
                    if n in fed:
                        act.wait_ge(xnew.sem, xnew.at((n, b)))
                        nc.scalar.activation(xh[:, 2 * b:2 * b + 2, :], x[:, 2 * b:2 * b + 2, :], ACT.Copy)\
                            .then_inc(xhi.sem, 1)

            def copy_out(dst, c, bank_ap):
                act.wait_ge(used.sem, used.at(c["c"]))
                nc.scalar.activation(dst, bank_ap, ACT.Copy).then_inc(act_took.sem, 1)

            def take(c, pos):
                r, j, l = c["role"], c["j"], c["l"]
                if "ends" in c:
                    norm(c["ends"], lambda: split_at(pos + 2))
                    if c["ends"] == END1:
                        norm(END1 + 1)
                    return
                src = banks_of[c["c"]] if c["kind"] not in ("O", "M") else None
                pair = src.rearrange("p (m s) -> p m s", m=2) if c["kind"] in ("F", "T") else None
                if r in ("dq", "dk"):
                    copy_out(rraw[:, (r == "dk") * 1, :], c, src)
                elif r in ("va", "vb"):
                    copy_out((va if r == "va" else vb)[:, :, j * S:(j + 1) * S], c, pair)
                elif r in ("qb", "kb"):
                    copy_out((qb if r == "qb" else kb)[:, 2 * j:2 * j + 2, :], c, pair)
                elif r in ("gb", "gc"):
                    if j == 1:
                        act.wait_ge(yc_sum.sem, yc_sum.at((layer_of(c), 0)))
                    copy_out((gbv if r == "gb" else gcv)[:, :, :], c, pair)
                elif r == "hc":
                    key = (layer_of(c), j)
                    act.wait_ge(yc_sum.sem, yc_sum.at(key))
                    nc.scalar.activation(yh[:, 2, 2 * j:2 * j + 2, :], cv[:, :, :], ACT.Copy)\
                        .then_inc(yc_hi.sem, 1)
                elif r == "gate":
                    if c["half"] == 1:
                        old = [b for b in by_role["branch", l] if b["half"] == 0 and b["b"] == c["b"]][0]
                        act.wait_ge(dve_took.sem, dve_took.at(old["c"]))
                    act.wait_ge(used.sem, used.at(c["c"]))
                    nc.scalar.activation(gates[:, c["b"], 2 * j:2 * j + 2, :], pair, ACT.Tanh, scale=0.5)\
                        .then_inc(act_took.sem, 1)
                elif r == "branch" and c["b"] == 2:
                    key = (layer_of(c), c["half"])
                    act.wait_ge(merged.sem, merged.at(key))
                    nc.scalar.activation(mh[:, 4 * c["half"]:4 * c["half"] + 4, :], macc[:, :, :], ACT.Copy,
                                         scale=0.5).then_inc(merged_hi.sem, 1)
                elif r == "xk":
                    copy_out(kx[:, 2 * j:2 * j + 2, :], c, pair)
                elif r == "xv":
                    copy_out(vx[:, :, j * S:(j + 1) * S], c, pair)
                elif r == "xq":
                    copy_out(qx[:, j % 2, :, :], c, pair)
                elif r == "fu":
                    copy_out(fu[:, j % 2, :], c, src)
                elif r == "fg":
                    copy_out(fgp[:, j % 2, :, 1:S + 1], c, pair)
                    split_at(pos + 2)
                    act.wait_ge(f_conv.sem, f_conv.at(c["c"]))
                    nc.scalar.activation(fth[:, :], fa[:, :], ACT.Tanh, scale=0.5).then_inc(f_tanh.sem, 1)
                    hidden(c)
                    return
                elif r == "sg":
                    act.wait_ge(dve_took.sem, dve_took.at(c["c"]))
                    nc.scalar.activation(fth[:, :], fa[:, :], ACT.Tanh, scale=0.5).then_inc(f_tanh.sem, 1)
                elif r == "su":
                    split_at(pos + 2)
                    hidden(c)
                    return
                elif r in ("vm", "vd", "up"):
                    act.wait_ge(used.sem, used.at(c["c"]))
                    act.wait_ge(rooted.sem, rooted.at(END1 + 2 + 3 * layer_of(c)))
                    for t in range(2):
                        dst = up[:, t, :] if r == "up" else v2[:, t, (r == "vd") * S:(r == "vd") * S + S]
                        ins = nc.scalar.activation(dst, pair[:, t, :], ACT.Copy, scale=root[:, t:t + 1])
                    ins.then_inc(act_took.sem, 1)
                elif r == "cg":
                    act.wait_ge(dve_took.sem, dve_took.at(c["c"]))
                    nc.scalar.activation(sgm[:, :], sgm[:, :], ACT.Tanh, scale=0.5).then_inc(cg_tanh.sem, 1)
                if r != "ends":
                    split_at(pos + 2)

            def hidden(c):
                j = c["j"]
                if (j >= 2):
                    down = by_role["fo" if c["role"] == "fg" else "sd", c["l"]]
                    down = [d for d in down if d.get("f") == c.get("f") and d["j"] == j - 2][0]
                    await_chunk(act, down)
                act.wait_ge(f_prod.sem, f_prod.at(c["c"]))
                nc.scalar.activation(fh[:, j % 2, :, :].rearrange("p m s -> p (m s)"), fp[:, :], ACT.Copy,
                                     scale=0.5).then_inc(f_hi.sem, 1)

            def step(name, what):
                if name == "lam":
                    act.wait_ge(lam_sum.sem, lam_sum.at(what))
                    nc.scalar.activation(lame, lamv, ACT.Exp).then_inc(lam_exp.sem, 1)
                elif name == "scores":
                    n, kind = what["n"], what["kind"]
                    scale = 0.125 if kind == "diff" else 1.0 if kind != "xa" else 0.0625
                    e0 = 0 if kind == "diff" else 2 * (what["j"] % 2)
                    act.wait_ge(maxed.sem, maxed.at(n))
                    for i in range(4 if kind == "diff" else 2):
                        if kind == "diff":
                            src = scoreP[:, i // 2, (i % 2) * S:(i % 2 + 1) * S]
                        elif kind == "xa":
                            src = scoreP[:, what["j"] % 2, i * S:(i + 1) * S]
                        else:
                            src = logit[:, what["j"] % 2, i, :]
                        ins = nc.scalar.activation(ew[:, e0 + i, :], src, ACT.Exp, bias=negmax[:, e0 + i:e0 + i + 1],
                                                   scale=scale, accum_out=rsum[:, e0 + i:e0 + i + 1])
                    ins.then_inc(expd.sem, 1)
                elif name == "turn":
                    n = what["n"]
                    act.wait_ge(turned.sem, turned.at(n))
                    nc.scalar.activation(eT[:, what["j"] % 2, :, :].rearrange("p a b -> p (a b)"), turnP[:, :],
                                         ACT.Copy).then_inc(turn_kept.sem, 1)
                elif name == "mix" and what["kind"] == "diff":
                    n = what["n"]
                    act.wait_ge(mixed.sem, mixed.at(n))
                    for t in range(2):
                        ins = nc.scalar.activation(osq[:, t * P:(t + 1) * P], outP[:, t * P:(t + 1) * P], ACT.Square,
                                                   accum_out=oss[:, t:t + 1])
                    ins.then_inc(o2.sem, 1)
                elif name == "back":
                    n, kind, j = what["n"], what["kind"], what["j"]
                    act.wait_ge(backed.sem, backed.at(n))
                    if kind == "xa":
                        dst, kw = oh[:, 2 * j:2 * j + 2, :].rearrange("p a b -> p (a b)"), {}
                        src = outP[:, :]
                    else:
                        src = outP[:, 0:S]
                        dst = head_place(kind, j, 0)
                        kw = dict(scale=gsub) if kind == "diff" else {}
                    nc.scalar.activation(dst, src, ACT.Copy, **kw).then_inc(back_hi.sem, 1)
                elif name == "trig":
                    act.wait_ge(angled, 1)
                    nc.scalar.activation(cs2[:, :, :], angle[:, :, :], ACT.Sin).then_inc(tabled, 1)
                elif name == "csquare":
                    act.wait_ge(tapped.sem, tapped.at(what))
                    nc.scalar.activation(yc2[:, :, :], yc[:, :, :], ACT.Square).then_inc(c_sq.sem, 1)
                elif name == "cspread":
                    act.wait_ge(c_cen.sem, c_cen.at(what))
                    for m in range(2):
                        ins = nc.scalar.activation(yc2[:, m, :], yc[:, m, :], ACT.Identity,
                                                   bias=col("cln_b", m, 1, P2), scale=col("cln_g", m, 1, P2))
                    ins.then_inc(c_norm.sem, 1)
                    act.wait_ge(c_norm.sem, c_norm.at(what))
                    nc.scalar.activation(sgm[:, :], yc2[:, :, :].rearrange("p a b -> p (a b)"), ACT.Tanh,
                                         scale=0.5).then_inc(c_tanh.sem, 1)
                    act.wait_ge(c_act.sem, c_act.at(what))
                    nc.scalar.activation(zh[:, 6:8, :], yc[:, :, :], ACT.Copy, scale=0.5).then_inc(c_hi.sem, 1)
                elif name == "pool":
                    act.wait_ge(pool_done.sem, pool_done.at(what["l"]))
                    nc.scalar.activation(pooled[:, :, :].rearrange("p a b -> p (a b)"), outP[:, :], ACT.Copy)\
                        .then_inc(pool_kept.sem, 1)
                elif name == "poolw":
                    act.wait_ge(poolw_done.sem, poolw_done.at(what["l"]))
                    for m in range(2):
                        ins = nc.scalar.activation(zh[:, m, :], outP[:, m * S:(m + 1) * S], ACT.Copy,
                                                   scale=col("pool_s", m, 1, P2))
                    ins.then_inc(poolw_hi.sem, 1)

            norm(0)
            split_at(0)
            split_at(1)
            for c in chunks:
                pos = c["c"]
                if pos == 0:
                    split_at(2)
                else:
                    take(chunks[pos - 1], pos)
                for name, what, *more in steps.get(pos, []):
                    step(name, what)
            take(chunks[-1], len(chunks))

        @block.tensor
        def _(pe):
            accB = [Bank() for _ in range(4)]
            scoreB = [Bank() for _ in range(2)]
            turnB, outB = Bank(), Bank()
            bank = {"turn": turnB, "out": outB, "score0": scoreB[0], "score1": scoreB[1]}
            bank.update({f"acc{i}": b for i, b in enumerate(accB)})

            def mm(dst, a, b, start, stop=True):
                return nc.tensor.matmul(dst, a, b, start=start, stop=stop, skip_group_check=True)

            def norm_stats(n):
                outB.claim(pe, varied, n)
                pe.wait_ge(summed.sem, summed.at((n, NB - 1)))
                for t in range(2):
                    for q in range(2) if n <= END1 else (1,):
                        for half in range(2):
                            a = acc[:, q, half * S + t * P:half * S + (t + 1) * P]
                            ins = mm(outP[:, 2 * t + q:2 * t + q + 1], a, ones[:, 0:1], half == 0, half == 1)
                ins.then_inc(stats.sem, 1)

            def norm_spread(n):
                turnB.claim(pe, *((centred, (n, NB - 1)) if n in lns + [LAST] else (spread_kept, n)))
                pe.wait_ge(diaged.sem, diaged.at(n))
                for q in range(2 if n in lns else 1):
                    for t in range(2):
                        ins = mm(turnP[:, q * S + t * P:q * S + (t + 1) * P], ones[:, :], diag[:, t, q, :], True)
                ins.then_inc(spread.sem, 1)

            def product(c, hooks):
                r, kind = c["role"], c["kind"]
                if kind == "M":
                    return
                pe.wait_ge(split_lo.sem, split_lo.at(c["c"]))
                hi, lo = unpack(whi, c), unpack(wlo, c)
                a_hi, a_lo = (mh, ml) if r == "mo" else (oh, ol) if r == "xo" else (zh, zl) if r == "wo" \
                    else (memh, meml) if r in ("xk", "xv") else (xh, xl)
                if r in ("fo", "sd"):
                    a_hi, a_lo = fh[:, c["j"] % 2, :, :], fl[:, c["j"] % 2, :, :]
                if r in ("xk", "xv"):
                    mem = by_role["mem", c["l"]][0]["c"]
                    pe.wait_ge(split_lo.sem, split_lo.at(mem))
                if kind in ("F", "T"):
                    for name in claims[c["c"]]:
                        bank[name].claim(pe, *taker(c))
                    dst = banks_of[c["c"]]
                    for k in range(KT):
                        for fn in hooks.get(k, []):
                            fn()
                        if c.get("norm") is not None and k % 2 == 0:
                            pe.wait_ge(xlo.sem, xlo.at((c["norm"], k // 2)))
                        for m in range(2):
                            first, last = k == 0 and m == 0, k == KT - 1
                            o = dst[:, m * S:(m + 1) * S]
                            if kind == "F":
                                w_hi, w_lo = hi[:, k, m * P:(m + 1) * P], lo[:, k, m * P:(m + 1) * P]
                                mm(o, w_hi, a_hi[:, k, :], first, False)
                                mm(o, w_hi, a_lo[:, k, :], False, False)
                                ins = mm(o, w_lo, a_hi[:, k, :], False, last)
                            else:
                                t_hi, t_lo = a_hi[:, k, m * P:(m + 1) * P], a_lo[:, k, m * P:(m + 1) * P]
                                mm(o, t_hi, hi[:, k, :], first, False)
                                mm(o, t_hi, lo[:, k, :], False, False)
                                ins = mm(o, t_lo, hi[:, k, :], False, last)
                    ins.then_inc(used.sem, 1)
                elif kind == "B":
                    b = c["b"]
                    a_hi, a_lo = yh[:, b, :, :], yl[:, b, :, :]
                    need = {0: (back_lo, [h["n"] for h in heads if h["kind"] == "diff" and h["l"] == c["l"]][-1]),
                            1: (back_lo, [h["n"] for h in heads if h["kind"] == "win" and h["l"] == c["l"]][-1]),
                            2: (yc_lo, (c["l"], 1))}[b]
                    if c["half"] == 0:
                        pe.wait_ge(need[0].sem, need[0].at(need[1]))
                    for name in claims[c["c"]]:
                        bank[name].claim(pe, *taker(c))
                    dst = banks_of[c["c"]]
                    for k in range(4):
                        for m in range(4):
                            o = dst[:, m * S:(m + 1) * S]
                            w_hi, w_lo = hi[:, k, m * P:(m + 1) * P], lo[:, k, m * P:(m + 1) * P]
                            mm(o, w_hi, a_hi[:, k, :], k == 0 and m % 2 == 0, False)
                            mm(o, w_hi, a_lo[:, k, :], False, False)
                            ins = mm(o, w_lo, a_hi[:, k, :], False, k == 3)
                    ins.then_inc(used.sem, 1)
                else:
                    n = next(d["ends"] for d in chunks[c["c"]:] if "ends" in d)
                    group = [d for d in by_role[r, c["l"]] if d.get("f") == c.get("f")]
                    j = c["j"]
                    if r == "mo":
                        pe.wait_ge(merged_lo.sem, merged_lo.at((c["l"], j // 2)))
                    elif r == "xo":
                        h = [h["n"] for h in heads if h["kind"] == "xa" and h["l"] == c["l"] and h["j"] == j][0]
                        pe.wait_ge(back_lo.sem, back_lo.at(h))
                    elif r == "fo":
                        pe.wait_ge(f_lo.sem, f_lo.at(by_role["fg", c["l"]][j]["c"]))
                    elif r == "sd":
                        g = [d for d in by_role["su", c["l"]] if d["f"] == c["f"] and d["j"] == j][0]
                        pe.wait_ge(f_lo.sem, f_lo.at(g["c"]))
                    elif j == 0:
                        pe.wait_ge(poolw_lo.sem, poolw_lo.at(c["l"]))
                    elif j == 3:
                        pe.wait_ge(c_lo.sem, c_lo.at(c["l"]))
                    else:
                        kind_ = "moba" if j == 1 else "dil"
                        h = [h["n"] for h in heads if h["kind"] == kind_ and h["l"] == c["l"]][-1]
                        pe.wait_ge(back_lo.sem, back_lo.at(h))
                    first, last = c is group[0], c is group[-1]
                    for b in range(NB):
                        if first:
                            accB[b].claim(pe, resid, (n, b))
                        for kk in range(2):
                            k = kk if r in ("fo", "sd") else 2 * j + kk
                            for m in (2 * b, 2 * b + 1):
                                o = accM[:, b, (m % 2) * S:(m % 2 + 1) * S]
                                w_hi, w_lo = hi[:, kk, m * P:(m + 1) * P], lo[:, kk, m * P:(m + 1) * P]
                                mm(o, w_hi, a_hi[:, k, :], first and kk == 0 and m % 2 == 0, False)
                                mm(o, w_hi, a_lo[:, k, :], False, False)
                                ins = mm(o, w_lo, a_hi[:, k, :], False, last and kk == 1)
                        if last and b < NB - 1:
                            ins.then_inc(obank.sem, 1)
                    if last:
                        ins.then_inc(obank.sem, 1)
                    else:
                        ins.then_inc(used.sem, 1)

            def step(name, what):
                if name == "rot":
                    c = what
                    p2 = c["role"] in ("qm", "km", "qd", "kd")
                    outB.claim(pe, roped, c["c"])
                    pe.wait_ge((dve_took if p2 else act_took).sem, (dve_took if p2 else act_took).at(c["c"]))
                    i = 1 if c["role"] in ("dk", "km", "kd") else 0
                    mm(outP[:, :], con("rot2" if p2 else "rot1"), rraw[:, i, :], True).then_inc(rotated.sem, 1)
                elif name == "scores":
                    n, kind, j = what["n"], what["kind"], what["j"]
                    if kind == "diff":
                        for i in range(2):
                            scoreB[i].claim(pe, expd, n)
                        pe.wait_ge(roped.sem, roped.at(by_role["dk", what["l"]][j // 2]["c"]))
                        for i in range(4):
                            mp, t = i // 2, i % 2
                            rows = slice(64 * mp, 64 * mp + 64)
                            ins = mm(scoreP[:, mp, t * S:(t + 1) * S], qr[rows, j, t * P:(t + 1) * P],
                                     kr[rows, j, :], True)
                    elif kind == "xa":
                        scoreB[j % 2].claim(pe, expd, n)
                        for r in ("xq", "xk"):
                            c = [c for c in by_role[r, what["l"]] if c["j"] == j][0]
                            pe.wait_ge(act_took.sem, act_took.at(c["c"]))
                        for t in range(2):
                            for k in range(2):
                                ins = mm(scoreP[:, j % 2, t * S:(t + 1) * S], qx[:, j % 2, k, t * P:(t + 1) * P],
                                         kx[:, 2 * j + k, :], k == 0, k == 1)
                    else:
                        scoreB[j % 2].claim(pe, biased, n)
                        rows = slice(64 * (j % 2), 64 * (j % 2) + 64)
                        if kind == "win":
                            q, k = qb[rows, j // 2, :], kb[rows, j // 2, :]
                            pe.wait_ge(act_took.sem, act_took.at(by_role["kb", what["l"]][j // 4]["c"]))
                        else:
                            i = (kind == "dil") * 1
                            q, k = q2[rows, i, j // 2, :], k2[rows, i, j // 2, :]
                            pe.wait_ge(roped.sem, roped.at(by_role["kd" if i else "km", what["l"]][0]["c"]))
                        for t in range(2):
                            ins = mm(scoreP[:, j % 2, t * S:(t + 1) * S], q[:, t * P:(t + 1) * P], k, True)
                    ins.then_inc(scored.sem, 1)
                elif name == "turn":
                    n, kind, j = what["n"], what["kind"], what["j"]
                    turnB.claim(pe, turn_kept, n)
                    if kind == "diff":
                        pe.wait_ge(weighed.sem, weighed.at(n))
                        src = [wd[:, t, :] for t in range(2)]
                    else:
                        pe.wait_ge(expd.sem, expd.at(n))
                        src = [ew[:, 2 * (j % 2) + t, :] for t in range(2)]
                    for t in range(2):
                        for k in range(2):
                            ins = nc.tensor.transpose(turnP[:, k * S + t * P:k * S + (t + 1) * P],
                                                      src[t][:, k * P:(k + 1) * P], ident)
                    ins.then_inc(turned.sem, 1)
                elif name == "mix":
                    n, kind, j, l = what["n"], what["kind"], what["j"], what["l"]
                    outB.claim(pe, oscaled, n)
                    pe.wait_ge(turn_kept.sem, turn_kept.at(n))
                    w = {"diff": P, "xa": S}.get(kind, 64)
                    v, c = {"diff": (va, by_role.get(("va", l))), "win": (vb, by_role.get(("vb", l))),
                            "moba": (v2, by_role.get(("vm", l))), "dil": (v2, by_role.get(("vd", l))),
                            "xa": (vx, by_role.get(("xv", l)))}[kind]
                    v0 = w * j + (S if kind == "dil" else 0)
                    c = c[{"diff": j // 2, "win": j // 4, "moba": 0, "dil": 0, "xa": 0}[kind]]
                    if kind == "xa":
                        c = [d for d in by_role["xv", l] if d["j"] == j][0]
                    pe.wait_ge(act_took.sem, act_took.at(c["c"]))
                    for t in range(2):
                        for k in range(2):
                            ins = mm(outP[:, t * w:(t + 1) * w], eT[:, j % 2, k, t * P:(t + 1) * P],
                                     v[:, k, v0:v0 + w], k == 0, k == 1)
                    ins.then_inc(mixed.sem, 1)
                elif name == "back":
                    n, kind, j = what["n"], what["kind"], what["j"]
                    outB.claim(pe, back_lo, n)
                    pe.wait_ge(oscaled.sem, oscaled.at(n))
                    for d in range(2 if kind == "xa" else 1):
                        for t in range(2):
                            ins = nc.tensor.transpose(outP[:, d * S + t * P:d * S + (t + 1) * P],
                                                      otok[:, t, d * P:(d + 1) * P], ident)
                    ins.then_inc(backed.sem, 1)
                elif name == "pool":
                    outB.claim(pe, pool_kept, what["l"])
                    pe.wait_ge(act_took.sem, act_took.at(what["c"]))
                    pe.wait_ge(cc_in, 16)
                    for g in range(4):
                        for t in range(2):
                            ins = mm(outP[64 * (g % 2):64 * (g % 2) + 64, (g // 2) * S:(g // 2 + 1) * S],
                                     up[:, t, 64 * g:64 * g + 64], poolm[:, t, g, :], t == 0, t == 1)
                    ins.then_inc(pool_done.sem, 1)
                elif name == "poolw":
                    outB.claim(pe, poolw_lo, what["l"])
                    pe.wait_ge(pool_kept.sem, pool_kept.at(what["l"]))
                    pw = par[:, P2["pool_w"][0]:P2["pool_w"][1]].rearrange("p (t d) -> p t d", t=2)
                    for g in range(4):
                        rows = slice(64 * (g % 2), 64 * (g % 2) + 64)
                        ins = mm(outP[rows, (g // 2) * S:(g // 2 + 1) * S], pw[rows, g // 2, :],
                                 pooled[rows, g // 2, :], True)
                    ins.then_inc(poolw_done.sem, 1)
                elif name == "cstats":
                    outB.claim(pe, c_var, what)
                    pe.wait_ge(c_sq.sem, c_sq.at(what))
                    for t in range(2):
                        for q in range(2):
                            for m in range(2):
                                a = (yc, yc2)[q][:, m, t * P:(t + 1) * P]
                                ins = mm(outP[:, 2 * t + q:2 * t + q + 1], a, ones[:, 0:1], m == 0, m == 1)
                    ins.then_inc(c_stats.sem, 1)
                elif name == "cspread":
                    outB.claim(pe, c_cen, what)
                    pe.wait_ge(c_diag.sem, c_diag.at(what))
                    for q in range(2):
                        for t in range(2):
                            ins = mm(outP[:, q * S + t * P:q * S + (t + 1) * P], ones[:, :], diag[:, t, q, :], True)
                    ins.then_inc(c_spread.sem, 1)

            pe.wait_ge(set_up, 2)
            pe.wait_ge(c0_in, 16)
            hooks = {}

            def hook(c, k, fn):
                hooks.setdefault(c, {}).setdefault(k, []).append(fn)

            norm_stats(0)
            norm_spread(0)
            for c in chunks:
                pos = c["c"]
                for name, what, *more in steps.get(pos, []):
                    step(name, what)
                product(c, hooks.get(pos, {}))
                n = c.get("ends")
                if n is None:
                    continue
                if c["role"] == "mo":
                    hook(pos + 1, 5, lambda n=n: norm_stats(n))
                    hook(pos + 2, 1, lambda n=n: norm_spread(n))
                elif n <= END1 or n == LAST:
                    norm_stats(n)
                    norm_spread(n)
                    if n == END1:
                        hook(pos + 1, 7, lambda n=n + 1: norm_stats(n))
                        hook(pos + 2, 3, lambda n=n + 1: norm_spread(n))
                else:
                    hook(pos + 1, 7, lambda n=n: norm_stats(n))
                    hook(pos + 2, 3, lambda n=n: norm_spread(n))

        @block.vector
        def _(dve):
            chain = sem("dve_chain")
            links = [0]

            def link(ins):
                links[0] += 1
                ins.then_inc(chain, 1)
                dve.wait_ge(chain, links[0])

            v = nc.vector

            def split(c):
                n = c["c"]
                dve.wait_ge(split_hi.sem, split_hi.at(n))
                if c["kind"] == "M":
                    v.tensor_tensor(meml[:, :, :].rearrange("p k s -> p (k s)"), raw[:, n % RING, :],
                                    memh[:, :, :].rearrange("p k s -> p (k s)").bitcast(F32), ALU.subtract)\
                        .then_inc(split_lo.sem, 1)
                    return
                v.tensor_tensor(wlo[:, slot(c), :], raw[:, n % RING, :], whi[:, slot(c), :].bitcast(F32),
                                ALU.subtract).then_inc(split_lo.sem, 1)

            def split_at(pos):
                if pos < len(chunks):
                    split(chunks[pos])

            def bank_of_x(b):
                return x[:, 2 * b:2 * b + 2, :]

            def norm(n, between=None):
                rms = n > END1
                accy, accq = acc[:, 0, :], acc[:, 1, :]
                split_here = rms and n != LAST

                def lo_part(b):
                    dve.wait_ge(xhi.sem, xhi.at((n, b)))
                    if not split_here:
                        v.tensor_tensor(xl[:, 2 * b:2 * b + 2, :], bank_of_x(b), xh[:, 2 * b:2 * b + 2, :].bitcast(F32),
                                        ALU.subtract).then_inc(xlo.sem, 1)
                        return
                    for m in range(2):
                        k = 2 * b + m
                        g = col("norm_g", ((n - END1 - 1) % 3) * KT + k, 1, P2)
                        ins = v.scalar_tensor_tensor(xl[:, k, :], x[:, k, :], g, xh[:, k, :].bitcast(F32),
                                                     ALU.mult, ALU.subtract)
                    ins.then_inc(xlo.sem, 1)

                def add_squares(b):
                    dve.wait_ge(squared.sem, squared.at((n, b)))
                    if b == 0:
                        return
                    if b > 1:
                        dve.wait_ge(summed.sem, summed.at((n, b - 1)))
                    a = sq[:, 0, :] if b == 1 else accq
                    v.tensor_tensor(accq, a, sq[:, b % 2, :], ALU.add).then_inc(summed.sem, 1)

                for b in range(NB):
                    if n in ended:
                        dve.wait_ge(obank.sem, obank.at((n, b)))
                        factor = ALPHA if n <= END1 else 0.5
                        p = accM[:, b, :].rearrange("p (m s) -> p m s", m=2)
                        if n <= END1:
                            ins = v.scalar_tensor_tensor(bank_of_x(b), bank_of_x(b), ALPHA, p, ALU.mult, ALU.add)
                        else:
                            f = 1.0 if (n - END1 - 1) % 3 == 2 else 0.5
                            ins = v.scalar_tensor_tensor(bank_of_x(b), p, f, bank_of_x(b), ALU.mult, ALU.add)
                        ins.then_inc(resid.sem, 1)
                    elif n == 0:
                        dve.wait_ge(x_in, 16 * NB)
                    else:
                        dve.wait_ge(xnew.sem, xnew.at((END1, b)))
                    if split_here:
                        lo_part(b)
                    if not rms and b >= 1:
                        if n in ended:
                            dve.wait_ge(resid.sem, resid.at((n, b)))
                        a = bank_of_x(0) if b == 1 else accy.rearrange("p (m s) -> p m s", m=2)
                        link(v.tensor_tensor(accy.rearrange("p (m s) -> p m s", m=2), a, bank_of_x(b), ALU.add))
                    if b >= 1:
                        add_squares(b - 1)
                add_squares(NB - 1)
                if between:
                    between()
                dve.wait_ge(stats.sem, stats.at(n))
                st = outP[:, 0:4].rearrange("p (t q) -> p q t", q=2)
                tiny_stats(st, 1.0 / D, not rms, mean, msq, var, LN_EPS if not rms else RMS_EPS, varied.sem)
                dve.wait_ge(rooted.sem, rooted.at(n))
                diagonals(not rms, mean, root, mroot, diaged.sem)
                if rms and n != LAST:
                    return
                dve.wait_ge(spread.sem, spread.at(n))
                for b in range(NB):
                    if b >= 2:
                        dve.wait_ge(xnew.sem, xnew.at((n, b - 2)))
                    c3 = cen[:, b % 2, :].rearrange("p (m s) -> p m s", m=2)
                    ra = turnP[:, 0:S].unsqueeze(1).broadcast_to([P, 2, S])
                    ma = turnP[:, S:2 * S].unsqueeze(1).broadcast_to([P, 2, S])
                    ins = v.tensor_tensor(c3, bank_of_x(b), ra, ALU.mult)
                    if not rms:
                        link(ins)
                        ins = v.tensor_tensor(c3, c3, ma, ALU.subtract)
                    ins.then_inc(centred.sem, 1)
                    if n in fed and b >= 1:
                        lo_part(b - 1)
                if n in fed:
                    lo_part(NB - 1)

            def tiny_stats(st, inv, centre, mean_, msq_, var_, eps, done):
                if centre:
                    link(v.tensor_scalar(mean_, st[:, 0, :], inv, None, ALU.mult))
                    link(v.tensor_tensor(msq_, mean_, mean_, ALU.mult))
                    link(v.scalar_tensor_tensor(var_, st[:, 1, :], inv, msq_, ALU.mult, ALU.subtract))
                    v.tensor_scalar(var_, var_, 0.0, eps, ALU.max, ALU.add).then_inc(done, 1)
                else:
                    v.tensor_scalar(var_, st[:, 1, :], inv, eps, ALU.mult, ALU.add).then_inc(done, 1)

            def diagonals(centre, mean_, root_, mroot_, done):
                if centre:
                    link(v.tensor_tensor(mroot_, mean_, root_, ALU.mult))
                for t in range(2):
                    for q in range(2 if centre else 1):
                        s = (root_, mroot_)[q]
                        ins = v.tensor_scalar(diag[:, t, q, :], ident, s[:, t:t + 1], None, ALU.mult)
                ins.then_inc(done, 1)

            def take(c, pos):
                r, j, l = c["role"], c["j"], c["l"]
                if "ends" in c:
                    norm(c["ends"], lambda: split_at(pos + 2))
                    if c["ends"] == END1:
                        norm(END1 + 1)
                    return
                src = banks_of[c["c"]] if c["kind"] not in ("O", "M") else None
                pair = src.rearrange("p (m s) -> p m s", m=2) if c["kind"] in ("F", "T") else None
                if r in DVE_TAKES:
                    dve.wait_ge(used.sem, used.at(c["c"]))
                if r == "hc":
                    if j == 0:
                        for e in (0, S + 1):
                            link(v.memset(pc[:, :, e:e + 1], 0.0))
                    dve.wait_ge(act_took.sem, act_took.at(by_role["gc", l][j]["c"]))
                    v.tensor_tensor(pc[:, :, 1:S + 1], gcv[:, :, :], pair, ALU.mult).then_inc(dve_took.sem, 1)
                    dve.wait_ge(dve_took.sem, dve_took.at(c["c"]))
                    if j == 1:
                        dve.wait_ge(yc_hi.sem, yc_hi.at((l, 0)))
                    for m in range(2):
                        w = [col("sc_w", 4 * i + 2 * j + m) for i in range(3)]
                        link(v.tensor_scalar(cv[:, m, :], pc[:, m, 0:S], w[0], None, ALU.mult))
                        for i in (1, 2):
                            link(v.scalar_tensor_tensor(cv[:, m, :], pc[:, m, i:i + S], w[i], cv[:, m, :],
                                                        ALU.mult, ALU.add))
                    v.tensor_tensor(cv[:, :, :], cv[:, :, :], gbv[:, :, :], ALU.mult).then_inc(yc_sum.sem, 1)
                    dve.wait_ge(yc_hi.sem, yc_hi.at((l, j)))
                    v.tensor_tensor(yl[:, 2, 2 * j:2 * j + 2, :], cv[:, :, :],
                                    yh[:, 2, 2 * j:2 * j + 2, :].bitcast(F32), ALU.subtract).then_inc(yc_lo.sem, 1)
                elif r == "branch":
                    half, b = c["half"], c["b"]
                    dst = macc if b == 0 else mtmp
                    if b == 0:
                        last = [g for g in by_role["gate", l] if g["half"] == half][-1]
                        dve.wait_ge(act_took.sem, act_took.at(last["c"]))
                        if half:
                            dve.wait_ge(merged_lo.sem, merged_lo.at((l, 0)))
                    v.scalar_tensor_tensor(dst[:, :, :].rearrange("p a b -> p (a b)"),
                                           gates[:, b, :, :].rearrange("p a b -> p (a b)"), 1.0, src,
                                           ALU.add, ALU.mult).then_inc(dve_took.sem, 1)
                    if b:
                        dve.wait_ge(dve_took.sem, dve_took.at(c["c"]))
                        ins = v.tensor_tensor(macc[:, :, :], macc[:, :, :], mtmp[:, :, :], ALU.add)
                        if b == 1:
                            link(ins)
                        else:
                            ins.then_inc(merged.sem, 1)
                            dve.wait_ge(merged_hi.sem, merged_hi.at((l, half)))
                            v.scalar_tensor_tensor(ml[:, 4 * half:4 * half + 4, :], macc[:, :, :], 0.5,
                                                   mh[:, 4 * half:4 * half + 4, :].bitcast(F32),
                                                   ALU.mult, ALU.subtract).then_inc(merged_lo.sem, 1)
                elif r == "fg":
                    f = j % 2
                    dve.wait_ge(act_took.sem, act_took.at(c["c"]))
                    for m in range(2):
                        k = 2 * j + m
                        w = [col("ffn_w", 22 * i + k) for i in range(3)]
                        a = fa[:, m * S:(m + 1) * S]
                        link(v.tensor_scalar(a, fgp[:, f, m, 0:S], w[0], col("ffn_b", k), ALU.mult, ALU.add))
                        link(v.scalar_tensor_tensor(a, fgp[:, f, m, 1:S + 1], w[1], a, ALU.mult, ALU.add))
                        ins = v.scalar_tensor_tensor(a, fgp[:, f, m, 2:S + 2], w[2], a, ALU.mult, ALU.add)
                        if m == 0:
                            link(ins)
                    ins.then_inc(f_conv.sem, 1)
                    split_at(pos + 2)
                    dve.wait_ge(f_tanh.sem, f_tanh.at(c["c"]))
                    link(v.scalar_tensor_tensor(fp[:, :], fth[:, :], 1.0, fa[:, :], ALU.add, ALU.mult))
                    v.tensor_tensor(fp[:, :], fp[:, :], fu[:, f, :], ALU.mult).then_inc(f_prod.sem, 1)
                    hidden_lo(c)
                    return
                elif r == "sg":
                    if c.get("norm") is not None:
                        keep_spread(c["norm"])
                    v.tensor_tensor(fa[:, :].rearrange("p (m s) -> p m s", m=2), pair,
                                    rstdb[:, :].unsqueeze(1).broadcast_to([P, 2, S]), ALU.mult)\
                        .then_inc(dve_took.sem, 1)
                    dve.wait_ge(dve_took.sem, dve_took.at(c["c"]))
                    split_at(pos + 2)
                    dve.wait_ge(f_tanh.sem, f_tanh.at(c["c"]))
                    link(v.scalar_tensor_tensor(fa[:, :], fth[:, :], 1.0, fa[:, :], ALU.add, ALU.mult))
                    return
                elif r == "su":
                    v.tensor_tensor(fu[:, 0, :].rearrange("p (m s) -> p m s", m=2), pair,
                                    rstdb[:, :].unsqueeze(1).broadcast_to([P, 2, S]), ALU.mult)\
                        .then_inc(dve_took.sem, 1)
                    dve.wait_ge(dve_took.sem, dve_took.at(c["c"]))
                    v.tensor_tensor(fp[:, :], fu[:, 0, :], fa[:, :], ALU.mult).then_inc(f_prod.sem, 1)
                    split_at(pos + 2)
                    hidden_lo(c)
                    return
                elif r in ("qm", "km", "qd", "kd", "cg"):
                    if c.get("norm") is not None:
                        keep_spread(c["norm"])
                    dst = sgm[:, :] if r == "cg" else rraw[:, (r[0] == "k") * 1, :]
                    v.tensor_tensor(dst.rearrange("p (m s) -> p m s", m=2), pair,
                                    rstdb[:, :].unsqueeze(1).broadcast_to([P, 2, S]), ALU.mult)\
                        .then_inc(dve_took.sem, 1)
                elif r == "ca":
                    v.tensor_tensor(yc[:, :, :], pair, rstdb[:, :].unsqueeze(1).broadcast_to([P, 2, S]),
                                    ALU.mult).then_inc(dve_took.sem, 1)
                    dve.wait_ge(dve_took.sem, dve_took.at(c["c"]))
                    dve.wait_ge(cg_tanh.sem, cg_tanh.at(l))
                    link(v.scalar_tensor_tensor(hpad[:, :, TAPS - 1:], sgm[:, :].rearrange("p (m s) -> p m s", m=2),
                                                1.0, yc[:, :, :], ALU.add, ALU.mult))
                split_at(pos + 2)

            def keep_spread(n):
                dve.wait_ge(spread.sem, spread.at(n))
                v.tensor_copy(rstdb[:, :], turnP[:, 0:S]).then_inc(spread_kept.sem, 1)
                dve.wait_ge(spread_kept.sem, spread_kept.at(n))

            def hidden_lo(c):
                j = c["j"]
                dve.wait_ge(f_hi.sem, f_hi.at(c["c"]))
                v.scalar_tensor_tensor(fl[:, j % 2, :, :].rearrange("p m s -> p (m s)"), fp[:, :], 0.5,
                                       fh[:, j % 2, :, :].rearrange("p m s -> p (m s)").bitcast(F32),
                                       ALU.mult, ALU.subtract).then_inc(f_lo.sem, 1)

            def step(name, what):
                if name == "lam":
                    dve.wait_ge(par_in, 16 * (what + 1))
                    a = P1["lam"][0]
                    p2 = logit[:, 0, 0, 0:128].rearrange("p (a b) -> p a b", a=2)
                    q = par[:, a:a + 256].rearrange("p (a b c) -> p a b c", a=2, b=2)
                    link(v.tensor_tensor(p2, q[:, :, 0, :], q[:, :, 1, :], ALU.mult))
                    v.tensor_reduce(lamv, p2, AX, ALU.add).then_inc(lam_sum.sem, 1)
                    dve.wait_ge(lam_exp.sem, lam_exp.at(what))
                    link(v.tensor_tensor(neglam, lame[:, 1:2], lame[:, 0:1], ALU.subtract))
                    link(v.tensor_tensor(neglam, neglam, col("lam_init", 0), ALU.subtract))
                    link(v.tensor_tensor(gsub, col("subln", 0), col("one_minus", 0), ALU.mult))
                elif name == "rot":
                    c = what
                    p2 = c["role"] in ("qm", "km", "qd", "kd")
                    k = c["role"] in ("dk", "km", "kd")
                    if p2:
                        dve.wait_ge(tabled, 1)
                        cos, sin = cs2[:, 0, :], cs2[:, 1, :]
                        dst = (k2 if k else q2)[:, (c["role"][1] == "d") * 1, :, :]
                    else:
                        cos, sin = con("cos1"), con("sin1")
                        dst = (kr if k else qr)[:, 2 * c["j"]:2 * c["j"] + 2, :]
                    rr = rraw[:, k * 1, :].rearrange("p (m s) -> p m s", m=2)
                    dve.wait_ge(rotated.sem, rotated.at(c["c"]))
                    link(v.tensor_tensor(rr, rr, cos.unsqueeze(1).broadcast_to([P, 2, S]), ALU.mult))
                    link(v.tensor_tensor(dst, outP[:, :].rearrange("p (m s) -> p m s", m=2),
                                         sin.unsqueeze(1).broadcast_to([P, 2, S]), ALU.mult))
                    v.tensor_tensor(dst, dst, rr, ALU.add).then_inc(roped.sem, 1)
                elif name == "scores":
                    n, kind, j = what["n"], what["kind"], what["j"]
                    e0 = 0 if kind == "diff" else 2 * (j % 2)
                    m = 4 if kind == "diff" else 2
                    nm = negmax[:, e0:e0 + m]
                    dve.wait_ge(scored.sem, scored.at(n))
                    if kind in ("win", "moba", "dil"):
                        lg = logit[:, j % 2, :, :]
                        if kind == "win":
                            w = wins.index(n)
                            dve.wait_ge(bias_in[w % 3], 16 * (w // 3 + 1))
                            bias_ = biasr[:, w % 3, :, :]
                        else:
                            bias_ = biasc[:, (kind == "dil") * 1, :, :]
                        v.scalar_tensor_tensor(lg, scoreP[:, j % 2, :].rearrange("p (t s) -> p t s", t=2), 0.125,
                                               bias_, ALU.mult, ALU.add).then_inc(biased.sem, 1)
                        dve.wait_ge(biased.sem, biased.at(n))
                        v.tensor_reduce(nm, lg, AX, ALU.max, negate=True).then_inc(maxed.sem, 1)
                    else:
                        src = scoreP[:, :, :].rearrange("p a (t s) -> p (a t) s", t=2) if kind == "diff" else \
                            scoreP[:, j % 2, :].rearrange("p (t s) -> p t s", t=2)
                        link(v.tensor_reduce(mrs[:, 0:m], src, AX, ALU.max, negate=True))
                        v.tensor_scalar(nm, mrs[:, 0:m], 0.125 if kind == "diff" else 0.0625, None, ALU.mult)\
                            .then_inc(maxed.sem, 1)
                    rs = rsum[:, e0:e0 + m]
                    i0 = inverse_column(kind, j)
                    inv = mrs[:, i0:i0 + m]
                    dve.wait_ge(expd.sem, expd.at(n))
                    v.reciprocal(inv, rs).then_inc(inverted.sem, 1)
                    dve.wait_ge(inverted.sem, inverted.at(n))
                    if kind == "diff":
                        link(v.tensor_scalar(mrs[:, 8:10], mrs[:, 6:8], neglam, None, ALU.mult))
                        for t in range(2):
                            last = v.tensor_scalar(ew[:, 2 + t, :], ew[:, 2 + t, :], mrs[:, 8 + t:9 + t], None,
                                                   ALU.mult)
                        link(last)
                        for t in range(2):
                            last = v.scalar_tensor_tensor(wd[:, t, :], ew[:, t, :], mrs[:, 4 + t:5 + t],
                                                          ew[:, 2 + t, :], ALU.mult, ALU.add)
                        last.then_inc(weighed.sem, 1)
                elif name == "mix":
                    n, kind, j = what["n"], what["kind"], what["j"]
                    if kind == "diff":
                        dve.wait_ge(o2.sem, o2.at(n))
                        v.tensor_scalar(oms, oss, 1.0 / P, LN_EPS, ALU.mult, ALU.add).then_inc(omean.sem, 1)
                        dve.wait_ge(oroot.sem, oroot.at(n))
                        w, at, s = P, 0, ort
                    else:
                        dve.wait_ge(mixed.sem, mixed.at(n))
                        w, at = (S, 0) if kind == "xa" else (64, 64 * (j % 2))
                        i = inverse_column(kind, j)
                        s = mrs[:, i:i + 2]
                    for t in range(2):
                        last = v.tensor_scalar(otok[:, t, at:at + w], outP[:, t * w:(t + 1) * w], s[:, t:t + 1], None,
                                               ALU.mult)
                    last.then_inc(oscaled.sem, 1)
                elif name == "back":
                    n, kind, j = what["n"], what["kind"], what["j"]
                    dve.wait_ge(back_hi.sem, back_hi.at(n))
                    if kind == "xa":
                        v.tensor_tensor(ol[:, 2 * j:2 * j + 2, :].rearrange("p a b -> p (a b)"), outP[:, :],
                                        oh[:, 2 * j:2 * j + 2, :].rearrange("p a b -> p (a b)").bitcast(F32),
                                        ALU.subtract).then_inc(back_lo.sem, 1)
                        return
                    hi, lo = head_place(kind, j, 0), head_place(kind, j, 1)
                    if kind == "diff":
                        v.scalar_tensor_tensor(lo, outP[:, 0:S], gsub, hi.bitcast(F32), ALU.mult, ALU.subtract)\
                            .then_inc(back_lo.sem, 1)
                    else:
                        v.tensor_tensor(lo, outP[:, 0:S], hi.bitcast(F32), ALU.subtract).then_inc(back_lo.sem, 1)
                elif name == "trig":
                    trig()
                elif name == "taps":
                    l, part = what, tap_part[0] % 4
                    tap_part[0] += 1
                    if part == 0:
                        for m in range(2):
                            link(v.tensor_scalar(hpad[:, m, TAPS - 1:], hpad[:, m, TAPS - 1:], 0.5, None, ALU.mult))
                            link(v.tensor_scalar(yc[:, m, :], hpad[:, m, 0:S], col("conv_w", m * TAPS, 1, P2),
                                                 col("conv_b", m, 1, P2), ALU.mult, ALU.add))
                    for i in range(max(1, 8 * part), min(TAPS, 8 * part + 8)):
                        for m in range(2):
                            ins = v.scalar_tensor_tensor(yc[:, m, :], hpad[:, m, i:i + S],
                                                         col("conv_w", m * TAPS + i, 1, P2), yc[:, m, :],
                                                         ALU.mult, ALU.add)
                            if i == TAPS - 1 and m == 1:
                                ins.then_inc(tapped.sem, 1)
                            elif m == 1:
                                link(ins)
                elif name == "cstats":
                    dve.wait_ge(c_stats.sem, c_stats.at(what))
                    st = outP[:, 0:4].rearrange("p (t q) -> p q t", q=2)
                    tiny_stats(st, 1.0 / S, True, cmean, cmsq, cvar, LN_EPS, c_var.sem)
                    dve.wait_ge(c_root.sem, c_root.at(what))
                    diagonals(True, cmean, croot, cmroot, c_diag.sem)
                elif name == "cspread":
                    dve.wait_ge(c_spread.sem, c_spread.at(what))
                    for q, op in ((0, ALU.mult), (1, ALU.subtract)):
                        a = outP[:, q * S:(q + 1) * S].unsqueeze(1).broadcast_to([P, 2, S])
                        ins = v.tensor_tensor(yc[:, :, :], yc[:, :, :], a, op)
                        if q == 0:
                            link(ins)
                    ins.then_inc(c_cen.sem, 1)
                    dve.wait_ge(c_tanh.sem, c_tanh.at(what))
                    v.scalar_tensor_tensor(yc[:, :, :], sgm[:, :].rearrange("p (m s) -> p m s", m=2), 1.0,
                                           yc2[:, :, :], ALU.add, ALU.mult).then_inc(c_act.sem, 1)
                    dve.wait_ge(c_hi.sem, c_hi.at(what))
                    v.scalar_tensor_tensor(zl[:, 6:8, :], yc[:, :, :], 0.5, zh[:, 6:8, :].bitcast(F32), ALU.mult,
                                           ALU.subtract).then_inc(c_lo.sem, 1)
                elif name == "poolw":
                    dve.wait_ge(poolw_hi.sem, poolw_hi.at(what["l"]))
                    for m in range(2):
                        ins = v.scalar_tensor_tensor(zl[:, m, :], outP[:, m * S:(m + 1) * S],
                                                     col("pool_s", m, 1, P2), zh[:, m, :].bitcast(F32),
                                                     ALU.mult, ALU.subtract)
                    ins.then_inc(poolw_lo.sem, 1)

            tap_part = [0]

            def trig():
                dve.wait_ge(pos_in, 16)
                dve.wait_ge(cc_in, 16)
                link(v.tensor_copy(posf[:, :], posi[:, :]))
                for m in range(2):
                    link(v.memset(hpad[:, m, 0:TAPS - 1], 0.0))
                link(v.tensor_scalar(posf[:, :], posf[:, :], c0[:, C0["inv2"][0]:C0["inv2"][0] + 1], None, ALU.mult))
                whole = 1.5 * 2.0 ** 23
                for q, off in ((0, 0.25), (1, 0.0)):
                    k, a = cs2[:, q, :], angle[:, q, :]
                    link(v.tensor_scalar(k, posf[:, :], 1.0 / (2 * math.pi), off, ALU.mult, ALU.add))
                    link(v.tensor_scalar(k, k, whole, None, ALU.add))
                    link(v.tensor_scalar(k, k, whole, None, ALU.subtract))
                    link(v.scalar_tensor_tensor(a, k, -TURN[0], posf[:, :], ALU.mult, ALU.add))
                    link(v.scalar_tensor_tensor(a, k, -TURN[1], a, ALU.mult, ALU.add))
                    link(v.scalar_tensor_tensor(a, k, -TURN[2], a, ALU.mult, ALU.add))
                    link(v.tensor_scalar(a, a, math.pi / 2 if q == 0 else 0.0, PI32, ALU.add, ALU.min))
                    ins = v.tensor_scalar(a, a, -PI32, None, ALU.max)
                    if q == 0:
                        link(ins)
                ins.then_inc(angled, 1)

            dve.wait_ge(c0_in, 16)
            norm(0)
            split_at(0)
            split_at(1)
            for c in chunks:
                pos = c["c"]
                if pos == 0:
                    split_at(2)
                else:
                    take(chunks[pos - 1], pos)
                if c["role"] in ("fu",) and c["j"] == 0:
                    for e in (0, S + 1):
                        link(v.memset(fgp[:, :, :, e:e + 1], 0.0))
                for name, what, *more in steps.get(pos, []):
                    step(name, what)
            take(chunks[-1], len(chunks))


def tiles(v):
    v = v.reshape(-1, v.shape[-1] // P, P)
    return v.transpose(2, 0, 1).reshape(P, -1)


def weight_chunks(i, products):
    w = np.empty((len(products), P, CH), np.float32)
    at = {"dq": 0, "dk": 512, "va": 1024, "qb": 1536, "kb": 2048, "vb": 2560, "gb": 3072, "gc": 3584, "hc": 4096}
    at2 = {"up": 0, "qm": 256, "km": 512, "vm": 768, "qd": 1024, "kd": 1280, "vd": 1536, "ca": 1792, "cg": 2048}
    for c in products:
        r, j, l = c["role"], c["j"], c["l"] % DEPTH
        if c["kind"] == "B":
            src = i["w_branch"][l, c["b"]][:, c["half"] * 512:c["half"] * 512 + 512]
        elif c["kind"] == "O":
            m = {"mo": "w_mix_out", "xo": "xa_o", "fo": "ffn_w_out", "wo": "w_out_2",
                 "sd": f"ffn{c.get('f', 0) + 1}_down_2"}[r]
            src = i[m][l][j * 256:j * 256 + 256]
        else:
            if r in at:
                m, n0 = "w_in", at[r] + j * 256
            elif r in at2:
                m, n0 = "w_in_2", at2[r]
            elif r == "gate":
                m, n0 = "w_in", 4608 + c["b"] * D + c["half"] * 512 + j * 256
            elif r == "xq":
                m, n0 = "xa_q", j * 256
            elif r in ("xk", "xv"):
                m, n0 = "xa_kv", j * 256 + D * (r == "xv")
            elif r in ("fu", "fg"):
                m, n0 = "ffn_w_in", j * 256 + FF * (r == "fg")
            else:
                m, n0 = f"ffn{c['f'] + 1}_{'gate' if r == 'sg' else 'up'}_2", j * 256
            src = i[m][l][:, n0:n0 + 256]
        k = src.shape[0] // P
        w[c["p"]] = src.reshape(k, P, -1).transpose(1, 0, 2).reshape(P, CH)
    return w


def layout(i):
    _, products, _, _, _ = plan()
    out = {}
    for name, key in (("xT", "x"), ("memT", "mem")):
        out[name] = np.ascontiguousarray(i[key][0].T.reshape(KT, P, S).transpose(1, 0, 2))
    out["memT"] = out["memT"].reshape(P, CH)

    p = np.arange(P)
    rot1, rot2 = np.zeros((P, P), np.float32), np.zeros((P, P), np.float32)
    for m in range(P):
        d = m % 64
        rot1[m + 32 if d < 32 else m - 32, m] = -1.0 if d < 32 else 1.0
        if d < 16:
            rot2[m + 8 if d < 8 else m - 8, m] = -1.0 if d < 8 else 1.0
    inv1 = np.float32(10000.0) ** (-(p % 32).astype(np.float32) * np.float32(2.0) / np.float32(64))
    ang = (np.arange(S, dtype=np.float32)[None, :] * inv1[:, None].astype(np.float32)).astype(np.float64)
    inv2 = np.float32(500000.0) ** (-((p % 8) * 2).astype(np.float32) / np.float32(16))
    inv2 = np.where(p % 64 < 16, inv2, 0).astype(np.float32)[:, None]
    out["consts"] = np.ascontiguousarray(np.concatenate(
        [np.eye(P, dtype=np.float32), rot1, rot2, np.cos(ang).astype(np.float32), np.sin(ang).astype(np.float32), inv2,
         tiles(i["emb_ln_g"]), tiles(i["emb_ln_b"]), tiles(i["final_norm_2"])], axis=1))

    t = np.arange(S)
    pools = []
    for w in (2, 4, 8, 16):
        inside = (t[:, None] <= t[None, :]) & (t[:, None] > t[None, :] - w)
        pools.append((inside / np.minimum(t + 1, w)[None, :] - (t[:, None] == t[None, :])).astype(np.float32))
    pools = np.stack(pools).reshape(4, 2, P, S).transpose(2, 1, 0, 3).reshape(P, -1)
    back = t[:, None] - t[None, :]
    often = (back >= 0) * ((back <= 128) * 1 + (back % 4 == 0) + (back % 16 == 0))
    causal = np.where(back >= 0, 0.0, -1e30)
    dilated = np.where(often > 0, np.log(np.maximum(often, 1)), -1e30)
    logit = np.stack([causal, dilated]).astype(np.float32).reshape(2, 2, P, S).transpose(2, 0, 1, 3).reshape(P, -1)
    out["consts2"] = np.ascontiguousarray(np.concatenate([pools, logit], axis=1))
    out["pos"] = np.ascontiguousarray(np.broadcast_to(i["positions_2"][0][None, :], (P, S)))

    par1, par2 = [], []
    for l in range(DEPTH):
        lam = np.concatenate([i[k][l] for k in ("lam_q1", "lam_k1", "lam_q2", "lam_k2")])
        init = 0.8 - 0.6 * math.exp(-0.3 * l)
        par1.append(np.concatenate(
            [tiles(i["ln_g"][l]), tiles(i["ln_b"][l]), tiles(i["ffn_conv_w"][l]), tiles(i["ffn_conv_b"][l]),
             tiles(i["sc_conv_w"][l]), tiles(i["subln_g"][l]), np.broadcast_to(lam[None, :], (P, 256)),
             np.full((P, 1), init, np.float32), np.full((P, 1), 1.0 - init, np.float32)], axis=1))
        conv = i["conv_w_2"][l].reshape(TAPS, 2, P).transpose(2, 1, 0).reshape(P, 2 * TAPS)
        pw = i["pool_w_2"][l].reshape(2, 2, 64, 64).transpose(1, 2, 0, 3).reshape(P, 128)
        par2.append(np.concatenate(
            [tiles(i["ffn1_norm_2"][l]), tiles(i["mix_norm_2"][l]), tiles(i["ffn2_norm_2"][l]),
             tiles(i["pool_scale_2"][l]), conv, tiles(i["conv_b_2"][l]), tiles(i["conv_ln_g_2"][l]),
             tiles(i["conv_ln_b_2"][l]), pw], axis=1))
    out["par1"] = np.ascontiguousarray(np.stack(par1))
    out["par2"] = np.ascontiguousarray(np.stack(par2))

    row, colm = t // 64, t % 64
    lo = np.clip(colm - 8, 0, 48)
    ok = (colm[None, :] >= lo[:, None]) & (colm[None, :] < lo[:, None] + 16)
    dr = row[None, :] - row[:, None] + 7
    dc = np.clip(colm[None, :] - colm[:, None] + 15, 0, 30)
    table = np.concatenate([i["rpb"].reshape(DEPTH * 8, -1), np.full((DEPTH * 8, 1), -1e30, np.float32)], axis=1)
    bias = table[:, np.where(ok, dr * 31 + dc, 15 * 31)]
    out["bias"] = np.ascontiguousarray(bias.reshape(DEPTH * 8, 2, P, S).transpose(0, 2, 1, 3))
    out["W"] = weight_chunks(i, products)
    return out



def kernel(**inputs):
    import concourse.bacc as bacc
    from concourse import mybir as mb
    from concourse.bass_utils import run_bass_kernel_spmd as run

    i = {k: np.asarray(v) for k, v in inputs.items()}
    arrays = layout(i)
    nc = bacc.Bacc("TRN2", target_bir_lowering=False, num_devices=1)
    aps = [nc.dram_tensor(f"in_{n}", a.shape, mb.dt.from_np(a.dtype), kind="ExternalInput").ap()
           for n, a in arrays.items()]
    o = nc.dram_tensor("out", (P, KT, S), mb.dt.float32, kind="ExternalOutput").ap()
    kernel_program(nc, *aps, o)
    r = run(nc, [{f"in_{n}": a for n, a in arrays.items()}], core_ids=[0])
    got = r.results[0]["out"]
    return np.ascontiguousarray(got.transpose(2, 1, 0)).reshape(1, S, D)
```

```python
import math
from contextlib import ExitStack

import numpy as np

import concourse.bass as bass
from concourse import mybir

P = 128
S = 256
D = 1024
KT = D // P
NB = KT // 2
DEPTH = 2
FF = 2816
FG = FF // 256
CH = 2048
RING = 3
LN_EPS, RMS_EPS = 1e-5, 1e-6
ALPHA = (2.0 * DEPTH) ** 0.25
TAPS = 31
TAP_PARTS = 5
TAP_RING = 3
DVE_TAPS = 10
LNS = 3
TURN = (6.28125, 2029 / 2.0 ** 20, 2 * math.pi - 6.28125 - 2029 / 2.0 ** 20)
PI32 = 3.1415925

F32 = mybir.dt.float32
F32R = mybir.dt.float32r
ALU = mybir.AluOpType
ACT = mybir.ActivationFunctionType
AX = mybir.AxisListType.X

P1 = {}
_at = 0
for _name, _n in (("ln_g", 24), ("ln_b", 24), ("ffn_w", 66), ("ffn_b", 22), ("sc_w", 12), ("subln", 1),
                  ("lam", 256), ("lam_init", 1), ("one_minus", 1)):
    P1[_name] = (_at, _at + _n)
    _at += _n
NP1 = _at
P2 = {}
_at = 0
for _name, _n in (("norm_g", 24), ("pool_s", 2), ("conv_w", 62), ("conv_b", 2), ("cln_g", 2), ("cln_b", 2),
                  ("pool_w", 128)):
    P2[_name] = (_at, _at + _n)
    _at += _n
NP2 = _at
C0 = {}
_at = 0
for _name, _n in (("ident", 128), ("rot1", 128), ("rot2", 128), ("cos1", 256), ("sin1", 256), ("inv2", 1),
                  ("emb_g", 8), ("emb_b", 8), ("fin_g", 8), ("first_g", 8)):
    C0[_name] = (_at, _at + _n)
    _at += _n
NC0 = _at
NC2 = 4 * 512 + 512 + 512


class Signal:

    def __init__(self, sem, steps):
        self.sem = sem
        self.value = {k: n + 1 for n, k in enumerate(steps)}

    def at(self, key):
        return self.value[key]


class Bank:

    def __init__(self):
        self.reader = None

    def claim(self, pe, signal, key):
        if self.reader is not None:
            pe.wait_ge(self.reader[0].sem, self.reader[0].at(self.reader[1]))
        self.reader = (signal, key)


def plan():
    chunks, heads, steps = [], [], {}

    def add(kind, role, l, j=0, **more):
        chunks.append(dict(kind=kind, role=role, l=l, j=j, c=len(chunks), **more))
        return len(chunks) - 1

    def at(pos, *step):
        steps.setdefault(pos, []).append(step)

    norm = 0
    for l in range(DEPTH):
        base = len(chunks)
        todo = {}

        def at(pos, *step):
            todo.setdefault(pos, []).append(step)

        def head(kind, j, pos, last):
            h = dict(kind=kind, l=l, j=j, n=len(heads))
            heads.append(h)
            at(pos, "scores", h)
            at(pos + 1, "turn", h)
            at(pos + 2, "mix", h)
            if last:
                at(pos + 3, "back", h)

        at(base + 1, "lam", l)
        for j in range(2):
            at(add("F", "dq", l, j) + 2, "rot", chunks[-1])
            at(add("F", "dk", l, j) + 2, "rot", chunks[-1])
            add("T", "va", l, j)
        for j in range(2):
            add("F", "qb", l, j)
            add("F", "kb", l, j)
            add("T", "vb", l, j)
        for j in range(2):
            add("F", "gc", l, j)
            c = add("F", "hc", l, j)
            add("F", "gb", l, j)
            at(c + 2, "short", (l, j))
            at(c + 4, "yc", (l, j))
        for half in range(2):
            for b in range(3):
                for j in range(2):
                    add("F", "gate", l, j, half=half, b=b)
            for b in range(3):
                add("B", "branch", l, 0, half=half, b=b)
        for j in range(3):
            add("O", "mo", l, j)
        add("M", "mem", l)
        chunks[-1]["after"] = [c["c"] for c in chunks if c["role"] == "branch"][-1]
        add("O", "mo", l, 3)
        chunks[base]["norm"] = norm
        norm += 1
        chunks[-1]["ends"] = norm
        where = {}
        for r, j in (("xk", 0), ("xv", 0), ("xk", 1), ("xv", 1), ("xq", 0), ("xk", 2), ("xq", 1), ("xk", 3),
                     ("xq", 2), ("xq", 3), ("xv", 2), ("xv", 3)):
            where[r, j] = add("T" if r == "xv" else "F", r, l, j)
        chunks[where["xq", 0]]["norm"] = norm
        for j in range(4):
            add("O", "xo", l, j)
        norm += 1
        chunks[-1]["ends"] = norm
        for j in range(FG + 1):
            if j < FG:
                c = add("F", "fu", l, j)
                if j == 0:
                    chunks[c]["norm"] = norm
                add("F", "fg", l, j)
            for k in {FG - 2: (), FG - 1: (FG - 3, FG - 2)}.get(j, (j - 1,)) if j else ():
                add("O", "fo", l, k)
        norm += 1
        chunks[-1]["ends"] = norm
        for j in range(4):
            head("diff", j, base + 4 + 2 * j, True)
        for j in range(8):
            head("win", j, base + 12 + j, j % 2 == 1)
        for j in range(4):
            head("xa", j, where["xq", j] + 2, True)
        order = dict(lam=-1, scores=0, rot=1, back=2, mix=3, turn=4, short=5, yc=6)
        for pos, some in todo.items():
            steps[pos] = sorted(some, key=lambda s: order[s[0]])
    norm += 1
    chunks[0]["part2"] = len(chunks)
    for l in range(DEPTH, 2 * DEPTH):
        for f in range(2):
            for j in range(FG + 1):
                if j < FG:
                    c = add("F", "sg", l, j, f=f)
                    if j == 0:
                        chunks[c]["norm"] = norm
                    add("F", "su", l, j, f=f)
                if j:
                    add("O", "sd", l, j - 1, f=f)
            norm += 1
            chunks[-1]["ends"] = norm
            if l == DEPTH and f == 0:
                for n in range(3):
                    steps.setdefault(chunks[0]["part2"] + 3 + 2 * n, []).append(("trig", l, n))
            if f:
                continue
            base = len(chunks)
            todo = {}

            def at(pos, *step):
                todo.setdefault(pos, []).append(step)

            def head(kind, j, pos):
                h = dict(kind=kind, l=l, j=j, n=len(heads))
                heads.append(h)
                at(pos, "scores", h)
                at(pos + 1, "turn", h)
                at(pos + 2, "mix", h)
                if j % 2:
                    at(pos + 3, "back", h)

            for r, k in (("cg", "F"), ("ca", "F"), ("qm", "F"), ("km", "F"), ("qd", "F"), ("kd", "F"),
                         ("up", "T"), ("vm", "T"), ("vd", "T")):
                c = add(k, r, l)
                if r in ("qm", "km", "qd", "kd"):
                    at(c + 2, "rot", chunks[c])
                if r == "up":
                    at(c + 2, "pool", chunks[c])
                    at(c + 2, "poolw", chunks[c])
            chunks[base]["norm"] = norm
            for j in (0, 1, 3, 2):
                add("O", "wo", l, j)
            norm += 1
            chunks[-1]["ends"] = norm
            for j in range(4):
                head("moba", j, base + 6 + j // 2)
            for j in range(4):
                head("dil", j, base + 8 + j // 2)
            for n in range(TAP_PARTS):
                at(base + 3 + n, "taps", l, n)
            at(base + 3 + TAP_PARTS, "csquare", l)
            at(base + 9, "cstats", l)
            at(base + 10, "cspread", l)
            order = dict(rot=1, cstats=2, cspread=2, pool=2, back=3, mix=4, turn=5, scores=6, poolw=7, taps=8,
                         csquare=9)
            for pos in sorted(todo):
                steps.setdefault(min(pos, base + 12), []).extend(sorted(todo[pos], key=lambda s: order[s[0]]))
    products = [c for c in chunks if c["kind"] != "M"]
    for n, c in enumerate(products):
        c["p"] = n
    return chunks, products, heads, steps, norm


def kernel_program(nc, xT, memT, consts, consts2, pos, par1, par2, bias, W, out):
    chunks, products, heads, steps, LAST = plan()
    END1 = 3 * DEPTH
    ctx = ExitStack()
    with ctx:
        def sb(name, shape, dt=F32, where=ctx):
            return where.enter_context(nc.sbuf_tensor(name, shape, dt))

        def sem(name):
            return ctx.enter_context(nc.semaphore(name))

        raw = sb("raw", [P, RING, CH])
        whi = sb("whi", [P, RING, CH], F32R)
        wlo = sb("wlo", [P, RING, CH], F32R)
        x = sb("x", [P, KT, S])
        xh = sb("xh", [P, KT, S], F32R)
        xl = sb("xl", [P, KT, S], F32R)
        c0 = sb("c0", [P, NC0])
        ones = sb("ones", [P, P])
        par = sb("par", [P, NP1])
        small = sb("small", [P, 64])
        mrs = sb("mrs", [P, 16])
        negmax = sb("negmax", [P, 16])
        rsum = sb("rsum", [P, 16])
        diag = sb("diag", [P, 2, 2, P])
        rstdb = sb("rstdb", [P, S])
        rraw = sb("rraw", [P, 2, 512])
        osq = sb("osq", [P, 2 * P])

        lnreg = ExitStack()
        sq = sb("sq", [P, 2, 512], where=lnreg)
        acc = sb("acc", [P, 512], where=lnreg)
        cen = sb("cen", [P, 2, 512], where=lnreg)
        lnreg.close()
        logit = sb("logit", [P, 2, 2, S])
        ew = sb("ew", [P, 4, S])
        wd = sb("wd", [P, 2, S])
        eT = sb("eT", [P, 2, 2, S])
        otok = sb("otok", [P, 2, S])

        part1 = ExitStack()
        yh = sb("yh", [P, 3, 4, S], F32R, part1)
        yl = sb("yl", [P, 3, 4, S], F32R, part1)
        att = ExitStack()
        biasr = sb("biasr", [P, 3, 2, S], where=att)
        qr = sb("qr", [P, 4, S], where=att)
        kr = sb("kr", [P, 4, S], where=att)
        qb = sb("qb", [P, 4, S], where=att)
        kb = sb("kb", [P, 4, S], where=att)
        va = sb("va", [P, 2, 512], where=att)
        vb = sb("vb", [P, 2, 512], where=att)
        att.close()
        mrg = ExitStack()
        mh = sb("mh", [P, KT, S], F32R, mrg)
        ml = sb("ml", [P, KT, S], F32R, mrg)
        macc = sb("macc", [P, 4, S], where=mrg)
        mrg.close()
        hold = ExitStack()
        _skip = sb("skip_att", [P, 30 * 256], where=hold)
        gates = sb("gates", [P, 3, 4, S], where=hold)
        gbv = sb("gbv", [P, 2, S], where=hold)
        gcv = sb("gcv", [P, 2, S], where=hold)
        pc = sb("pc", [P, 2, S + 2], where=hold)
        cv = sb("cv", [P, 2, S], where=hold)
        mtmp = sb("mtmp", [P, 4, S], where=hold)
        hold.close()
        part1.close()
        xat = ExitStack()
        memh = sb("memh", [P, KT, S], F32R, xat)
        meml = sb("meml", [P, KT, S], F32R, xat)
        _skip2 = sb("skip_y", [P, 8 * 256], where=xat)
        _skip3 = sb("skip_m", [P, 20 * 256], where=xat)
        kx = sb("kx", [P, KT, S], where=xat)
        vx = sb("vx", [P, 2, D], where=xat)
        qx = sb("qx", [P, 2, 2, S], where=xat)
        xat.close()
        oxs = ExitStack()
        _skip4 = sb("skip_mem", [P, 24 * 256], where=oxs)
        oh = sb("oh", [P, KT, S], F32R, oxs)
        ol = sb("ol", [P, KT, S], F32R, oxs)
        oxs.close()
        conv = ExitStack()
        taprod = sb("taprod", [P, TAP_RING, 2, S], where=conv)
        tapsum = sb("tapsum", [P, 2, S], where=conv)
        conv.close()
        ff = ExitStack()
        fu = sb("fu", [P, 2, 512], where=ff)
        fgp = sb("fgp", [P, 2, 2, S + 2], where=ff)
        fa = sb("fa", [P, 512], where=ff)
        fth = sb("fth", [P, 512], where=ff)
        fp = sb("fp", [P, 512], where=ff)
        fh = sb("fh", [P, 2, 2, S], F32R, ff)
        fl = sb("fl", [P, 2, 2, S], F32R, ff)
        cc = sb("cc", [P, NC2], where=ff)
        cs2 = sb("cs2", [P, 2, S], where=ff)
        angle = sb("angle", [P, 2, S], where=ff)
        posf = sb("posf", [P, S], where=ff)
        posi = sb("posi", [P, S], mybir.dt.int32, ff)
        q2 = sb("q2", [P, 2, 2, S], where=ff)
        k2 = sb("k2", [P, 2, 2, S], where=ff)
        v2 = sb("v2", [P, 2, 512], where=ff)
        up = sb("up", [P, 2, S], where=ff)
        pooled = sb("pooled", [P, 2, S], where=ff)
        hpad = sb("hpad", [P, 2, S + TAPS - 1], where=ff)
        sgm = sb("sgm", [P, 512], where=ff)
        yc = sb("yc", [P, 2, S], where=ff)
        yc2 = sb("yc2", [P, 2, S], where=ff)
        zh = sb("zh", [P, KT, S], F32R, ff)
        zl = sb("zl", [P, KT, S], F32R, ff)
        ff.close()

        accM = ctx.enter_context(nc.psum_tensor("accM", [P, 4, 512], F32))
        scoreP = ctx.enter_context(nc.psum_tensor("scoreP", [P, 2, 512], F32))
        turnP = ctx.enter_context(nc.psum_tensor("turnP", [P, 512], F32))
        outP = ctx.enter_context(nc.psum_tensor("outP", [P, 512], F32))

        def con(name):
            return c0[:, C0[name][0]:C0[name][1]]

        ident = con("ident")

        def col(name, i, n=1, table=P1):
            a = table[name][0] + i
            return par[:, a:a + n]

        accq = acc[:, :]
        poolm = cc[:, 0:2048].rearrange("p (t g s) -> p t g s", t=2, g=4)
        biasc = cc[:, 2048:3072].rearrange("p (b t s) -> p b t s", b=2, t=2)

        banks_of, claims, rot_bank, mix_bank, turn = {}, {}, {}, {}, 0
        for c in chunks:
            if c["role"] in ("fu", "fg", "sg", "su"):
                odd, second = c["j"] % 2, c["role"] in ("fg", "su")
                name = ("out" if second else "turn") if odd else f"score{int(second)}"
                claims[c["c"]] = [name]
                banks_of[c["c"]] = {"out": outP, "turn": turnP}[name][:, :] if odd else scoreP[:, int(second), :]
            elif c["kind"] in ("F", "T"):
                claims[c["c"]] = [f"acc{turn % 4}"]
                banks_of[c["c"]] = accM[:, turn % 4, :]
                turn += 1
            elif c["kind"] == "B":
                turn += turn % 2
                claims[c["c"]] = [f"acc{turn % 4}", f"acc{turn % 4 + 1}"]
                banks_of[c["c"]] = accM[:, turn % 4:turn % 4 + 2, :].rearrange("p b n -> p (b n)")
                turn += 2
            for name, what, *_ in steps.get(c["c"], []):
                if name == "rot":
                    rot_bank[what["c"]] = turn % 4
                    turn += 1
                if name == "mix" and c["kind"] in ("F", "T"):
                    mix_bank[what["n"]] = (f"acc{turn % 4}", accM[:, turn % 4, :])
                    turn += 1
                elif name == "mix":
                    mix_bank[what["n"]] = ("out", outP[:, :])

        def sig(name, keys):
            return Signal(sem(name), keys)

        stage = {}
        for c in chunks:
            for name, what, *more in steps.get(c["c"], []):
                key = what["n"] if isinstance(what, dict) and "n" in what else what["c"] if isinstance(what, dict) \
                    else what
                stage.setdefault(name, []).append(key)
        hs = {h["n"]: h for h in heads}
        cs = [c["c"] for c in chunks]
        landed = [sem(f"landed{i}") for i in range(RING)]
        split_hi = sig("split_hi", cs)
        by_pool = [c["c"] + 2 for c in chunks if "ends" in c and c["c"] + 2 < len(chunks)]
        split_lo = sig("split_lo", [c for c in cs if c not in by_pool])
        pool_lo = sig("pool_lo", by_pool)

        def await_split(engine, c):
            signal = pool_lo if c in by_pool else split_lo
            engine.wait_ge(signal.sem, signal.at(c))

        used = sig("used", [c["c"] for c in products if "ends" not in c])
        ACT_TAKES = ("dq", "dk", "va", "qb", "kb", "vb", "gb", "gc", "gate", "xk", "xv", "xq", "fu", "fg",
                     "vm", "vd", "up")
        DVE_TAKES = ("hc", "branch", "sg", "su", "qm", "km", "qd", "kd", "cg", "ca")
        act_took = sig("act_took", [c["c"] for c in products if c["role"] in ACT_TAKES])
        dve_took = sig("dve_took", [c["c"] for c in products if c["role"] in DVE_TAKES])

        def finished(c):
            return (obank, (c["ends"], NB - 1)) if "ends" in c else (used, c["c"])

        def await_chunk(engine, c):
            signal, key = finished(c)
            engine.wait_ge(signal.sem, signal.at(key))

        def await_x(engine, n, b):
            if n in ended:
                engine.wait_ge(resid.sem, resid.at((n, b)))
            elif n == 0:
                engine.wait_ge(x_in[b], 16)
            else:
                engine.wait_ge(xnew.sem, xnew.at((END1, b)))

        def gain(n, k):
            if n == END1 + 1:
                return c0[:, C0["first_g"][0] + k:C0["first_g"][0] + k + 1]
            return col("norm_g", ((n - END1 - 1) % 3) * KT + k, 1, P2)

        def taker(c):
            return (act_took if c["role"] in ACT_TAKES else dve_took), c["c"]

        norms = list(range(LAST + 1))
        ended = [n for n in norms if n not in (0, END1 + 1)]
        lns = [n for n in norms if n <= END1]
        fed = [n for n in norms if n not in (END1, LAST)]
        obank = sig("obank", [(n, b) for n in ended for b in range(NB)])
        resid = sig("resid", [(n, b) for n in ended for b in range(NB)])
        squared = sig("squared", [(n, b) for n in norms for b in range(NB)])
        summed = sig("summed", [(n, b) for n in norms for b in range(1, NB - 1)])
        ystats = sig("ystats", [n for n in norms if n <= END1])
        ysums = sig("ysums", [n for n in norms if n <= END1])
        stats = sig("stats", norms)
        varied = sig("varied", norms)
        rooted = sig("rooted", norms)
        diaged = sig("diaged", norms)
        spread = sig("spread", norms)
        mdiaged = sig("mdiaged", lns)
        mspread = sig("mspread", lns)
        scaled = sig("scaled", [(n, b) for n in lns for b in range(NB)])
        centred = sig("centred", [(n, b) for n in lns + [LAST] for b in range(NB)])
        xnew = sig("xnew", [(n, b) for n in lns + [LAST] for b in range(NB)])
        spread_kept = sig("spread_kept", [n for n in norms if END1 < n < LAST])
        xhi = sig("xhi", [(n, b) for n in fed for b in range(NB)])
        xlo0 = sig("xlo0", [(n, 0) for n in fed if n <= END1])
        xlo1 = sig("xlo1", [(n, b) for n in fed if n <= END1 for b in range(1, NB)])
        xlo2 = sig("xlo2", [(n, b) for n in fed if n > END1 for b in range(NB)])
        x_in = [sem(f"x_in{b}") for b in range(NB)]
        c0_in = sem("c0_in")
        cc_in = sem("cc_in")
        par_in = sem("par_in")
        pos_in = sem("pos_in")
        set_up = sem("set_up")
        bias_in = [sem(f"bias_in{i}") for i in range(3)]
        out_done = sem("out_done")

        inverse_order = []
        for c in chunks:
            for name, what, *_ in steps.get(c["c"], []):
                if (name == "scores" and what["kind"] == "diff") or (name == "mix" and what["kind"] != "diff"):
                    inverse_order.append(what["n"])
        scored = sig("scored", stage["scores"])
        biased = sig("biased", [n for n in stage["scores"] if hs[n]["kind"] in ("win", "moba", "dil")])
        maxed = sig("maxed", stage["scores"])
        expd = sig("expd", stage["scores"])
        weighed = sig("weighed", [n for n in stage["scores"] if hs[n]["kind"] == "diff"])
        inverted = sig("inverted", inverse_order)
        turned = sig("turned", stage["turn"])
        turn_kept = sig("turn_kept", stage["turn"])
        mixed = sig("mixed", stage["mix"])
        oscaled = sig("oscaled", stage["mix"])
        o2 = sig("o2", [n for n in stage["mix"] if hs[n]["kind"] == "diff"])
        omean = sig("omean", [n for n in stage["mix"] if hs[n]["kind"] == "diff"])
        oroot = sig("oroot", [n for n in stage["mix"] if hs[n]["kind"] == "diff"])
        backed = sig("backed", stage["back"])
        back_hi = sig("back_hi", stage["back"])
        back_lo = sig("back_lo", stage["back"])
        rotated = sig("rotated", stage["rot"])
        roped = sig("roped", stage["rot"])
        lam_sum = sig("lam_sum", range(DEPTH))
        lam_exp = sig("lam_exp", range(DEPTH))
        yc_sum = sig("yc_sum", [(l, j) for l in range(DEPTH) for j in range(2)])
        short_summed = sig("short_summed", [(l, j) for l in range(DEPTH) for j in range(2)])
        yc_hi = sig("yc_hi", [(l, j) for l in range(DEPTH) for j in range(2)])
        yc_lo = sig("yc_lo", [(l, j) for l in range(DEPTH) for j in range(2)])
        merged = sig("merged", [(l, h) for l in range(DEPTH) for h in range(2)])
        merged_hi = sig("merged_hi", [(l, h) for l in range(DEPTH) for h in range(2)])
        merged_lo = sig("merged_lo", [(l, h) for l in range(DEPTH) for h in range(2)])
        groups = [c["c"] for c in chunks if c["role"] in ("fg", "su")]
        gated = [c["c"] for c in chunks if c["role"] in ("fg", "sg")]
        f_conv = sig("f_conv", [c["c"] for c in chunks if c["role"] == "fg"])
        f_tanh = sig("f_tanh", [c for c in gated])
        f_prod = sig("f_prod", groups)
        f_hi = sig("f_hi", groups)
        f_lo = sig("f_lo", groups)
        L2 = list(range(DEPTH, 2 * DEPTH))
        cg_tanh = sig("cg_tanh", L2)
        hpadded = sig("hpadded", L2)
        far = [(l, i) for l in L2 for i in range(DVE_TAPS, TAPS)]
        tap_made = sig("tap_made", far)
        tap_added = sig("tap_added", [k for k in far if k[1] > DVE_TAPS])
        tapped = sig("tapped", L2)
        c_sq = sig("c_sq", L2)
        c_stats = sig("c_stats", L2)
        c_var = sig("c_var", L2)
        c_root = sig("c_root", L2)
        c_diag = sig("c_diag", L2)
        c_mdiag = sig("c_mdiag", L2)
        c_spread = sig("c_spread", L2)
        c_cen = sig("c_cen", L2)
        c_norm = sig("c_norm", L2)
        c_tanh = sig("c_tanh", L2)
        c_act = sig("c_act", L2)
        c_hi = sig("c_hi", L2)
        c_lo = sig("c_lo", L2)
        pool_done = sig("pool_done", L2)
        pool_kept = sig("pool_kept", L2)
        poolw_done = sig("poolw_done", L2)
        poolw_hi = sig("poolw_hi", L2)
        poolw_lo = sig("poolw_lo", L2)
        angled = sem("angled")
        tabled = sem("tabled")

        by_role = {}
        for c in chunks:
            by_role.setdefault((c["role"], c["l"]), []).append(c)
        part2_from = by_role["sg", DEPTH][0]["c"]
        wins = [n for n in stage["scores"] if hs[n]["kind"] == "win"]

        def slot(c):
            return c["p"] % RING

        def layer_of(c):
            return c["l"] % DEPTH

        def unpack(t, c):
            v = t[:, slot(c), :]
            if c["kind"] == "B":
                return v.rearrange("p (k n) -> p k n", k=4)
            if c["kind"] == "O":
                return v.rearrange("p (k n) -> p k n", k=2)
            return v.rearrange("p (k n) -> p k n", k=KT)

        def head_place(kind, j, part):
            if kind in ("diff", "win"):
                return (yh, yl)[part][:, 0, j, :] if kind == "diff" else (yh, yl)[part][:, 1, j // 2, :]
            return (zh, zl)[part][:, (2 if kind == "moba" else 4) + j // 2, :]

        def sum_column(kind, j):
            return 0 if kind == "diff" else 2 * (j % 4)

        def tap_range(part, dve):
            n, first = (DVE_TAPS, 0) if dve else (TAPS - DVE_TAPS, DVE_TAPS)
            size = -(-n // TAP_PARTS)
            return range(first + min(n, part * size), first + min(n, (part + 1) * size))

        def tap(i, m):
            return hpad[:, m, i:i + S], col("conv_w", m * TAPS + i, 1, P2)

        sums, var = small[:, 34:38], small[:, 2:4]
        root, mroot = small[:, 4:6], small[:, 6:8]
        msq = small[:, 8:10]
        csums, cvar = small[:, 38:42], small[:, 12:14]
        croot, cmroot = small[:, 14:16], small[:, 16:18]
        cmsq = small[:, 18:20]
        lamv, lame, neglam, gsub = small[:, 20:22], small[:, 22:24], small[:, 24:25], small[:, 25:26]
        oss, oms, ort = small[:, 26:28], small[:, 28:30], small[:, 30:32]
        mhalf = small[:, 32:34]

        block = ctx.enter_context(nc.Block())

        @block.sync
        def _(sp):
            for b in range(NB):
                sp.dma_start(x[:, 2 * b:2 * b + 2, :], xT[:, 2 * b:2 * b + 2, :]).then_inc(x_in[b], 16)
            sp.dma_start(c0[:, :], consts).then_inc(c0_in, 16)
            nbias = 0
            for c in chunks:
                r = c["c"] % RING
                if c["c"] >= RING:
                    await_split(sp, c["c"] - RING)
                src = memT if c["kind"] == "M" else W[c["p"]]
                sp.dma_start(raw[:, r, :], src).then_inc(landed[r], 16)
                for n in wins:
                    if c["c"] == by_role["dq", hs[n]["l"]][0]["c"] + 12 + hs[n]["j"]:
                        if nbias >= 3:
                            sp.wait_ge(biased.sem, biased.at(wins[nbias - 3]))
                        sp.dma_start(biasr[:, nbias % 3, :, :], bias[nbias]).then_inc(bias_in[nbias % 3], 16)
                        nbias += 1
            for b in range(NB):
                sp.wait_ge(xnew.sem, xnew.at((LAST, b)))
                sp.dma_start(out[:, 2 * b:2 * b + 2, :], x[:, 2 * b:2 * b + 2, :]).then_inc(out_done, 16)
            sp.wait_ge(out_done, 16 * NB)

        @block.gpsimd
        def _(pool):
            chain = sem("pool_chain")
            links = [0]

            def link(ins):
                links[0] += 1
                ins.then_inc(chain, 1)
                pool.wait_ge(chain, links[0])

            nc.gpsimd.memset(ones[:, :], 1.0).then_inc(set_up, 1)
            nc.gpsimd.memset(mhalf, -0.5).then_inc(set_up, 1)
            pool.wait_ge(set_up, 2)
            pool.dma_start(par[:, 0:NP1], par1[0]).then_inc(par_in, 16)

            def norm(n):
                pool.wait_ge(varied.sem, varied.at(n))
                nc.gpsimd.tensor_tensor(root, var, mhalf, ALU.pow).then_inc(rooted.sem, 1)
                if n in fed and n <= END1:
                    for b in range(1, NB):
                        pool.wait_ge(xhi.sem, xhi.at((n, b)))
                        k = slice(2 * b, 2 * b + 2)
                        nc.gpsimd.tensor_tensor(xl[:, k, :], x[:, k, :], xh[:, k, :].bitcast(F32), ALU.subtract)\
                            .then_inc(xlo1.sem, 1)
                if n == LNS:
                    pool.wait_ge(xnew.sem, xnew.at((n, NB - 1)))
                    pool.dma_start(par[:, 0:NP1], par1[1]).then_inc(par_in, 16)
                if n == END1 - 1:
                    last = by_role["xo", DEPTH - 1][-1]
                    await_chunk(pool, last)
                    pool.dma_start(cc[:, :], consts2).then_inc(cc_in, 16)
                    pool.dma_start(posi[:, :], pos).then_inc(pos_in, 16)
                if n == END1:
                    pool.wait_ge(xnew.sem, xnew.at((n, NB - 1)))
                    pool.dma_start(par[:, 0:NP2], par2[0]).then_inc(par_in, 16)
                if n == END1 + 3:
                    pool.wait_ge(xlo2.sem, xlo2.at((n, NB - 1)))
                    pool.dma_start(par[:, 0:NP2], par2[1]).then_inc(par_in, 16)

            norm(0)
            for c in chunks:
                for name, what, *more in steps.get(c["c"], []):
                    if name == "mix" and what["kind"] == "diff":
                        pool.wait_ge(omean.sem, omean.at(what["n"]))
                        nc.gpsimd.tensor_tensor(ort, oms, mhalf, ALU.pow).then_inc(oroot.sem, 1)
                    if name == "short":
                        pool.wait_ge(short_summed.sem, short_summed.at(what))
                        pool.wait_ge(act_took.sem, act_took.at(by_role["gb", what[0]][what[1]]["c"]))
                        nc.gpsimd.tensor_tensor(cv[:, :, :], cv[:, :, :], gbv[:, :, :], ALU.mult)\
                            .then_inc(yc_sum.sem, 1)
                    if name == "taps":
                        for i in tap_range(*more, False):
                            n = L2.index(what) * (TAPS - DVE_TAPS) + i - DVE_TAPS
                            pool.wait_ge(tap_made.sem, tap_made.at((what, i)))
                            if i > DVE_TAPS + 1:
                                pool.wait_ge(tap_added.sem, tap_added.at((what, i - 1)))
                            ins = None
                            if i > DVE_TAPS:
                                a = taprod[:, (n - 1) % TAP_RING, :, :] if i == DVE_TAPS + 1 else tapsum[:, :, :]
                                ins = nc.gpsimd.tensor_tensor(tapsum[:, :, :], a, taprod[:, n % TAP_RING, :, :], ALU.add)
                                ins.then_inc(tap_added.sem, 1)
                    if name == "cstats":
                        pool.wait_ge(c_var.sem, c_var.at(what))
                        nc.gpsimd.tensor_tensor(croot, cvar, mhalf, ALU.pow).then_inc(c_root.sem, 1)
                if c["c"] + 2 in by_pool:
                    n = c["c"] + 2
                    pool.wait_ge(split_hi.sem, split_hi.at(n))
                    nc.gpsimd.tensor_tensor(wlo[:, slot(chunks[n]), :], raw[:, n % RING, :],
                                            whi[:, slot(chunks[n]), :].bitcast(F32), ALU.subtract)\
                        .then_inc(pool_lo.sem, 1)
                if "ends" in c:
                    norm(c["ends"])
                    if c["ends"] == END1:
                        norm(END1 + 1)

        @block.scalar
        def _(act):
            BEFORE_SPLIT = ("scores", "rot", "back",
                            "mix", "csquare", "yc", "lam", "cstats", "cspread", "pool", "poolw")

            def split(c):
                n = c["c"]
                act.wait_ge(landed[n % RING], 16 * (n // RING + 1))
                if c["kind"] == "M":
                    act.wait_ge(used.sem, used.at(c["after"]))
                    nc.scalar.activation(memh[:, :, :].rearrange("p k s -> p (k s)"), raw[:, n % RING, :],
                                         ACT.Copy).then_inc(split_hi.sem, 1)
                    return
                if c["p"] >= RING:
                    await_chunk(act, products[c["p"] - RING])
                nc.scalar.activation(whi[:, slot(c), :], raw[:, n % RING, :], ACT.Copy).then_inc(split_hi.sem, 1)

            splits = [0]

            def split_at(pos):
                while splits[0] <= min(pos, len(chunks) - 1):
                    splits[0] += 1
                    split(chunks[splits[0] - 1])

            def upper(n, b):
                for k in (2 * b, 2 * b + 1):
                    ins = nc.scalar.activation(xh[:, k, :], x[:, k, :], ACT.Copy, scale=gain(n, k))
                ins.then_inc(xhi.sem, 1)

            def square(n, b):
                if b >= 2:
                    act.wait_ge(summed.sem, summed.at((n, b - 1)))
                nc.scalar.activation(sq[:, b % 2, :], x[:, 2 * b:2 * b + 2, :].rearrange("p k s -> p (k s)"),
                                     ACT.Square).then_inc(squared.sem, 1)

            def norm(n, between=None, late=None):
                if END1 + 1 < n < LAST:
                    act.wait_ge(par_in, 16 * (DEPTH + 1 + (n > END1 + 3)))
                    for b in range(NB):
                        await_x(act, n, b)
                        upper(n, b)
                        if b >= 1:
                            square(n, b - 1)
                    square(n, NB - 1)
                else:
                    for b in range(NB):
                        await_x(act, n, b)
                        square(n, b)
                if between and (n > END1 or n % LNS == 1):
                    between()
                if END1 < n < LAST:
                    return
                if n == 0:
                    act.wait_ge(c0_in, 16)
                elif n == LAST:
                    pass
                else:
                    act.wait_ge(par_in, 16 * (1 + (n > LNS)))
                if late:
                    late()
                for b in range(NB):
                    act.wait_ge(centred.sem, centred.at((n, b)))
                    for m in range(2):
                        k = 2 * b + m
                        src = cen[:, b % 2, m * S:(m + 1) * S]
                        if n == LAST:
                            g0 = C0["fin_g"][0] + k
                            ins = nc.scalar.activation(x[:, k, :], src, ACT.Copy, scale=c0[:, g0:g0 + 1])
                        else:
                            if n == 0:
                                g, bb = (c0[:, C0[q][0] + k:C0[q][0] + k + 1] for q in ("emb_g", "emb_b"))
                            else:
                                g, bb = (col(q, ((n - 1) % 3) * KT + k) for q in ("ln_g", "ln_b"))
                            ins = nc.scalar.activation(x[:, k, :], src, ACT.Identity, bias=bb, scale=g)
                    ins.then_inc(xnew.sem, 1)
                    if n in fed:
                        act.wait_ge(xnew.sem, xnew.at((n, b)))
                        nc.scalar.activation(xh[:, 2 * b:2 * b + 2, :], x[:, 2 * b:2 * b + 2, :], ACT.Copy)\
                            .then_inc(xhi.sem, 1)
                    elif n == END1:
                        act.wait_ge(xnew.sem, xnew.at((n, b)))
                        upper(n + 1, b)
                if between and n <= END1 and n % LNS != 1:
                    between()

            def copy_out(dst, c, bank_ap):
                act.wait_ge(used.sem, used.at(c["c"]))
                nc.scalar.activation(dst, bank_ap, ACT.Copy).then_inc(act_took.sem, 1)

            def take(c, pos):
                r, j, l = c["role"], c["j"], c["l"]
                if "ends" in c:
                    norm(c["ends"], lambda: split_at(pos + 2),
                         (lambda: split_at(pos + 3)) if c["role"] == "mo" else None)
                    if c["ends"] == END1:
                        norm(END1 + 1)
                    return True
                src = banks_of[c["c"]] if c["kind"] not in ("O", "M") else None
                pair = src.rearrange("p (m s) -> p m s", m=2) if c["kind"] in ("F", "T") else None
                if r in ("dq", "dk"):
                    if j == 1:
                        act.wait_ge(roped.sem, roped.at(by_role[r, l][0]["c"]))
                    copy_out(rraw[:, (r == "dk") * 1, :], c, src)
                elif r in ("va", "vb"):
                    copy_out((va if r == "va" else vb)[:, :, j * S:(j + 1) * S], c, pair)
                elif r in ("qb", "kb"):
                    copy_out((qb if r == "qb" else kb)[:, 2 * j:2 * j + 2, :], c, pair)
                elif r in ("gb", "gc"):
                    if j == 1 and r == "gb":
                        act.wait_ge(yc_sum.sem, yc_sum.at((l, 0)))
                    if j == 1 and r == "gc":
                        act.wait_ge(dve_took.sem, dve_took.at(by_role["hc", l][0]["c"]))
                    copy_out((gbv if r == "gb" else gcv)[:, :, :], c, pair)
                elif r == "gate":
                    if c["half"] == 1:
                        old = [b for b in by_role["branch", l] if b["half"] == 0 and b["b"] == c["b"]][0]
                        act.wait_ge(dve_took.sem, dve_took.at(old["c"]))
                    act.wait_ge(used.sem, used.at(c["c"]))
                    nc.scalar.activation(gates[:, c["b"], 2 * j:2 * j + 2, :], pair, ACT.Tanh, scale=0.5)\
                        .then_inc(act_took.sem, 1)
                elif r == "branch" and c["b"] == 2:
                    key = (layer_of(c), c["half"])
                    act.wait_ge(merged.sem, merged.at(key))
                    nc.scalar.activation(mh[:, 4 * c["half"]:4 * c["half"] + 4, :], macc[:, :, :], ACT.Copy,
                                         scale=0.5).then_inc(merged_hi.sem, 1)
                elif r == "xk":
                    copy_out(kx[:, 2 * j:2 * j + 2, :], c, pair)
                elif r == "xv":
                    copy_out(vx[:, :, j * S:(j + 1) * S], c, pair)
                elif r == "xq":
                    copy_out(qx[:, j % 2, :, :], c, pair)
                elif r == "fu":
                    copy_out(fu[:, j % 2, :], c, src)
                elif r == "fg":
                    copy_out(fgp[:, j % 2, :, 1:S + 1], c, pair)
                    split_at(pos + 2)
                    act.wait_ge(f_conv.sem, f_conv.at(c["c"]))
                    nc.scalar.activation(fth[:, :], fa[:, :], ACT.Tanh, scale=0.5).then_inc(f_tanh.sem, 1)
                    hidden(c)
                    return True
                elif r == "sg":
                    act.wait_ge(dve_took.sem, dve_took.at(c["c"]))
                    nc.scalar.activation(fth[:, :], fa[:, :], ACT.Tanh, scale=0.5).then_inc(f_tanh.sem, 1)
                elif r == "su":
                    split_at(pos + 2)
                    hidden(c)
                    return True
                elif r in ("vm", "vd", "up"):
                    act.wait_ge(used.sem, used.at(c["c"]))
                    act.wait_ge(rooted.sem, rooted.at(END1 + 2 + 3 * layer_of(c)))
                    for t in range(2):
                        dst = up[:, t, :] if r == "up" else v2[:, t, (r == "vd") * S:(r == "vd") * S + S]
                        ins = nc.scalar.activation(dst, pair[:, t, :], ACT.Copy, scale=root[:, t:t + 1])
                    ins.then_inc(act_took.sem, 1)
                elif r == "cg":
                    act.wait_ge(dve_took.sem, dve_took.at(c["c"]))
                    nc.scalar.activation(sgm[:, :], sgm[:, :], ACT.Tanh, scale=0.5).then_inc(cg_tanh.sem, 1)
                return False

            def hidden(c):
                j = c["j"]
                if (j >= 2):
                    down = by_role["fo" if c["role"] == "fg" else "sd", c["l"]]
                    down = [d for d in down if d.get("f") == c.get("f") and d["j"] == j - 2][0]
                    await_chunk(act, down)
                act.wait_ge(f_prod.sem, f_prod.at(c["c"]))
                nc.scalar.activation(fh[:, j % 2, :, :].rearrange("p m s -> p (m s)"), fp[:, :], ACT.Copy,
                                     scale=0.5).then_inc(f_hi.sem, 1)

            def step(name, what, part=0):
                if name == "yc":
                    j = what[1]
                    act.wait_ge(yc_sum.sem, yc_sum.at(what))
                    nc.scalar.activation(yh[:, 2, 2 * j:2 * j + 2, :], cv[:, :, :], ACT.Copy)\
                        .then_inc(yc_hi.sem, 1)
                elif name == "lam":
                    act.wait_ge(lam_sum.sem, lam_sum.at(what))
                    nc.scalar.activation(lame, lamv, ACT.Exp).then_inc(lam_exp.sem, 1)
                elif name == "scores":
                    n, kind = what["n"], what["kind"]
                    scale = 0.125 if kind == "diff" else 1.0 if kind != "xa" else 0.0625
                    e0 = 0 if kind == "diff" else 2 * (what["j"] % 2)
                    s0 = sum_column(kind, what["j"])
                    act.wait_ge(maxed.sem, maxed.at(n))
                    for i in range(4 if kind == "diff" else 2):
                        if kind == "diff":
                            src = scoreP[:, i // 2, (i % 2) * S:(i % 2 + 1) * S]
                        elif kind == "xa":
                            src = scoreP[:, what["j"] % 2, i * S:(i + 1) * S]
                        else:
                            src = logit[:, what["j"] % 2, i, :]
                        ins = nc.scalar.activation(ew[:, e0 + i, :], src, ACT.Exp, bias=negmax[:, e0 + i:e0 + i + 1],
                                                   scale=scale, accum_out=rsum[:, s0 + i:s0 + i + 1])
                    ins.then_inc(expd.sem, 1)
                elif name == "turn":
                    n = what["n"]
                    act.wait_ge(turned.sem, turned.at(n))
                    nc.scalar.activation(eT[:, what["j"] % 2, :, :].rearrange("p a b -> p (a b)"), turnP[:, :],
                                         ACT.Copy).then_inc(turn_kept.sem, 1)
                elif name == "mix" and what["kind"] == "diff":
                    n = what["n"]
                    act.wait_ge(mixed.sem, mixed.at(n))
                    for t in range(2):
                        ins = nc.scalar.activation(osq[:, t * P:(t + 1) * P], mix_bank[n][1][:, t * P:(t + 1) * P],
                                                   ACT.Square,
                                                   accum_out=oss[:, t:t + 1])
                    ins.then_inc(o2.sem, 1)
                elif name == "back":
                    n, kind, j = what["n"], what["kind"], what["j"]
                    act.wait_ge(backed.sem, backed.at(n))
                    if kind == "xa":
                        dst, kw = oh[:, 2 * j:2 * j + 2, :].rearrange("p a b -> p (a b)"), {}
                        src = outP[:, :]
                    else:
                        src = outP[:, 0:S]
                        dst = head_place(kind, j, 0)
                        kw = dict(scale=gsub) if kind == "diff" else {}
                    nc.scalar.activation(dst, src, ACT.Copy, **kw).then_inc(back_hi.sem, 1)
                elif name == "trig" and part == 2:
                    act.wait_ge(angled, 1)
                    nc.scalar.activation(cs2[:, :, :], angle[:, :, :], ACT.Sin).then_inc(tabled, 1)
                elif name == "taps":
                    act.wait_ge(hpadded.sem, hpadded.at(what))
                    for i in tap_range(part, False):
                        n = L2.index(what) * (TAPS - DVE_TAPS) + i - DVE_TAPS
                        if n >= TAP_RING:
                            act.wait_ge(tap_added.sem, tap_added.at(far[n - TAP_RING] if far[n - TAP_RING][1] > DVE_TAPS
                                                                         else far[n - TAP_RING + 1]))
                        for m in range(2):
                            src, w = tap(i, m)
                            ins = nc.scalar.activation(taprod[:, n % TAP_RING, m, :], src, ACT.Copy, scale=w)
                        ins.then_inc(tap_made.sem, 1)
                elif name == "csquare":
                    act.wait_ge(tapped.sem, tapped.at(what))
                    nc.scalar.activation(yc2[:, :, :], yc[:, :, :], ACT.Square).then_inc(c_sq.sem, 1)
                elif name == "cspread":
                    act.wait_ge(c_cen.sem, c_cen.at(what))
                    for m in range(2):
                        ins = nc.scalar.activation(yc2[:, m, :], yc[:, m, :], ACT.Identity,
                                                   bias=col("cln_b", m, 1, P2), scale=col("cln_g", m, 1, P2))
                    ins.then_inc(c_norm.sem, 1)
                    act.wait_ge(c_norm.sem, c_norm.at(what))
                    nc.scalar.activation(sgm[:, :], yc2[:, :, :].rearrange("p a b -> p (a b)"), ACT.Tanh,
                                         scale=0.5).then_inc(c_tanh.sem, 1)
                    act.wait_ge(c_act.sem, c_act.at(what))
                    nc.scalar.activation(zh[:, 6:8, :], yc[:, :, :], ACT.Copy, scale=0.5).then_inc(c_hi.sem, 1)
                elif name == "pool":
                    act.wait_ge(pool_done.sem, pool_done.at(what["l"]))
                    nc.scalar.activation(pooled[:, :, :].rearrange("p a b -> p (a b)"), outP[:, :], ACT.Copy)\
                        .then_inc(pool_kept.sem, 1)
                elif name == "poolw":
                    act.wait_ge(poolw_done.sem, poolw_done.at(what["l"]))
                    for m in range(2):
                        ins = nc.scalar.activation(zh[:, m, :], outP[:, m * S:(m + 1) * S], ACT.Copy,
                                                   scale=col("pool_s", m, 1, P2))
                    ins.then_inc(poolw_hi.sem, 1)

            norm(0, late=lambda: split_at(0))
            split_at(1)
            for c in chunks:
                pos = c["c"]
                split_done = pos > 0 and take(chunks[pos - 1], pos)
                for name, what, *more in sorted(steps.get(pos, []), key=lambda s: s[0] != "taps"):
                    if name not in BEFORE_SPLIT and not split_done:
                        split_at(pos + 2)
                        split_done = True
                    step(name, what, *more)
                if not split_done:
                    split_at(pos + 2)
            take(chunks[-1], len(chunks))

        @block.tensor
        def _(pe):
            accB = [Bank() for _ in range(4)]
            scoreB = [Bank() for _ in range(2)]
            turnB, outB = Bank(), Bank()
            bank = {"turn": turnB, "out": outB, "score0": scoreB[0], "score1": scoreB[1]}
            bank.update({f"acc{i}": b for i, b in enumerate(accB)})

            def mm(dst, a, b, start, stop=True):
                return nc.tensor.matmul(dst, a, b, start=start, stop=stop, skip_group_check=True)

            def norm_stats(n):
                outB.claim(pe, varied, n)
                if n <= END1:
                    turnB.claim(pe, ysums, n)
                    for k in range(KT):
                        if k % 2 == 0:
                            await_x(pe, n, k // 2)
                        ins = mm(turnP[:, 0:S], ones[:, :], x[:, k, :], k == 0, k == KT - 1)
                    ins.then_inc(ystats.sem, 1)
                for signal, key, src in ((summed, (n, NB - 2), accq), (squared, (n, NB - 1), sq[:, (NB - 1) % 2, :])):
                    pe.wait_ge(signal.sem, signal.at(key))
                    for h in range(2):
                        ins = mm(outP[:, 0:S], ones[:, :], src[:, h * S:(h + 1) * S], signal is summed and h == 0,
                                 signal is squared and h == 1)
                ins.then_inc(stats.sem, 1)

            def norm_spread(n):
                turnB.claim(pe, *((centred, (n, NB - 1)) if n in lns + [LAST] else (spread_kept, n)))
                pe.wait_ge(diaged.sem, diaged.at(n))
                for t in range(2):
                    ins = mm(turnP[:, t * P:(t + 1) * P], ones[:, :], diag[:, t, 0, :], True)
                ins.then_inc(spread.sem, 1)
                if n in lns:
                    outB.claim(pe, centred, (n, NB - 1))
                    pe.wait_ge(mdiaged.sem, mdiaged.at(n))
                    for t in range(2):
                        ins = mm(outP[:, t * P:(t + 1) * P], ones[:, :], diag[:, t, 1, :], True)
                    ins.then_inc(mspread.sem, 1)

            def product(c, hooks):
                r, kind = c["role"], c["kind"]
                if kind == "M":
                    return
                await_split(pe, c["c"])
                hi, lo = unpack(whi, c), unpack(wlo, c)
                a_hi, a_lo = (mh, ml) if r == "mo" else (oh, ol) if r == "xo" else (zh, zl) if r == "wo" \
                    else (memh, meml) if r in ("xk", "xv") else (xh, xl)
                if r in ("fo", "sd"):
                    a_hi, a_lo = fh[:, c["j"] % 2, :, :], fl[:, c["j"] % 2, :, :]
                if r in ("xk", "xv"):
                    mem = by_role["mem", c["l"]][0]["c"]
                    await_split(pe, mem)
                if kind in ("F", "T"):
                    for name in claims[c["c"]]:
                        bank[name].claim(pe, *taker(c))
                    dst = banks_of[c["c"]]
                    for k in range(KT):
                        for fn in hooks.get(k, []):
                            fn()
                        if c.get("norm") is not None and k % 2 == 0:
                            xlo = xlo2 if c["norm"] > END1 else xlo1 if k else xlo0
                            pe.wait_ge(xlo.sem, xlo.at((c["norm"], k // 2)))
                        for m in range(2):
                            first, last = k == 0 and m == 0, k == KT - 1
                            o = dst[:, m * S:(m + 1) * S]
                            if kind == "F":
                                w_hi, w_lo = hi[:, k, m * P:(m + 1) * P], lo[:, k, m * P:(m + 1) * P]
                                mm(o, w_hi, a_hi[:, k, :], first, False)
                                mm(o, w_hi, a_lo[:, k, :], False, False)
                                ins = mm(o, w_lo, a_hi[:, k, :], False, last)
                            else:
                                t_hi, t_lo = a_hi[:, k, m * P:(m + 1) * P], a_lo[:, k, m * P:(m + 1) * P]
                                mm(o, t_hi, hi[:, k, :], first, False)
                                mm(o, t_hi, lo[:, k, :], False, False)
                                ins = mm(o, t_lo, hi[:, k, :], False, last)
                    ins.then_inc(used.sem, 1)
                elif kind == "B":
                    b = c["b"]
                    a_hi, a_lo = yh[:, b, :, :], yl[:, b, :, :]
                    need = {0: (back_lo, [h["n"] for h in heads if h["kind"] == "diff" and h["l"] == c["l"]][-1]),
                            1: (back_lo, [h["n"] for h in heads if h["kind"] == "win" and h["l"] == c["l"]][-1]),
                            2: (yc_lo, (c["l"], 1))}[b]
                    if c["half"] == 0:
                        pe.wait_ge(need[0].sem, need[0].at(need[1]))
                    for name in claims[c["c"]]:
                        bank[name].claim(pe, *taker(c))
                    dst = banks_of[c["c"]]
                    for k in range(4):
                        for fn in hooks.get(2 * k, []) + hooks.get(2 * k + 1, []):
                            fn()
                        for m in range(4):
                            o = dst[:, m * S:(m + 1) * S]
                            w_hi, w_lo = hi[:, k, m * P:(m + 1) * P], lo[:, k, m * P:(m + 1) * P]
                            mm(o, w_hi, a_hi[:, k, :], k == 0 and m % 2 == 0, False)
                            mm(o, w_hi, a_lo[:, k, :], False, False)
                            ins = mm(o, w_lo, a_hi[:, k, :], False, k == 3)
                    ins.then_inc(used.sem, 1)
                else:
                    n = next(d["ends"] for d in chunks[c["c"]:] if "ends" in d)
                    group = [d for d in by_role[r, c["l"]] if d.get("f") == c.get("f")]
                    j = c["j"]
                    if r == "mo":
                        pe.wait_ge(merged_lo.sem, merged_lo.at((c["l"], j // 2)))
                    elif r == "xo":
                        h = [h["n"] for h in heads if h["kind"] == "xa" and h["l"] == c["l"] and h["j"] == j][0]
                        pe.wait_ge(back_lo.sem, back_lo.at(h))
                    elif r == "fo":
                        pe.wait_ge(f_lo.sem, f_lo.at(by_role["fg", c["l"]][j]["c"]))
                    elif r == "sd":
                        g = [d for d in by_role["su", c["l"]] if d["f"] == c["f"] and d["j"] == j][0]
                        pe.wait_ge(f_lo.sem, f_lo.at(g["c"]))
                    elif j == 0:
                        pe.wait_ge(poolw_lo.sem, poolw_lo.at(c["l"]))
                    elif j == 3:
                        pe.wait_ge(c_lo.sem, c_lo.at(c["l"]))
                    else:
                        kind_ = "moba" if j == 1 else "dil"
                        h = [h["n"] for h in heads if h["kind"] == kind_ and h["l"] == c["l"]][-1]
                        pe.wait_ge(back_lo.sem, back_lo.at(h))
                    first, last = c is group[0], c is group[-1]
                    for b in range(NB):
                        for fn in hooks.get(2 * b, []) + hooks.get(2 * b + 1, []):
                            fn()
                        if first:
                            accB[b].claim(pe, resid, (n, b))
                        for kk in range(2):
                            k = kk if r in ("fo", "sd") else 2 * j + kk
                            for m in (2 * b, 2 * b + 1):
                                o = accM[:, b, (m % 2) * S:(m % 2 + 1) * S]
                                w_hi, w_lo = hi[:, kk, m * P:(m + 1) * P], lo[:, kk, m * P:(m + 1) * P]
                                mm(o, w_hi, a_hi[:, k, :], first and kk == 0 and m % 2 == 0, False)
                                mm(o, w_hi, a_lo[:, k, :], False, False)
                                ins = mm(o, w_lo, a_hi[:, k, :], False, last and kk == 1)
                        if last and b < NB - 1:
                            ins.then_inc(obank.sem, 1)
                    if last:
                        ins.then_inc(obank.sem, 1)
                    else:
                        ins.then_inc(used.sem, 1)

            def step(name, what):
                if name == "rot":
                    c = what
                    p2 = c["role"] in ("qm", "km", "qd", "kd")
                    accB[rot_bank[c["c"]]].claim(pe, roped, c["c"])
                    pe.wait_ge((dve_took if p2 else act_took).sem, (dve_took if p2 else act_took).at(c["c"]))
                    i = 1 if c["role"] in ("dk", "km", "kd") else 0
                    mm(accM[:, rot_bank[c["c"]], :], con("rot2" if p2 else "rot1"), rraw[:, i, :], True).then_inc(rotated.sem, 1)
                elif name == "scores":
                    n, kind, j = what["n"], what["kind"], what["j"]
                    if kind == "diff":
                        for i in range(2):
                            scoreB[i].claim(pe, expd, n)
                        pe.wait_ge(roped.sem, roped.at(by_role["dk", what["l"]][j // 2]["c"]))
                        for i in range(4):
                            mp, t = i // 2, i % 2
                            rows = slice(64 * mp, 64 * mp + 64)
                            ins = mm(scoreP[:, mp, t * S:(t + 1) * S], qr[rows, j, t * P:(t + 1) * P],
                                     kr[rows, j, :], True)
                    elif kind == "xa":
                        scoreB[j % 2].claim(pe, expd, n)
                        for r in ("xq", "xk"):
                            c = [c for c in by_role[r, what["l"]] if c["j"] == j][0]
                            pe.wait_ge(act_took.sem, act_took.at(c["c"]))
                        for t in range(2):
                            for k in range(2):
                                ins = mm(scoreP[:, j % 2, t * S:(t + 1) * S], qx[:, j % 2, k, t * P:(t + 1) * P],
                                         kx[:, 2 * j + k, :], k == 0, k == 1)
                    else:
                        scoreB[j % 2].claim(pe, biased, n)
                        rows = slice(64 * (j % 2), 64 * (j % 2) + 64)
                        if kind == "win":
                            q, k = qb[rows, j // 2, :], kb[rows, j // 2, :]
                            pe.wait_ge(act_took.sem, act_took.at(by_role["kb", what["l"]][j // 4]["c"]))
                        else:
                            i = (kind == "dil") * 1
                            q, k = q2[rows, i, j // 2, :], k2[rows, i, j // 2, :]
                            pe.wait_ge(roped.sem, roped.at(by_role["kd" if i else "km", what["l"]][0]["c"]))
                        for t in range(2):
                            ins = mm(scoreP[:, j % 2, t * S:(t + 1) * S], q[:, t * P:(t + 1) * P], k, True)
                    ins.then_inc(scored.sem, 1)
                elif name == "turn":
                    n, kind, j = what["n"], what["kind"], what["j"]
                    turnB.claim(pe, turn_kept, n)
                    if kind == "diff":
                        pe.wait_ge(weighed.sem, weighed.at(n))
                        src = [wd[:, t, :] for t in range(2)]
                    else:
                        pe.wait_ge(expd.sem, expd.at(n))
                        src = [ew[:, 2 * (j % 2) + t, :] for t in range(2)]
                    for t in range(2):
                        for k in range(2):
                            ins = nc.tensor.transpose(turnP[:, k * S + t * P:k * S + (t + 1) * P],
                                                      src[t][:, k * P:(k + 1) * P], ident)
                    ins.then_inc(turned.sem, 1)
                elif name == "mix":
                    n, kind, j, l = what["n"], what["kind"], what["j"], what["l"]
                    bank[mix_bank[n][0]].claim(pe, oscaled, n)
                    pe.wait_ge(turn_kept.sem, turn_kept.at(n))
                    w = {"diff": P, "xa": S}.get(kind, 64)
                    v, c = {"diff": (va, by_role.get(("va", l))), "win": (vb, by_role.get(("vb", l))),
                            "moba": (v2, by_role.get(("vm", l))), "dil": (v2, by_role.get(("vd", l))),
                            "xa": (vx, by_role.get(("xv", l)))}[kind]
                    v0 = w * j + (S if kind == "dil" else 0)
                    c = c[{"diff": j // 2, "win": j // 4, "moba": 0, "dil": 0, "xa": 0}[kind]]
                    if kind == "xa":
                        c = [d for d in by_role["xv", l] if d["j"] == j][0]
                    pe.wait_ge(act_took.sem, act_took.at(c["c"]))
                    for t in range(2):
                        for k in range(2):
                            ins = mm(mix_bank[n][1][:, t * w:(t + 1) * w], eT[:, j % 2, k, t * P:(t + 1) * P],
                                     v[:, k, v0:v0 + w], k == 0, k == 1)
                    ins.then_inc(mixed.sem, 1)
                elif name == "back":
                    n, kind, j = what["n"], what["kind"], what["j"]
                    outB.claim(pe, back_lo, n)
                    pe.wait_ge(oscaled.sem, oscaled.at(n))
                    for d in range(2 if kind == "xa" else 1):
                        for t in range(2):
                            ins = nc.tensor.transpose(outP[:, d * S + t * P:d * S + (t + 1) * P],
                                                      otok[:, t, d * P:(d + 1) * P], ident)
                    ins.then_inc(backed.sem, 1)
                elif name == "pool":
                    outB.claim(pe, pool_kept, what["l"])
                    pe.wait_ge(act_took.sem, act_took.at(what["c"]))
                    pe.wait_ge(cc_in, 16)
                    for g in range(4):
                        for t in range(2):
                            ins = mm(outP[64 * (g % 2):64 * (g % 2) + 64, (g // 2) * S:(g // 2 + 1) * S],
                                     up[:, t, 64 * g:64 * g + 64], poolm[:, t, g, :], t == 0, t == 1)
                    ins.then_inc(pool_done.sem, 1)
                elif name == "poolw":
                    outB.claim(pe, poolw_lo, what["l"])
                    pe.wait_ge(pool_kept.sem, pool_kept.at(what["l"]))
                    pw = par[:, P2["pool_w"][0]:P2["pool_w"][1]].rearrange("p (t d) -> p t d", t=2)
                    for g in range(4):
                        rows = slice(64 * (g % 2), 64 * (g % 2) + 64)
                        ins = mm(outP[rows, (g // 2) * S:(g // 2 + 1) * S], pw[rows, g // 2, :],
                                 pooled[rows, g // 2, :], True)
                    ins.then_inc(poolw_done.sem, 1)
                elif name == "cstats":
                    outB.claim(pe, c_var, what)
                    pe.wait_ge(c_sq.sem, c_sq.at(what))
                    for q in range(2):
                        for m in range(2):
                            ins = mm(outP[:, (1 - q) * S:(2 - q) * S], ones[:, :], (yc, yc2)[q][:, m, :], m == 0,
                                     m == 1)
                    ins.then_inc(c_stats.sem, 1)
                elif name == "cspread":
                    outB.claim(pe, c_cen, what)
                    for q in range(2):
                        signal = (c_diag, c_mdiag)[q]
                        pe.wait_ge(signal.sem, signal.at(what))
                        for t in range(2):
                            ins = mm(outP[:, q * S + t * P:q * S + (t + 1) * P], ones[:, :], diag[:, t, q, :], True)
                    ins.then_inc(c_spread.sem, 1)

            PE_STEPS = ("rot", "back", "mix", "turn", "scores", "pool", "poolw", "cstats", "cspread")
            SPREAD = 8
            pe.wait_ge(set_up, 2)
            def needs(c, name, what):
                if c["role"] == "wo":
                    return (name, what["kind"] if name == "back" else "") in {
                        0: [("poolw", "")], 1: [("back", "moba")], 2: [("back", "dil")], 3: [("cspread", "")]}[c["j"]]
                return c["role"] == "xo" and name == "back" and what["j"] == c["j"]

            hooks = {}

            def hook(c, k, fn):
                hooks.setdefault(c, {}).setdefault(k, []).append(fn)

            norm_stats(0)
            pe.wait_ge(c0_in, 16)
            norm_spread(0)
            for c in chunks:
                pos = c["c"]
                mine = [s for s in steps.get(pos, []) if s[0] in PE_STEPS]
                needed = [i + 1 for i, (name, what, *_) in enumerate(mine) if c["kind"] == "M" or needs(c, name, what)]
                first = max(needed, default=0)
                for i, (name, what, *more) in enumerate(mine):
                    if i < first:
                        step(name, what)
                    else:
                        hook(pos, SPREAD * (i - first) // (len(mine) - first),
                             lambda name=name, what=what: step(name, what))
                product(c, hooks.get(pos, {}))
                n = c.get("ends")
                if n is None:
                    continue
                if c["role"] == "mo":
                    hook(pos + 1, 5, lambda n=n: norm_stats(n))
                    hook(pos + 2, 1, lambda n=n: norm_spread(n))
                elif n <= END1 or n == LAST:
                    norm_stats(n)
                    norm_spread(n)
                    if n == END1:
                        hook(pos + 1, 7, lambda n=n + 1: norm_stats(n))
                        hook(pos + 2, 6, lambda n=n + 1: norm_spread(n))
                else:
                    hook(pos + 1, 7, lambda n=n: norm_stats(n))
                    hook(pos + 2, 6, lambda n=n: norm_spread(n))

        @block.vector
        def _(dve):
            chain = sem("dve_chain")
            links = [0]

            def link(ins):
                links[0] += 1
                ins.then_inc(chain, 1)
                dve.wait_ge(chain, links[0])

            v = nc.vector

            BEFORE_SPLIT = ("scores", "rot", "back",
                            "mix", "turn", "csquare", "yc", "lam", "cstats", "cspread", "pool", "poolw")

            def split(c):
                n = c["c"]
                if n in by_pool:
                    return
                dve.wait_ge(split_hi.sem, split_hi.at(n))
                if c["kind"] == "M":
                    v.tensor_tensor(meml[:, :, :].rearrange("p k s -> p (k s)"), raw[:, n % RING, :],
                                    memh[:, :, :].rearrange("p k s -> p (k s)").bitcast(F32), ALU.subtract)\
                        .then_inc(split_lo.sem, 1)
                    return
                v.tensor_tensor(wlo[:, slot(c), :], raw[:, n % RING, :], whi[:, slot(c), :].bitcast(F32),
                                ALU.subtract).then_inc(split_lo.sem, 1)

            splits = [0]

            def split_at(pos):
                while splits[0] <= min(pos, len(chunks) - 1):
                    splits[0] += 1
                    split(chunks[splits[0] - 1])

            def bank_of_x(b):
                return x[:, 2 * b:2 * b + 2, :]

            def lo_part(n, b):
                dve.wait_ge(xhi.sem, xhi.at((n, b)))
                for k in (2 * b, 2 * b + 1):
                    ins = v.scalar_tensor_tensor(xl[:, k, :], x[:, k, :], gain(n, k), xh[:, k, :].bitcast(F32),
                                                 ALU.mult, ALU.subtract)
                ins.then_inc(xlo2.sem, 1)

            def norm(n, between=None, late=None):
                rms = n > END1
                split_here = END1 + 1 < n < LAST

                def add_squares(b):
                    dve.wait_ge(squared.sem, squared.at((n, b)))
                    if b == 0:
                        return
                    if b > 1:
                        dve.wait_ge(summed.sem, summed.at((n, b - 1)))
                    a = sq[:, 0, :] if b == 1 else accq
                    v.tensor_tensor(accq, a, sq[:, b % 2, :], ALU.add).then_inc(summed.sem, 1)

                for b in range(NB):
                    if n in ended:
                        dve.wait_ge(obank.sem, obank.at((n, b)))
                        p = accM[:, b, :].rearrange("p (m s) -> p m s", m=2)
                        if n <= END1:
                            ins = v.scalar_tensor_tensor(bank_of_x(b), bank_of_x(b), ALPHA, p, ALU.mult, ALU.add)
                        else:
                            f = 1.0 if (n - END1 - 1) % 3 == 2 else 0.5
                            ins = v.scalar_tensor_tensor(bank_of_x(b), p, f, bank_of_x(b), ALU.mult, ALU.add)
                        ins.then_inc(resid.sem, 1)
                    if split_here and b >= 1:
                        lo_part(n, b - 1)
                    if not split_here and b >= 1:
                        add_squares(b - 1)
                if split_here:
                    lo_part(n, NB - 1)
                    for b in range(NB - 1):
                        add_squares(b)
                if between and (n > END1 or n % LNS == 1):
                    between()
                if n == 0:
                    dve.wait_ge(c0_in, 16)
                if not rms:
                    dve.wait_ge(ystats.sem, ystats.at(n))
                    own_tokens(turnP[:, 0:S], sums[:, 0:2], 0).then_inc(ysums.sem, 1)
                dve.wait_ge(stats.sem, stats.at(n))
                tiny_stats(1.0 / D, not rms, sums, msq, var, LN_EPS if not rms else RMS_EPS, varied.sem)
                dve.wait_ge(rooted.sem, rooted.at(n))
                diagonals(1.0 / D, sums, root, mroot, diaged.sem, None if rms else mdiaged.sem)
                if rms and n != LAST:
                    return
                if late:
                    late()
                dve.wait_ge(spread.sem, spread.at(n))
                ra = turnP[:, 0:S].unsqueeze(1).broadcast_to([P, 2, S])
                ma = outP[:, 0:S].unsqueeze(1).broadcast_to([P, 2, S])

                def c3(b):
                    return cen[:, b % 2, :].rearrange("p (m s) -> p m s", m=2)

                def scale(b):
                    if b >= 2:
                        dve.wait_ge(xnew.sem, xnew.at((n, b - 2)))
                    v.tensor_tensor(c3(b), bank_of_x(b), ra, ALU.mult).then_inc((centred if rms else scaled).sem, 1)

                def shift(b):
                    if b == 0:
                        dve.wait_ge(mspread.sem, mspread.at(n))
                    dve.wait_ge(scaled.sem, scaled.at((n, b)))
                    v.tensor_tensor(c3(b), c3(b), ma, ALU.subtract).then_inc(centred.sem, 1)

                scale(0)
                scale(1)
                for b in range(NB):
                    if b >= 2:
                        scale(b)
                    if rms:
                        continue
                    shift(b)
                    if n == END1 and b >= 1:
                        lo_part(n + 1, b - 1)
                    if n in fed and b == 2:
                        dve.wait_ge(xhi.sem, xhi.at((n, 0)))
                        v.tensor_tensor(xl[:, 0:2, :], x[:, 0:2, :], xh[:, 0:2, :].bitcast(F32), ALU.subtract)\
                            .then_inc(xlo0.sem, 1)
                if n == END1:
                    lo_part(n + 1, NB - 1)
                if between and n <= END1 and n % LNS != 1:
                    between()

            def own_tokens(rows, dst, q):
                own = diag[:, :, q, :]
                link(v.tensor_tensor(own, rows.rearrange("p (g s) -> p g s", s=P),
                                     ident.unsqueeze(1).broadcast_to([P, 2, P]), ALU.mult))
                return v.tensor_reduce(dst, own, AX, ALU.add)

            def tiny_stats(inv, centre, sums, msq_, var_, eps, done):
                link(own_tokens(outP[:, 0:S], sums[:, 2:4], 1))
                if centre:
                    link(v.scalar_tensor_tensor(msq_, sums[:, 0:2], inv * inv, sums[:, 0:2], ALU.mult, ALU.mult))
                    link(v.scalar_tensor_tensor(var_, sums[:, 2:4], inv, msq_, ALU.mult, ALU.subtract))
                    v.tensor_scalar(var_, var_, 0.0, eps, ALU.max, ALU.add).then_inc(done, 1)
                else:
                    v.tensor_scalar(var_, sums[:, 2:4], inv, eps, ALU.mult, ALU.add).then_inc(done, 1)

            def diagonals(inv, sums, root_, mroot_, done, mdone):
                for t in range(2):
                    ins = v.tensor_scalar(diag[:, t, 0, :], ident, root_[:, t:t + 1], None, ALU.mult)
                ins.then_inc(done, 1)
                if mdone is None:
                    return
                link(v.scalar_tensor_tensor(mroot_, sums[:, 0:2], inv, root_, ALU.mult, ALU.mult))
                for t in range(2):
                    ins = v.tensor_scalar(diag[:, t, 1, :], ident, mroot_[:, t:t + 1], None, ALU.mult)
                ins.then_inc(mdone, 1)

            def take(c, pos):
                r, j, l = c["role"], c["j"], c["l"]
                if "ends" in c:
                    norm(c["ends"], lambda: split_at(pos + 2),
                         (lambda: split_at(pos + 3)) if c["role"] == "mo" else None)
                    if c["ends"] == END1:
                        norm(END1 + 1)
                    return True
                src = banks_of[c["c"]] if c["kind"] not in ("O", "M") else None
                pair = src.rearrange("p (m s) -> p m s", m=2) if c["kind"] in ("F", "T") else None
                if r in DVE_TAKES:
                    dve.wait_ge(used.sem, used.at(c["c"]))
                if r == "hc":
                    if j == 0:
                        for e in (0, S + 1):
                            link(v.memset(pc[:, :, e:e + 1], 0.0))
                    dve.wait_ge(act_took.sem, act_took.at(by_role["gc", l][j]["c"]))
                    v.tensor_tensor(pc[:, :, 1:S + 1], gcv[:, :, :], pair, ALU.mult).then_inc(dve_took.sem, 1)
                elif r == "branch":
                    half, b = c["half"], c["b"]
                    dst = macc if b == 0 else mtmp
                    if b == 0:
                        last = [g for g in by_role["gate", l] if g["half"] == half][-1]
                        dve.wait_ge(act_took.sem, act_took.at(last["c"]))
                        if half:
                            dve.wait_ge(merged_lo.sem, merged_lo.at((l, 0)))
                    v.scalar_tensor_tensor(dst[:, :, :].rearrange("p a b -> p (a b)"),
                                           gates[:, b, :, :].rearrange("p a b -> p (a b)"), 1.0, src,
                                           ALU.add, ALU.mult).then_inc(dve_took.sem, 1)
                    if b:
                        dve.wait_ge(dve_took.sem, dve_took.at(c["c"]))
                        ins = v.tensor_tensor(macc[:, :, :], macc[:, :, :], mtmp[:, :, :], ALU.add)
                        if b == 1:
                            link(ins)
                        else:
                            ins.then_inc(merged.sem, 1)
                            dve.wait_ge(merged_hi.sem, merged_hi.at((l, half)))
                            v.scalar_tensor_tensor(ml[:, 4 * half:4 * half + 4, :], macc[:, :, :], 0.5,
                                                   mh[:, 4 * half:4 * half + 4, :].bitcast(F32),
                                                   ALU.mult, ALU.subtract).then_inc(merged_lo.sem, 1)
                elif r == "fg":
                    f = j % 2
                    dve.wait_ge(act_took.sem, act_took.at(c["c"]))
                    for m in range(2):
                        k = 2 * j + m
                        w = [col("ffn_w", 22 * i + k) for i in range(3)]
                        a = fa[:, m * S:(m + 1) * S]
                        link(v.tensor_scalar(a, fgp[:, f, m, 0:S], w[0], col("ffn_b", k), ALU.mult, ALU.add))
                        link(v.scalar_tensor_tensor(a, fgp[:, f, m, 1:S + 1], w[1], a, ALU.mult, ALU.add))
                        ins = v.scalar_tensor_tensor(a, fgp[:, f, m, 2:S + 2], w[2], a, ALU.mult, ALU.add)
                        if m == 0:
                            link(ins)
                    ins.then_inc(f_conv.sem, 1)
                    split_at(pos + 2)
                    dve.wait_ge(f_tanh.sem, f_tanh.at(c["c"]))
                    link(v.scalar_tensor_tensor(fp[:, :], fth[:, :], 1.0, fa[:, :], ALU.add, ALU.mult))
                    v.tensor_tensor(fp[:, :], fp[:, :], fu[:, f, :], ALU.mult).then_inc(f_prod.sem, 1)
                    hidden_lo(c)
                    return True
                elif r == "sg":
                    if c.get("norm") is not None:
                        keep_spread(c["norm"])
                    v.tensor_tensor(fa[:, :].rearrange("p (m s) -> p m s", m=2), pair,
                                    rstdb[:, :].unsqueeze(1).broadcast_to([P, 2, S]), ALU.mult)\
                        .then_inc(dve_took.sem, 1)
                    dve.wait_ge(dve_took.sem, dve_took.at(c["c"]))
                    split_at(pos + 2)
                    dve.wait_ge(f_tanh.sem, f_tanh.at(c["c"]))
                    link(v.scalar_tensor_tensor(fa[:, :], fth[:, :], 1.0, fa[:, :], ALU.add, ALU.mult))
                    return True
                elif r == "su":
                    v.tensor_tensor(fu[:, 0, :].rearrange("p (m s) -> p m s", m=2), pair,
                                    rstdb[:, :].unsqueeze(1).broadcast_to([P, 2, S]), ALU.mult)\
                        .then_inc(dve_took.sem, 1)
                    dve.wait_ge(dve_took.sem, dve_took.at(c["c"]))
                    v.tensor_tensor(fp[:, :], fu[:, 0, :], fa[:, :], ALU.mult).then_inc(f_prod.sem, 1)
                    split_at(pos + 2)
                    hidden_lo(c)
                    return True
                elif r in ("qm", "km", "qd", "kd", "cg"):
                    if c.get("norm") is not None:
                        keep_spread(c["norm"])
                    dst = sgm[:, :] if r == "cg" else rraw[:, (r[0] == "k") * 1, :]
                    v.tensor_tensor(dst.rearrange("p (m s) -> p m s", m=2), pair,
                                    rstdb[:, :].unsqueeze(1).broadcast_to([P, 2, S]), ALU.mult)\
                        .then_inc(dve_took.sem, 1)
                elif r == "ca":
                    v.tensor_tensor(yc[:, :, :], pair, rstdb[:, :].unsqueeze(1).broadcast_to([P, 2, S]),
                                    ALU.mult).then_inc(dve_took.sem, 1)
                    dve.wait_ge(dve_took.sem, dve_took.at(c["c"]))
                    dve.wait_ge(cg_tanh.sem, cg_tanh.at(l))
                    hp = hpad[:, :, TAPS - 1:]
                    link(v.scalar_tensor_tensor(hp, sgm[:, :].rearrange("p (m s) -> p m s", m=2), 1.0, yc[:, :, :],
                                                ALU.add, ALU.mult))
                    v.tensor_scalar(hp, hp, 0.5, None, ALU.mult).then_inc(hpadded.sem, 1)
                    dve.wait_ge(hpadded.sem, hpadded.at(l))
                return False

            def keep_spread(n):
                dve.wait_ge(spread.sem, spread.at(n))
                v.tensor_copy(rstdb[:, :], turnP[:, 0:S]).then_inc(spread_kept.sem, 1)
                dve.wait_ge(spread_kept.sem, spread_kept.at(n))

            def hidden_lo(c):
                j = c["j"]
                dve.wait_ge(f_hi.sem, f_hi.at(c["c"]))
                v.scalar_tensor_tensor(fl[:, j % 2, :, :].rearrange("p m s -> p (m s)"), fp[:, :], 0.5,
                                       fh[:, j % 2, :, :].rearrange("p m s -> p (m s)").bitcast(F32),
                                       ALU.mult, ALU.subtract).then_inc(f_lo.sem, 1)

            def step(name, what, part=0):
                if name == "short":
                    j = what[1]
                    hc = by_role["hc", what[0]][j]["c"]
                    dve.wait_ge(dve_took.sem, dve_took.at(hc))
                    for i in range(3):
                        for m in range(2):
                            w = col("sc_w", 4 * i + 2 * j + m)
                            src = pc[:, m, i:i + S]
                            if i == 0:
                                ins = v.tensor_scalar(cv[:, m, :], src, w, None, ALU.mult)
                            else:
                                ins = v.scalar_tensor_tensor(cv[:, m, :], src, w, cv[:, m, :], ALU.mult, ALU.add)
                        if i < 2:
                            link(ins)
                    ins.then_inc(short_summed.sem, 1)
                elif name == "yc":
                    j = what[1]
                    dve.wait_ge(yc_hi.sem, yc_hi.at(what))
                    v.tensor_tensor(yl[:, 2, 2 * j:2 * j + 2, :], cv[:, :, :],
                                    yh[:, 2, 2 * j:2 * j + 2, :].bitcast(F32), ALU.subtract).then_inc(yc_lo.sem, 1)
                elif name == "lam":
                    dve.wait_ge(par_in, 16 * (what + 1))
                    a = P1["lam"][0]
                    p2 = logit[:, 0, 0, 0:128].rearrange("p (a b) -> p a b", a=2)
                    q = par[:, a:a + 256].rearrange("p (a b c) -> p a b c", a=2, b=2)
                    link(v.tensor_tensor(p2, q[:, :, 0, :], q[:, :, 1, :], ALU.mult))
                    v.tensor_reduce(lamv, p2, AX, ALU.add).then_inc(lam_sum.sem, 1)
                    dve.wait_ge(lam_exp.sem, lam_exp.at(what))
                    link(v.tensor_tensor(neglam, lame[:, 1:2], lame[:, 0:1], ALU.subtract))
                    link(v.tensor_tensor(neglam, neglam, col("lam_init", 0), ALU.subtract))
                    link(v.tensor_tensor(gsub, col("subln", 0), col("one_minus", 0), ALU.mult))
                elif name == "rot":
                    c = what
                    p2 = c["role"] in ("qm", "km", "qd", "kd")
                    k = c["role"] in ("dk", "km", "kd")
                    if p2:
                        dve.wait_ge(tabled, 1)
                        cos, sin = cs2[:, 0, :], cs2[:, 1, :]
                        dst = (k2 if k else q2)[:, (c["role"][1] == "d") * 1, :, :]
                    else:
                        cos, sin = con("cos1"), con("sin1")
                        dst = (kr if k else qr)[:, 2 * c["j"]:2 * c["j"] + 2, :]
                    rr = rraw[:, k * 1, :].rearrange("p (m s) -> p m s", m=2)
                    dve.wait_ge(rotated.sem, rotated.at(c["c"]))
                    link(v.tensor_tensor(rr, rr, cos.unsqueeze(1).broadcast_to([P, 2, S]), ALU.mult))
                    link(v.tensor_tensor(dst, accM[:, rot_bank[c["c"]], :].rearrange("p (m s) -> p m s", m=2),
                                         sin.unsqueeze(1).broadcast_to([P, 2, S]), ALU.mult))
                    v.tensor_tensor(dst, dst, rr, ALU.add).then_inc(roped.sem, 1)
                elif name == "scores":
                    n, kind, j = what["n"], what["kind"], what["j"]
                    e0 = 0 if kind == "diff" else 2 * (j % 2)
                    m = 4 if kind == "diff" else 2
                    nm = negmax[:, e0:e0 + m]
                    dve.wait_ge(scored.sem, scored.at(n))
                    if kind in ("win", "moba", "dil"):
                        lg = logit[:, j % 2, :, :]
                        if kind == "win":
                            w = wins.index(n)
                            dve.wait_ge(bias_in[w % 3], 16 * (w // 3 + 1))
                            bias_ = biasr[:, w % 3, :, :]
                        else:
                            bias_ = biasc[:, (kind == "dil") * 1, :, :]
                        v.scalar_tensor_tensor(lg, scoreP[:, j % 2, :].rearrange("p (t s) -> p t s", t=2), 0.125,
                                               bias_, ALU.mult, ALU.add).then_inc(biased.sem, 1)
                        dve.wait_ge(biased.sem, biased.at(n))
                        v.tensor_reduce(nm, lg, AX, ALU.max, negate=True).then_inc(maxed.sem, 1)
                    else:
                        src = scoreP[:, :, :].rearrange("p a (t s) -> p (a t) s", t=2) if kind == "diff" else \
                            scoreP[:, j % 2, :].rearrange("p (t s) -> p t s", t=2)
                        link(v.tensor_reduce(mrs[:, 0:m], src, AX, ALU.max, negate=True))
                        v.tensor_scalar(nm, mrs[:, 0:m], 0.125 if kind == "diff" else 0.0625, None, ALU.mult)\
                            .then_inc(maxed.sem, 1)
                    if kind == "diff":
                        dve.wait_ge(expd.sem, expd.at(n))
                        v.reciprocal(mrs[:, 4:8], rsum[:, 0:4]).then_inc(inverted.sem, 1)
                        dve.wait_ge(inverted.sem, inverted.at(n))
                        link(v.tensor_scalar(mrs[:, 8:10], mrs[:, 6:8], neglam, None, ALU.mult))
                        for t in range(2):
                            last = v.tensor_scalar(ew[:, 2 + t, :], ew[:, 2 + t, :], mrs[:, 8 + t:9 + t], None,
                                                   ALU.mult)
                        link(last)
                        for t in range(2):
                            last = v.scalar_tensor_tensor(wd[:, t, :], ew[:, t, :], mrs[:, 4 + t:5 + t],
                                                          ew[:, 2 + t, :], ALU.mult, ALU.add)
                        last.then_inc(weighed.sem, 1)
                elif name == "mix":
                    n, kind, j = what["n"], what["kind"], what["j"]
                    if kind == "diff":
                        dve.wait_ge(o2.sem, o2.at(n))
                        v.tensor_scalar(oms, oss, 1.0 / P, LN_EPS, ALU.mult, ALU.add).then_inc(omean.sem, 1)
                        dve.wait_ge(oroot.sem, oroot.at(n))
                        w, at, s = P, 0, ort
                    else:
                        dve.wait_ge(mixed.sem, mixed.at(n))
                        w, at = (S, 0) if kind == "xa" else (64, 64 * (j % 2))
                        i = 10 + 2 * (j % 2)
                        s = mrs[:, i:i + 2]
                        i0 = sum_column(kind, j)
                        v.reciprocal(s, rsum[:, i0:i0 + 2]).then_inc(inverted.sem, 1)
                        dve.wait_ge(inverted.sem, inverted.at(n))
                    for t in range(2):
                        last = v.tensor_scalar(otok[:, t, at:at + w], mix_bank[n][1][:, t * w:(t + 1) * w],
                                               s[:, t:t + 1], None, ALU.mult)
                    last.then_inc(oscaled.sem, 1)
                elif name == "back":
                    n, kind, j = what["n"], what["kind"], what["j"]
                    dve.wait_ge(back_hi.sem, back_hi.at(n))
                    if kind == "xa":
                        v.tensor_tensor(ol[:, 2 * j:2 * j + 2, :].rearrange("p a b -> p (a b)"), outP[:, :],
                                        oh[:, 2 * j:2 * j + 2, :].rearrange("p a b -> p (a b)").bitcast(F32),
                                        ALU.subtract).then_inc(back_lo.sem, 1)
                        return
                    hi, lo = head_place(kind, j, 0), head_place(kind, j, 1)
                    if kind == "diff":
                        v.scalar_tensor_tensor(lo, outP[:, 0:S], gsub, hi.bitcast(F32), ALU.mult, ALU.subtract)\
                            .then_inc(back_lo.sem, 1)
                    else:
                        v.tensor_tensor(lo, outP[:, 0:S], hi.bitcast(F32), ALU.subtract).then_inc(back_lo.sem, 1)
                elif name == "trig":
                    trig(part)
                elif name == "taps":
                    for i in tap_range(part, True):
                        for m in range(2):
                            src, w = tap(i, m)
                            if i == 0:
                                ins = v.tensor_scalar(yc[:, m, :], src, w, col("conv_b", m, 1, P2), ALU.mult, ALU.add)
                            else:
                                ins = v.scalar_tensor_tensor(yc[:, m, :], src, w, yc[:, m, :], ALU.mult, ALU.add)
                        link(ins)
                elif name == "csquare":
                    dve.wait_ge(tap_added.sem, tap_added.at((what, TAPS - 1)))
                    v.tensor_tensor(yc[:, :, :], yc[:, :, :], tapsum[:, :, :], ALU.add).then_inc(tapped.sem, 1)
                elif name == "cstats":
                    dve.wait_ge(c_stats.sem, c_stats.at(what))
                    own_tokens(outP[:, S:], csums[:, 0:2], 0)
                    tiny_stats(1.0 / S, True, csums, cmsq, cvar, LN_EPS, c_var.sem)
                    dve.wait_ge(c_root.sem, c_root.at(what))
                    diagonals(1.0 / S, csums, croot, cmroot, c_diag.sem, c_mdiag.sem)
                elif name == "cspread":
                    dve.wait_ge(c_spread.sem, c_spread.at(what))
                    for q, op in ((0, ALU.mult), (1, ALU.subtract)):
                        a = outP[:, q * S:(q + 1) * S].unsqueeze(1).broadcast_to([P, 2, S])
                        ins = v.tensor_tensor(yc[:, :, :], yc[:, :, :], a, op)
                        if q == 0:
                            link(ins)
                    ins.then_inc(c_cen.sem, 1)
                    dve.wait_ge(c_tanh.sem, c_tanh.at(what))
                    v.scalar_tensor_tensor(yc[:, :, :], sgm[:, :].rearrange("p (m s) -> p m s", m=2), 1.0,
                                           yc2[:, :, :], ALU.add, ALU.mult).then_inc(c_act.sem, 1)
                    dve.wait_ge(c_hi.sem, c_hi.at(what))
                    v.scalar_tensor_tensor(zl[:, 6:8, :], yc[:, :, :], 0.5, zh[:, 6:8, :].bitcast(F32), ALU.mult,
                                           ALU.subtract).then_inc(c_lo.sem, 1)
                elif name == "poolw":
                    dve.wait_ge(poolw_hi.sem, poolw_hi.at(what["l"]))
                    for m in range(2):
                        ins = v.scalar_tensor_tensor(zl[:, m, :], outP[:, m * S:(m + 1) * S],
                                                     col("pool_s", m, 1, P2), zh[:, m, :].bitcast(F32),
                                                     ALU.mult, ALU.subtract)
                    ins.then_inc(poolw_lo.sem, 1)

            def trig(part):
                if part == 0:
                    dve.wait_ge(pos_in, 16)
                    dve.wait_ge(cc_in, 16)
                    link(v.tensor_copy(posf[:, :], posi[:, :]))
                    for m in range(2):
                        link(v.memset(hpad[:, m, 0:TAPS - 1], 0.0))
                    link(v.tensor_scalar(posf[:, :], posf[:, :], con("inv2"), None, ALU.mult))
                    return
                whole = 1.5 * 2.0 ** 23
                q, off = ((0, 0.25), (1, 0.0))[part - 1]
                k, a = cs2[:, q, :], angle[:, q, :]
                link(v.tensor_scalar(k, posf[:, :], 1.0 / (2 * math.pi), off, ALU.mult, ALU.add))
                link(v.tensor_scalar(k, k, whole, None, ALU.add))
                link(v.tensor_scalar(k, k, whole, None, ALU.subtract))
                link(v.scalar_tensor_tensor(a, k, -TURN[0], posf[:, :], ALU.mult, ALU.add))
                link(v.scalar_tensor_tensor(a, k, -TURN[1], a, ALU.mult, ALU.add))
                link(v.scalar_tensor_tensor(a, k, -TURN[2], a, ALU.mult, ALU.add))
                link(v.tensor_scalar(a, a, math.pi / 2 if q == 0 else 0.0, PI32, ALU.add, ALU.min))
                ins = v.tensor_scalar(a, a, -PI32, None, ALU.max)
                if q == 0:
                    link(ins)
                    return
                ins.then_inc(angled, 1)

            norm(0, late=lambda: split_at(0))
            split_at(1)
            for c in chunks:
                pos = c["c"]
                split_done = pos > 0 and take(chunks[pos - 1], pos)
                if c["role"] in ("fu",) and c["j"] == 0:
                    for e in (0, S + 1):
                        link(v.memset(fgp[:, :, :, e:e + 1], 0.0))
                for name, what, *more in steps.get(pos, []):
                    if name not in BEFORE_SPLIT and not split_done:
                        split_at(pos + 2)
                        split_done = True
                    step(name, what, *more)
                if not split_done:
                    split_at(pos + 2)
            take(chunks[-1], len(chunks))


def tiles(v):
    v = v.reshape(-1, v.shape[-1] // P, P)
    return v.transpose(2, 0, 1).reshape(P, -1)


def weight_chunks(i, products):
    w = np.empty((len(products), P, CH), np.float32)
    at = {"dq": 0, "dk": 512, "va": 1024, "qb": 1536, "kb": 2048, "vb": 2560, "gb": 3072, "gc": 3584, "hc": 4096}
    at2 = {"up": 0, "qm": 256, "km": 512, "vm": 768, "qd": 1024, "kd": 1280, "vd": 1536, "ca": 1792, "cg": 2048}
    for c in products:
        r, j, l = c["role"], c["j"], c["l"] % DEPTH
        if c["kind"] == "B":
            src = i["w_branch"][l, c["b"]][:, c["half"] * 512:c["half"] * 512 + 512]
        elif c["kind"] == "O":
            m = {"mo": "w_mix_out", "xo": "xa_o", "fo": "ffn_w_out", "wo": "w_out_2",
                 "sd": f"ffn{c.get('f', 0) + 1}_down_2"}[r]
            src = i[m][l][j * 256:j * 256 + 256]
        else:
            if r in at:
                m, n0 = "w_in", at[r] + j * 256
            elif r in at2:
                m, n0 = "w_in_2", at2[r]
            elif r == "gate":
                m, n0 = "w_in", 4608 + c["b"] * D + c["half"] * 512 + j * 256
            elif r == "xq":
                m, n0 = "xa_q", j * 256
            elif r in ("xk", "xv"):
                m, n0 = "xa_kv", j * 256 + D * (r == "xv")
            elif r in ("fu", "fg"):
                m, n0 = "ffn_w_in", j * 256 + FF * (r == "fg")
            else:
                m, n0 = f"ffn{c['f'] + 1}_{'gate' if r == 'sg' else 'up'}_2", j * 256
            src = i[m][l][:, n0:n0 + 256]
        k = src.shape[0] // P
        w[c["p"]] = src.reshape(k, P, -1).transpose(1, 0, 2).reshape(P, CH)
    return w


def layout(i):
    _, products, _, _, _ = plan()
    out = {}
    for name, key in (("xT", "x"), ("memT", "mem")):
        out[name] = np.ascontiguousarray(i[key][0].T.reshape(KT, P, S).transpose(1, 0, 2))
    out["memT"] = out["memT"].reshape(P, CH)

    p = np.arange(P)
    rot1, rot2 = np.zeros((P, P), np.float32), np.zeros((P, P), np.float32)
    for m in range(P):
        d = m % 64
        rot1[m + 32 if d < 32 else m - 32, m] = -1.0 if d < 32 else 1.0
        if d < 16:
            rot2[m + 8 if d < 8 else m - 8, m] = -1.0 if d < 8 else 1.0
    inv1 = np.float32(10000.0) ** (-(p % 32).astype(np.float32) * np.float32(2.0) / np.float32(64))
    ang = (np.arange(S, dtype=np.float32)[None, :] * inv1[:, None].astype(np.float32)).astype(np.float64)
    inv2 = np.float32(500000.0) ** (-((p % 8) * 2).astype(np.float32) / np.float32(16))
    inv2 = np.where(p % 64 < 16, inv2, 0).astype(np.float32)[:, None]
    out["consts"] = np.ascontiguousarray(np.concatenate(
        [np.eye(P, dtype=np.float32), rot1, rot2, np.cos(ang).astype(np.float32), np.sin(ang).astype(np.float32), inv2,
         tiles(i["emb_ln_g"]), tiles(i["emb_ln_b"]), tiles(i["final_norm_2"]),
         tiles(i["ffn1_norm_2"][0])], axis=1))

    t = np.arange(S)
    pools = []
    for w in (2, 4, 8, 16):
        inside = (t[:, None] <= t[None, :]) & (t[:, None] > t[None, :] - w)
        pools.append((inside / np.minimum(t + 1, w)[None, :] - (t[:, None] == t[None, :])).astype(np.float32))
    pools = np.stack(pools).reshape(4, 2, P, S).transpose(2, 1, 0, 3).reshape(P, -1)
    back = t[:, None] - t[None, :]
    often = (back >= 0) * ((back <= 128) * 1 + (back % 4 == 0) + (back % 16 == 0))
    causal = np.where(back >= 0, 0.0, -1e30)
    dilated = np.where(often > 0, np.log(np.maximum(often, 1)), -1e30)
    logit = np.stack([causal, dilated]).astype(np.float32).reshape(2, 2, P, S).transpose(2, 0, 1, 3).reshape(P, -1)
    out["consts2"] = np.ascontiguousarray(np.concatenate([pools, logit], axis=1))
    out["pos"] = np.ascontiguousarray(np.broadcast_to(i["positions_2"][0][None, :], (P, S)))

    par1, par2 = [], []
    for l in range(DEPTH):
        lam = np.concatenate([i[k][l] for k in ("lam_q1", "lam_k1", "lam_q2", "lam_k2")])
        init = 0.8 - 0.6 * math.exp(-0.3 * l)
        par1.append(np.concatenate(
            [tiles(i["ln_g"][l]), tiles(i["ln_b"][l]), tiles(i["ffn_conv_w"][l]), tiles(i["ffn_conv_b"][l]),
             tiles(i["sc_conv_w"][l]), tiles(i["subln_g"][l]), np.broadcast_to(lam[None, :], (P, 256)),
             np.full((P, 1), init, np.float32), np.full((P, 1), 1.0 - init, np.float32)], axis=1))
        conv = i["conv_w_2"][l].reshape(TAPS, 2, P).transpose(2, 1, 0).reshape(P, 2 * TAPS)
        pw = i["pool_w_2"][l].reshape(2, 2, 64, 64).transpose(1, 2, 0, 3).reshape(P, 128)
        par2.append(np.concatenate(
            [tiles(i["ffn1_norm_2"][l]), tiles(i["mix_norm_2"][l]), tiles(i["ffn2_norm_2"][l]),
             tiles(i["pool_scale_2"][l]), conv, tiles(i["conv_b_2"][l]), tiles(i["conv_ln_g_2"][l]),
             tiles(i["conv_ln_b_2"][l]), pw], axis=1))
    out["par1"] = np.ascontiguousarray(np.stack(par1))
    out["par2"] = np.ascontiguousarray(np.stack(par2))

    row, colm = t // 64, t % 64
    lo = np.clip(colm - 8, 0, 48)
    ok = (colm[None, :] >= lo[:, None]) & (colm[None, :] < lo[:, None] + 16)
    dr = row[None, :] - row[:, None] + 7
    dc = np.clip(colm[None, :] - colm[:, None] + 15, 0, 30)
    table = np.concatenate([i["rpb"].reshape(DEPTH * 8, -1), np.full((DEPTH * 8, 1), -1e30, np.float32)], axis=1)
    bias = table[:, np.where(ok, dr * 31 + dc, 15 * 31)]
    out["bias"] = np.ascontiguousarray(bias.reshape(DEPTH * 8, 2, P, S).transpose(0, 2, 1, 3))
    out["W"] = weight_chunks(i, products)
    return out



def kernel(**inputs):
    import concourse.bacc as bacc
    from concourse import mybir as mb
    from concourse.bass_utils import run_bass_kernel_spmd as run

    i = {k: np.asarray(v) for k, v in inputs.items()}
    arrays = layout(i)
    nc = bacc.Bacc("TRN2", target_bir_lowering=False, num_devices=1)
    aps = [nc.dram_tensor(f"in_{n}", a.shape, mb.dt.from_np(a.dtype), kind="ExternalInput").ap()
           for n, a in arrays.items()]
    o = nc.dram_tensor("out", (P, KT, S), mb.dt.float32, kind="ExternalOutput").ap()
    kernel_program(nc, *aps, o)
    r = run(nc, [{f"in_{n}": a for n, a in arrays.items()}], core_ids=[0])
    got = r.results[0]["out"]
    return np.ascontiguousarray(got.transpose(2, 1, 0)).reshape(1, S, D)
```
